# Optimizing a Trainium2 kernel written in Bass

```python
import jax, jax.numpy as jnp
from jax import lax
import numpy as np

D_MODEL = 1024
BATCH = 1
SEQ = 512
DEPTH = 2

N_MIXERS = 2
N_HGRN_LAYERS = (DEPTH + 1) // 2
N_ATTN_LAYERS = DEPTH // 2

HGRN_EXPAND = 128
HGRN_HEADS = D_MODEL // HGRN_EXPAND
HGRN_KEY_DIM = HGRN_EXPAND
HGRN_VAL_DIM = D_MODEL // HGRN_HEADS
HGRN_QK_WIDTH = HGRN_HEADS * HGRN_KEY_DIM
HGRN_V_WIDTH = HGRN_HEADS * HGRN_VAL_DIM
HGRN_IN_WIDTH = 2 * HGRN_QK_WIDTH + 2 * HGRN_V_WIDTH
HGRN_CHUNK = 64

ATTN_HEAD_DIM = 128
DILATED_GROUPS = ((128, 1), (512, 4), (2048, 16))
HEADS_PER_GROUP = 4
N_GROUPS = len(DILATED_GROUPS)
ATTN_HEADS = HEADS_PER_GROUP * N_GROUPS
ATTN_WIDTH = ATTN_HEADS * ATTN_HEAD_DIM
ROPE_THETA = 10000.0

D_FF = ((8 * D_MODEL // 3 + 255) // 256) * 256

NORM_EPS = 1e-6


def rmsnorm(x, gain):
    xf = x.astype(jnp.float32)
    y = xf * lax.rsqrt(jnp.mean(xf * xf, axis=-1, keepdims=True) + NORM_EPS)
    return (y * gain.astype(jnp.float32)).astype(x.dtype)

def rope_tables(seq_len):
    inv_freq = 1.0 / (ROPE_THETA ** (jnp.arange(0, ATTN_HEAD_DIM, 2, dtype=jnp.float32) / ATTN_HEAD_DIM))
    pos = jnp.arange(seq_len, dtype=jnp.float32)
    ang = pos[:, None] * inv_freq[None, :]
    return jnp.cos(ang)[:, None, :], jnp.sin(ang)[:, None, :]

def apply_rope(x, cos, sin):
    xf = x.astype(jnp.float32)
    x1, x2 = jnp.split(xf, 2, axis=-1)
    out = jnp.concatenate([x1 * cos - x2 * sin, x2 * cos + x1 * sin], axis=-1)
    return out.astype(x.dtype)

def hgrn2_mixer(u, w_in, lower_bound, out_gain, w_out):
    B, S, _ = u.shape
    H, K, V, C = HGRN_HEADS, HGRN_KEY_DIM, HGRN_VAL_DIM, HGRN_CHUNK
    proj = u @ w_in
    q, f, i, g = jnp.split(proj, [HGRN_QK_WIDTH, 2 * HGRN_QK_WIDTH, 2 * HGRN_QK_WIDTH + HGRN_V_WIDTH], axis=-1)
    lb = lower_bound.astype(jnp.float32)
    forget = lb + (1.0 - lb) * jax.nn.sigmoid(f.astype(jnp.float32))
    key = 1.0 - forget
    log_f = jnp.log(forget)
    query = jax.nn.silu(q.astype(jnp.float32))
    value = i.astype(jnp.float32)

    def to_chunks(t, d):
        return t.reshape(B, S // C, C, H, d).transpose(1, 0, 3, 2, 4)

    xs = (to_chunks(query, K), to_chunks(key, K), to_chunks(value, V), to_chunks(log_f, K))
    causal = jnp.tril(jnp.ones((C, C), dtype=bool))[:, :, None]

    def chunk_step(state, inp):
        qc, kc, vc, gc = inp
        b = jnp.cumsum(gc, axis=2)
        o_inter = jnp.einsum('bhck,bhkv->bhcv', qc * jnp.exp(b), state)
        diff = b[:, :, :, None, :] - b[:, :, None, :, :]
        decay = jnp.exp(jnp.where(causal, diff, -jnp.inf))
        scores = jnp.einsum('bhtk,bhsk,bhtsk->bhts', qc, kc, decay)
        o_intra = jnp.einsum('bhts,bhsv->bhtv', scores, vc)
        b_last = b[:, :, -1, :]
        k_to_end = kc * jnp.exp(b_last[:, :, None, :] - b)
        new_state = jnp.exp(b_last)[..., None] * state + jnp.einsum('bhck,bhcv->bhkv', k_to_end, vc)
        return new_state, o_inter + o_intra

    state0 = jnp.zeros((B, H, K, V), dtype=jnp.float32)
    _, o = lax.scan(chunk_step, state0, xs)
    o = o.transpose(1, 0, 3, 2, 4).reshape(B, S, H, V)
    o = rmsnorm(o, out_gain)
    o = o * jax.nn.silu(g.astype(jnp.float32)).reshape(B, S, H, V)
    return o.reshape(B, S, H * V).astype(u.dtype) @ w_out

def dilated_window_group(q, k, v, window, dilation):
    B, S, Hg, D = q.shape
    span = window // dilation
    L = S // dilation
    nb = -(-L // span)
    Lp = nb * span

    def to_blocks(t):
        t = t.reshape(B, L, dilation, Hg, D).transpose(0, 2, 3, 1, 4)
        t = jnp.pad(t, ((0, 0), (0, 0), (0, 0), (0, Lp - L), (0, 0)))
        return t.reshape(B, dilation, Hg, nb, span, D)

    qb, kb, vb = to_blocks(q), to_blocks(k), to_blocks(v)

    def with_prev(t):
        prev = jnp.pad(t, ((0, 0), (0, 0), (0, 0), (1, 0), (0, 0), (0, 0)))[:, :, :, :-1]
        return jnp.concatenate([prev, t], axis=4)

    kw, vw = with_prev(kb), with_prev(vb)
    scores = jnp.einsum('bdhnqe,bdhnke->bdhnqk', qb, kw, preferred_element_type=jnp.float32) * (D ** -0.5)
    blk = jnp.arange(nb)[:, None, None] * span
    qpos = blk + jnp.arange(span)[None, :, None]
    kpos = blk - span + jnp.arange(2 * span)[None, None, :]
    mask = (kpos <= qpos) & (kpos >= qpos - span) & (kpos >= 0)
    scores = jnp.where(mask, scores, -jnp.inf)
    m = jnp.max(scores, axis=-1, keepdims=True)
    p = jnp.exp(scores - m)
    l = jnp.sum(p, axis=-1, keepdims=True)
    out = jnp.einsum('bdhnqk,bdhnke->bdhnqe', p, vw.astype(jnp.float32)) / l
    lse = (m + jnp.log(l))[..., 0]
    out = out.reshape(B, dilation, Hg, Lp, D)[:, :, :, :L].transpose(0, 3, 1, 2, 4).reshape(B, S, Hg, D)
    lse = lse.reshape(B, dilation, Hg, Lp)[:, :, :, :L].transpose(0, 3, 1, 2).reshape(B, S, Hg)
    return out, lse

def dilated_attention_mixer(u, w_qkv, w_out, cos, sin):
    B, S, _ = u.shape
    qkv = (u @ w_qkv).reshape(B, S, 3, ATTN_HEADS, ATTN_HEAD_DIM)
    q = apply_rope(qkv[:, :, 0], cos, sin)
    k = apply_rope(qkv[:, :, 1], cos, sin)
    v = qkv[:, :, 2]
    outs, lses = [], []
    for gi, (window, dilation) in enumerate(DILATED_GROUPS):
        hs = slice(gi * HEADS_PER_GROUP, (gi + 1) * HEADS_PER_GROUP)
        o_g, lse_g = dilated_window_group(q[:, :, hs], k[:, :, hs], v[:, :, hs], window, dilation)
        outs.append(o_g)
        lses.append(lse_g)
    o = jnp.stack(outs, axis=2)
    lse = jnp.stack(lses, axis=2)
    alpha = jax.nn.softmax(lse, axis=2)
    o = (o * alpha[..., None]).reshape(B, S, ATTN_WIDTH).astype(u.dtype)
    return o @ w_out

def swiglu_ffn(u, w_in, w_down):
    gate, up = jnp.split(u @ w_in, 2, axis=-1)
    return (jax.nn.silu(gate) * up) @ w_down

def first_inputs(seed: int = 0) -> dict:
    key = jax.random.key(seed)
    ks = jax.random.split(key, 13)
    f32 = jnp.float32

    def dense(k, shape, fan_in):
        return jax.random.normal(k, shape, f32) * (fan_in ** -0.5)

    def gain(k, shape):
        return 1.0 + 0.02 * jax.random.normal(k, shape, f32)

    return {
        "x": jax.random.normal(ks[0], (BATCH, SEQ, D_MODEL), f32),
        "norm_mix": gain(ks[1], (DEPTH, D_MODEL)),
        "norm_ffn": gain(ks[2], (DEPTH, D_MODEL)),
        "hgrn_w_in": dense(ks[3], (N_HGRN_LAYERS, D_MODEL, HGRN_IN_WIDTH), D_MODEL),
        "hgrn_lb_logits": 0.5 * jax.random.normal(ks[4], (DEPTH + 1, HGRN_QK_WIDTH), f32),
        "hgrn_out_norm": gain(ks[5], (N_HGRN_LAYERS, HGRN_VAL_DIM)),
        "hgrn_w_out": dense(ks[6], (N_HGRN_LAYERS, HGRN_V_WIDTH, D_MODEL), HGRN_V_WIDTH),
        "attn_w_qkv": dense(ks[7], (N_ATTN_LAYERS, D_MODEL, 3 * ATTN_WIDTH), D_MODEL),
        "attn_w_out": dense(ks[8], (N_ATTN_LAYERS, ATTN_WIDTH, D_MODEL), ATTN_WIDTH),
        "ffn_w_in": dense(ks[9], (DEPTH, D_MODEL, 2 * D_FF), D_MODEL),
        "ffn_w_down": dense(ks[10], (DEPTH, D_FF, D_MODEL), D_FF),
        "final_norm": gain(ks[11], (D_MODEL,)),
    }

def first_block(x, norm_mix, norm_ffn, hgrn_w_in, hgrn_lb_logits, hgrn_out_norm, hgrn_w_out,
              attn_w_qkv, attn_w_out, ffn_w_in, ffn_w_down, final_norm):
    lb_table = jnp.cumsum(jax.nn.softmax(hgrn_lb_logits.astype(jnp.float32), axis=0), axis=0)
    cos, sin = rope_tables(x.shape[1])
    h = x
    for layer in range(DEPTH):
        u = rmsnorm(h, norm_mix[layer])
        if layer % N_MIXERS == 0:
            a = layer // N_MIXERS
            mix = hgrn2_mixer(u, hgrn_w_in[a], lb_table[layer], hgrn_out_norm[a], hgrn_w_out[a])
        else:
            a = layer // N_MIXERS
            mix = dilated_attention_mixer(u, attn_w_qkv[a], attn_w_out[a], cos, sin)
        h = h + mix
        h = h + swiglu_ffn(rmsnorm(h, norm_ffn[layer]), ffn_w_in[layer], ffn_w_down[layer])
    return rmsnorm(h, final_norm)


DEPTH_2 = 1

D_RNN = D_MODEL
RG_HEADS = 4
RG_BLOCK = D_RNN // RG_HEADS
RG_C = 8.0
CONV4_WIDTH = 4
D_CONV = D_MODEL
CONV3_WIDTH = 3
D_FF_2 = ((8 * D_MODEL + 3 * 256 - 1) // (3 * 256)) * 256
PLE_DIM = 256
EPS = 1e-6
IN_SPLITS = (D_RNN, D_RNN, D_CONV, D_CONV, D_CONV, D_MODEL, D_MODEL)
W_IN = sum(IN_SPLITS)
IN_OFFSETS = tuple(int(v) for v in np.cumsum(IN_SPLITS)[:-1])


def rmsnorm_2(x, g):
    xf = x.astype(jnp.float32)
    y = xf * lax.rsqrt(jnp.mean(xf * xf, axis=-1, keepdims=True) + EPS)
    return (y * g.astype(jnp.float32)).astype(x.dtype)

def causal_depthwise_conv(x, w):
    k_w = w.shape[0]
    t = x.shape[1]
    xp = jnp.pad(x, ((0, 0), (k_w - 1, 0), (0, 0)))
    y = xp[:, 0:t] * w[0]
    for k in range(1, k_w):
        y = y + xp[:, k:k + t] * w[k]
    return y

def block_diag_linear(x, w, b):
    bsz, t, _ = x.shape
    xh = x.reshape(bsz, t, RG_HEADS, RG_BLOCK)
    y = jnp.einsum("bthi,hij->bthj", xh, w) + b
    return y.reshape(bsz, t, RG_HEADS * RG_BLOCK)

def rg_lru(x, w_r, b_r, w_i, b_i, lam):
    r = jax.nn.sigmoid(block_diag_linear(x, w_r, b_r).astype(jnp.float32))
    i = jax.nn.sigmoid(block_diag_linear(x, w_i, b_i).astype(jnp.float32))
    log_a = -RG_C * r * jax.nn.softplus(-lam.astype(jnp.float32))
    a = jnp.exp(log_a)
    mult = jnp.sqrt(-jnp.expm1(2.0 * log_a))
    u = mult * (i * x.astype(jnp.float32))

    def step(h, au):
        a_t, u_t = au
        h = a_t * h + u_t
        return h, h

    h0 = jnp.zeros((x.shape[0], x.shape[2]), jnp.float32)
    _, hs = lax.scan(step, h0, (jnp.swapaxes(a, 0, 1), jnp.swapaxes(u, 0, 1)))
    return jnp.swapaxes(hs, 0, 1).astype(x.dtype)

def hybrid_layer(x, p_i, g_mix, w_in, conv4_w, conv4_b, w_rg_r, b_rg_r, w_rg_i, b_rg_i,
                 lru_lambda, conv3_w, w_out, g_ffn, w_gate_up, w_down, g_ple, w_ple_gate, w_ple):
    h = rmsnorm_2(x, g_mix)
    z = h @ w_in
    rnn_x, rnn_y, conv_b, conv_c, conv_x, gate_rnn, gate_conv = jnp.split(z, IN_OFFSETS, axis=-1)
    rnn_x = causal_depthwise_conv(rnn_x, conv4_w) + conv4_b
    y_rnn = jax.nn.gelu(rnn_y) * rg_lru(rnn_x, w_rg_r, b_rg_r, w_rg_i, b_rg_i, lru_lambda)
    y_conv = conv_b * causal_depthwise_conv(conv_c * conv_x, conv3_w)
    merged = jax.nn.sigmoid(gate_rnn) * y_rnn + jax.nn.sigmoid(gate_conv) * y_conv
    x = x + merged @ w_out
    h = rmsnorm_2(x, g_ffn)
    g, u = jnp.split(h @ w_gate_up, 2, axis=-1)
    x = x + (jax.nn.silu(g) * u) @ w_down
    gate = jax.nn.sigmoid(rmsnorm_2(x, g_ple) @ w_ple_gate)
    x = x + gate * (p_i @ w_ple)
    return x

def second_inputs(seed: int = 0) -> dict:
    key = jax.random.key(seed)
    ks = jax.random.split(key, 20)

    def nrm(k, shape, fan_in):
        return jax.random.normal(k, shape, jnp.float32) * (fan_in ** -0.5)

    def gain(k, shape):
        return 1.0 + 0.05 * jax.random.normal(k, shape, jnp.float32)

    def bias(k, shape):
        return 0.02 * jax.random.normal(k, shape, jnp.float32)

    x = jax.random.normal(ks[0], (BATCH, SEQ, D_MODEL), jnp.float32)
    p = jax.random.normal(ks[1], (DEPTH_2, BATCH, SEQ, PLE_DIM), jnp.float32)
    g_mix = gain(ks[2], (DEPTH_2, D_MODEL))
    w_in = nrm(ks[3], (DEPTH_2, D_MODEL, W_IN), D_MODEL)
    conv4_w = nrm(ks[4], (DEPTH_2, CONV4_WIDTH, D_RNN), CONV4_WIDTH)
    conv4_b = bias(ks[5], (DEPTH_2, D_RNN))
    w_rg_r = nrm(ks[6], (DEPTH_2, RG_HEADS, RG_BLOCK, RG_BLOCK), RG_BLOCK)
    b_rg_r = bias(ks[7], (DEPTH_2, RG_HEADS, RG_BLOCK))
    w_rg_i = nrm(ks[8], (DEPTH_2, RG_HEADS, RG_BLOCK, RG_BLOCK), RG_BLOCK)
    b_rg_i = bias(ks[9], (DEPTH_2, RG_HEADS, RG_BLOCK))
    a_c = jax.random.uniform(ks[10], (DEPTH_2, D_RNN), jnp.float32, minval=0.9, maxval=0.999)
    a0 = a_c ** (1.0 / RG_C)
    lru_lambda = jnp.log(a0) - jnp.log1p(-a0)
    conv3_w = nrm(ks[11], (DEPTH_2, CONV3_WIDTH, D_CONV), CONV3_WIDTH)
    w_out = nrm(ks[12], (DEPTH_2, D_MODEL, D_MODEL), D_MODEL)
    g_ffn = gain(ks[13], (DEPTH_2, D_MODEL))
    w_gate_up = nrm(ks[14], (DEPTH_2, D_MODEL, 2 * D_FF_2), D_MODEL)
    w_down = nrm(ks[15], (DEPTH_2, D_FF_2, D_MODEL), D_FF_2)
    g_ple = gain(ks[16], (DEPTH_2, D_MODEL))
    w_ple_gate = nrm(ks[17], (DEPTH_2, D_MODEL, D_MODEL), D_MODEL)
    w_ple = nrm(ks[18], (DEPTH_2, PLE_DIM, D_MODEL), PLE_DIM)
    g_final = gain(ks[19], (D_MODEL,))
    return {"x": x, "p": p, "g_mix": g_mix, "w_in": w_in, "conv4_w": conv4_w,
            "conv4_b": conv4_b, "w_rg_r": w_rg_r, "b_rg_r": b_rg_r, "w_rg_i": w_rg_i,
            "b_rg_i": b_rg_i, "lru_lambda": lru_lambda, "conv3_w": conv3_w, "w_out": w_out,
            "g_ffn": g_ffn, "w_gate_up": w_gate_up, "w_down": w_down, "g_ple": g_ple,
            "w_ple_gate": w_ple_gate, "w_ple": w_ple, "g_final": g_final}

def second_block(x, p, g_mix, w_in, conv4_w, conv4_b, w_rg_r, b_rg_r, w_rg_i, b_rg_i,
              lru_lambda, conv3_w, w_out, g_ffn, w_gate_up, w_down, g_ple, w_ple_gate,
              w_ple, g_final):
    for i in range(DEPTH_2):
        x = hybrid_layer(x, p[i], g_mix[i], w_in[i], conv4_w[i], conv4_b[i], w_rg_r[i],
                         b_rg_r[i], w_rg_i[i], b_rg_i[i], lru_lambda[i], conv3_w[i], w_out[i],
                         g_ffn[i], w_gate_up[i], w_down[i], g_ple[i], w_ple_gate[i], w_ple[i])
    return rmsnorm_2(x, g_final)


def setup_inputs(seed=0):
    out = dict(first_inputs(seed))
    for name, value in second_inputs(seed + 1).items():
        if name != "x":
            out[name + "_2"] = value
    return out


def reference(
    x, norm_mix, norm_ffn, hgrn_w_in, hgrn_lb_logits, hgrn_out_norm, hgrn_w_out, attn_w_qkv,
    attn_w_out, ffn_w_in, ffn_w_down, final_norm, p_2, g_mix_2, w_in_2, conv4_w_2, conv4_b_2,
    w_rg_r_2, b_rg_r_2, w_rg_i_2, b_rg_i_2, lru_lambda_2, conv3_w_2, w_out_2, g_ffn_2,
    w_gate_up_2, w_down_2, g_ple_2, w_ple_gate_2, w_ple_2, g_final_2,
):
    x = first_block(
        x, norm_mix, norm_ffn, hgrn_w_in, hgrn_lb_logits, hgrn_out_norm, hgrn_w_out, attn_w_qkv,
        attn_w_out, ffn_w_in, ffn_w_down, final_norm,
    )
    return second_block(
        x, p_2, g_mix_2, w_in_2, conv4_w_2, conv4_b_2, w_rg_r_2, b_rg_r_2, w_rg_i_2, b_rg_i_2,
        lru_lambda_2, conv3_w_2, w_out_2, g_ffn_2, w_gate_up_2, w_down_2, g_ple_2, w_ple_gate_2,
        w_ple_2, g_final_2,
    )


_drawn_inputs = setup_inputs


def setup_inputs(seed=0):
    import zlib

    import numpy as np

    out = dict(_drawn_inputs(seed))
    spreads = {}
    factors = {'hgrn_out_norm': 3.08,
     'b_rg_r_2': 61.482,
     'b_rg_i_2': 32.893,
     'g_ple_2': 7.301,
     'norm_ffn': 3.586,
     'attn_w_qkv': 3.229,
     'attn_w_out': 3.226}
    for name, (base, spread) in spreads.items():
        noise = np.random.default_rng([zlib.crc32(name.encode()), seed]).standard_normal(out[name].shape)
        drawn = base * np.exp(spread * noise) if base else spread * noise
        out[name] = __import__('jax').numpy.asarray(drawn.astype(out[name].dtype))
    for name, factor in factors.items():
        out[name] = (out[name] * factor).astype(out[name].dtype)
    return out
```

```python
from contextlib import ExitStack

import numpy as np

import concourse.bass as bass
from concourse import mybir

F32 = mybir.dt.float32
F32R = mybir.dt.float32r
U8 = mybir.dt.uint8
ALU = mybir.AluOpType
ACT = mybir.ActivationFunctionType
AX_X = mybir.AxisListType.X

P = 128
S = 512
DM = 1024
KC = DM // P
DFF = 2816
FT = DFF // P
TT = S // P
HG = 8
AH = 12
GH = 4
PLE = 256
PANEL = 2048
HALF = PANEL // KC
LEVELS = (64, 32, 16, 8, 4, 2, 1)
EPS = 1e-6
ATT_SCALE = 128 ** -0.5
MASKED = -1e30
RG_C = 8.0

V_NORM = 0
V_LB = V_NORM + 9 * KC
V_HG = V_LB + 3 * KC
V_C4W = V_HG + 1
V_C4B = V_C4W + 4 * KC
V_BR = V_C4B + KC
V_BI = V_BR + KC
V_LAM = V_BI + KC
V_C3W = V_LAM + KC
V_ALL = V_C3W + 3 * KC


def panel_plan():
    at, first = 0, {}
    for name, n in (("f", 4), ("q", 4), ("i", 4), ("g", 4), ("hgrn_out", 4),
                    ("up0", FT), ("down0", 12),
                    ("aq", 6), ("ak", 6), ("av", 6), ("attn_out", 8),
                    ("up1", FT), ("down1", 12),
                    ("rx", 4), ("rg", 2), ("cx", 8), ("bg", 8), ("yg", 8), ("rg_out", 4),
                    ("up2", FT), ("down2", 12), ("ple", 1), ("gate", 4)):
        first[name] = at
        at += n
    first["end"] = at
    return first


def group_plan():
    at, first = 0, {}
    for name, n in (("f", 4), ("q", 4), ("i", 4), ("g", 4), ("hgrn_out", 4),
                    ("up0", FT), ("down0", 4),
                    ("aq", 6), ("ak", 6), ("av", 6), ("attn_out", 4),
                    ("up1", FT), ("down1", 4),
                    ("rx", 4), ("rg", 8), ("cx", 8), ("bg", 8), ("yg", 8), ("rg_out", 4),
                    ("up2", FT), ("down2", 4), ("ple", 4), ("gate", 4)):
        first[name] = at
        at += n
    return first


PAN = panel_plan()
GRP = group_plan()


class Chain:

    def __init__(self, eng, sem):
        self.eng, self.sem, self.base, self.k, self.i, self.per = eng, sem, 0, 0, None, 0

    def now(self):
        return self.base + self.k if self.i is None else self.per * self.i + (self.base + self.k)

    def step(self, ins):
        ins.then_inc(self.sem, 1)
        self.k += 1

    def settle(self):
        self.eng.wait_ge(self.sem, self.now())

    def link(self, ins):
        self.step(ins)
        self.settle()

    def enter(self, i, per):
        self.base += self.k
        self.k, self.i, self.per = 0, i, per

    def leave(self, n):
        assert self.k == self.per, f"{self.k} steps in the body, {self.per} stated"
        self.base += self.per * n
        self.k, self.i = 0, None


def build(nc, wall, x_t, p_t, vecs_d, ident_d, cs_d, lmask_d, amask_d, sel_d, out_t):
    with ExitStack() as ctx:
        UNIT = 4 * S

        def sb(name, shape, dt=F32):
            return ctx.enter_context(nc.sbuf_tensor(name, shape, dt))

        def sem(name):
            return ctx.enter_context(nc.semaphore(name))

        h = sb("h", [P, KC, S])
        raw = sb("raw", [P, 2, PANEL])
        w_hi = sb("w_hi", [P, 2, PANEL], F32R)
        w_lo = sb("w_lo", [P, 2, PANEL], F32R)
        sq = sb("sq", [P, 2, S])
        un = sb("un", [P, 2, S])
        ssq = sb("ssq", [P, S])
        rstd = sb("rstd", [P, S])
        ones = sb("ones", [P, P])
        ident = sb("ident", [P, P])
        vecs = sb("vecs", [P, V_ALL])
        eps = sb("eps", [P, 1])
        lb = sb("lb", [P, 6, KC])
        spl = sb("spl", [P, 6, KC])
        lmask = sb("lmask", [P, len(LEVELS) + 1, P], U8)
        amask = sb("amask", [P, 4, P])
        sel = sb("sel", [GH, GH, P])
        mst = sb("mst", [P, AH, TT])
        lst = sb("lst", [P, AH, TT])
        cols = sb("cols", [P, 4, TT])

        region = {}
        region["u"] = (nc.sbuf_base + 31) // 32 * 32
        sb("region_u", [P, 2 * KC * S])
        region["a"] = (nc.sbuf_base + 31) // 32 * 32
        sb("region_a", [P, 2 * FT * S])

        def place(name, where, unit, shape, dt=F32):
            return nc.alloc_sbuf_tensor_at(name, shape, dt, offset=region[where] + int(unit * UNIT))

        u_hi = place("u_hi", "u", 0, [P, KC, S], F32R)
        u_lo = place("u_lo", "u", KC, [P, KC, S], F32R)
        act_hi = place("act_hi", "a", 0, [P, FT, S], F32R)
        act_lo = place("act_lo", "a", FT, [P, FT, S], F32R)
        query = place("query", "a", 0, [P, HG, S])
        key = place("key", "a", 8, [P, HG, S])
        o_hi = place("o_hi", "a", 0, [P, HG, S], F32R)
        o_lo = place("o_lo", "a", 8, [P, HG, S], F32R)
        cum = place("cum", "a", 16, [P, HG, S])
        val = place("val", "a", 24, [P, TT, DM])
        gate = place("gate", "a", 32, [P, HG, S])
        lmask_f = place("lmask_f", "a", 41, [P, len(LEVELS) + 1, P])
        one_s = place("one_s", "a", 40, [P, P])
        zl = place("zl", "u", 0, [P, len(LEVELS), S])
        key_h = place("key_h", "u", 7, [P, S])
        val_h = place("val_h", "u", 8, [P, TT, P])
        q_dec = place("q_dec", "u", 9, [P, S])
        k_end = place("k_end", "u", 10, [P, S])
        k_endt = place("k_endt", "u", 11, [P, 3, P])
        sc = place("sc", "u", 12, [P, S])
        state = place("state", "u", 13, [P, 3, P])
        b_last = place("b_last", "u", 14, [P, TT])
        e_last = place("e_last", "u", 14.125, [P, TT])
        aqk = place("aqk", "a", 0, [P, 2 * AH, S])
        av = place("av", "a", 24, [P, 3, TT, S])
        o_raw = place("o_raw", "a", 0, [P, AH, S])
        ao_hi = place("ao_hi", "a", 12, [P, AH, S], F32R)
        ao_lo = place("ao_lo", "a", 24, [P, AH, S], F32R)
        cs = place("cs", "a", 36, [P, 2, S])
        rot = place("rot", "a", 38, [P, 2, S])
        q_h = place("q_h", "u", 0, [P, S])
        v_h = place("v_h", "u", 1, [P, TT, P])
        s_a = place("s_a", "u", 2, [P, TT, P])
        s_b = place("s_b", "u", 3, [P, TT, P])
        pt_a = place("pt_a", "u", 4, [P, TT, P])
        pt_b = place("pt_b", "u", 5, [P, TT, P])
        mrow = place("mrow", "u", 6, [GH, 3, S])
        lrow = place("lrow", "u", 9, [GH, 3, S])
        erow = place("erow", "u", 12, [GH, 3, S])
        trow = place("trow", "u", 15, [GH, S])
        x4 = place("x4", "a", 0, [P, KC, S])
        x4_hi = place("x4_hi", "a", 8, [P, KC, S], F32R)
        x4_lo = place("x4_lo", "a", 16, [P, KC, S], F32R)
        rr = place("rr", "a", 24, [P, KC, S])
        ii = place("ii", "a", 32, [P, KC, S])
        m_hi = place("m_hi", "a", 0, [P, KC, S], F32R)
        cc = place("cc", "a", 8, [P, KC, S])
        m_lo = place("m_lo", "a", 16, [P, KC, S], F32R)
        xpad = place("xpad", "a", 40, [P, 2, S + 8])
        gel = place("gel", "a", 42.5, [P, S])
        pf = place("pf", "u", 0, [P, 2, S])
        p_hi = place("p_hi", "u", 12, [P, 2, S], F32R)
        p_lo = place("p_lo", "u", 14, [P, 2, S], F32R)
        pp = place("pp", "a", 0, [P, KC, S])

        PB = [ctx.enter_context(nc.psum_tensor(f"bank{i}", [P, S], F32)) for i in range(8)]
        MS = PB[4]
        KV, OB = PB[2], PB[3]
        FAC = [PB[5], PB[6], PB[7], PB[3]]

        def pair(g):
            return PB[2 * (g % 2)], PB[2 * (g % 2) + 1]

        raw_loaded = [sem("raw_loaded0"), sem("raw_loaded1")]
        x_loaded = sem("x_loaded")
        p_loaded = sem("p_loaded")
        const_loaded = sem("const_loaded")
        cs_loaded = sem("cs_loaded")
        out_stored = sem("out_stored")
        hi_ready = sem("hi_ready")
        lo_ready = sem("lo_ready")
        panel_done = sem("panel_done")
        group_free = sem("group_free")
        consts_ready = sem("consts_ready")
        waits_apart = sem("waits_apart")
        act_chain = sem("act_chain")
        dve_chain = sem("dve_chain")
        masks_ready = sem("masks_ready")
        h_ready = sem("h_ready")
        sq_ready = sem("sq_ready")
        sum_added = sem("sum_added")
        ms_ready = sem("ms_ready")
        rstd_ready = sem("rstd_ready")
        un_ready = sem("un_ready")
        uhi_ready = sem("uhi_ready")
        u_ready = sem("u_ready")
        sg_ready = sem("sg_ready")
        act_ready = sem("act_ready")
        fsig_ready = sem("fsig_ready")
        logf_ready = sem("logf_ready")
        cum_ready = sem("cum_ready")
        heads_copied = sem("heads_copied")
        diff_ready = sem("diff_ready")
        exp_ready = sem("exp_ready")
        z_ready = sem("z_ready")
        lev_done = sem("lev_done")
        lev_free = sem("lev_free")
        blast_ready = sem("blast_ready")
        ends_ready = sem("ends_ready")
        dec_ready = sem("dec_ready")
        ket_done = sem("ket_done")
        ket_ready = sem("ket_ready")
        kv_done = sem("kv_done")
        states_ready = sem("states_ready")
        o_done = sem("o_done")
        osq_ready = sem("osq_ready")
        oms_done = sem("oms_done")
        orstd_ready = sem("orstd_ready")
        oh_ready = sem("oh_ready")
        rot_ready = sem("rot_ready")
        qv_copied = sem("qv_copied")
        s_done = sem("s_done")
        max_ready = sem("max_ready")
        p_ready = sem("p_ready")
        pt_done = sem("pt_done")
        pt_ready = sem("pt_ready")
        pv_done = sem("pv_done")
        oraw_ready = sem("oraw_ready")
        rows_done = sem("rows_done")
        row_log = sem("row_log")
        row_diff = sem("row_diff")
        row_exp = sem("row_exp")
        row_sum = sem("row_sum")
        row_logsum = sem("row_logsum")
        row_fac = sem("row_fac")
        fac_ready = sem("fac_ready")
        fac_done = sem("fac_done")
        ao_ready = sem("ao_ready")
        xp_ready = sem("xp_ready")
        x4_ready = sem("x4_ready")
        z8_ready = sem("z8_ready")
        decay_ready = sem("decay_ready")
        m2_ready = sem("m2_ready")
        mult_ready = sem("mult_ready")
        xs_ready = sem("xs_ready")
        sgc_ready = sem("sgc_ready")
        gel_ready = sem("gel_ready")
        mg_ready = sem("mg_ready")
        lam_exp = sem("lam_exp")
        lb_exp = sem("lb_exp")
        lb_in = sem("lb_in")
        pf_ready = sem("pf_ready")
        sgate_ready = sem("sgate_ready")
        gate_done = sem("gate_done")
        side_done = sem("side_done")

        def wait_apart(eng, s, value):
            eng.wait_ge(s, value)
            eng.sem_inc(waits_apart, 1)

        def vec(first, j):
            return vecs[:, first + j:first + j + 1]

        def vec_i(first, i, step, s):
            return vecs[:, bass.ds(i * step + (first + s), 1)]

        def blocks(t, m):
            return t.rearrange("p (n c) -> p n c", c=2 * m)

        def by_four(t):
            return t.rearrange("p (a r) -> p r a", r=TT)

        block = ctx.enter_context(nc.Block())

        @block.sync
        def _(sp):
            def load_panels(a, b):
                n = (b - a) // 2
                with sp.Fori(0, n) as i:
                    for s in range(2):
                        sp.wait_ge(lo_ready, i * 2 + (a + s - 1))
                        sp.dma_start(raw[:, (a + s) % 2, :], wall[i * 2 + (a + s)]).then_inc(raw_loaded[(a + s) % 2], 16)
                if (b - a) % 2:
                    sp.wait_ge(lo_ready, b - 2)
                    sp.dma_start(raw[:, (b - 1) % 2, :], wall[b - 1]).then_inc(raw_loaded[(b - 1) % 2], 16)

            x_v = x_t.rearrange("(k p) s -> p k s", p=P)
            sp.dma_start(h[:], x_v).then_inc(x_loaded, 16)
            for s in range(2):
                sp.dma_start(raw[:, s, :], wall[s]).then_inc(raw_loaded[s], 16)
            sp.dma_start(vecs[:], vecs_d).then_inc(const_loaded, 16)
            sp.dma_start(ident[:], ident_d).then_inc(const_loaded, 16)
            sp.dma_start(amask[:], amask_d).then_inc(const_loaded, 16)
            sp.dma_start(lmask_f[:], lmask_d).then_inc(const_loaded, 16)
            sp.dma_start(sel[:], sel_d).then_inc(const_loaded, 16)
            load_panels(2, PAN["aq"] + 2)
            sp.wait_ge(panel_done, PAN["aq"])
            sp.dma_start(cs[:], cs_d).then_inc(cs_loaded, 16)
            load_panels(PAN["aq"] + 2, PAN["down2"] + 2)
            sp.wait_ge(panel_done, PAN["down2"])
            sp.dma_start(pf[:], p_t.rearrange("(k p) s -> p k s", p=P)).then_inc(p_loaded, 16)
            load_panels(PAN["down2"] + 2, PAN["end"])
            out_v = out_t.rearrange("(k p) s -> p k s", p=P)
            for j in range(0, KC, 2):
                sp.wait_ge(h_ready, 8 * KC + j + 2)
                sp.dma_start(out_v[:, j:j + 2, :], h[:, j:j + 2, :]).then_inc(out_stored, 16)
            sp.wait_ge(out_stored, 16 * KC // 2)

        @block.gpsimd
        def _(pool):
            def lo(p, s, i=None):
                q = p if i is None else i * 2 + p
                pool.wait_ge(hi_ready, q + 1)
                nc.gpsimd.tensor_tensor(w_lo[:, s, :], raw[:, s, :], w_hi[:, s, :].bitcast(F32),
                                        ALU.subtract).then_inc(lo_ready, 1)

            def lo_panels(a, b):
                n = (b - a) // 2
                with pool.Fori(0, n) as i:
                    for s in range(2):
                        lo(a + s, (a + s) % 2, i)
                if (b - a) % 2:
                    lo(b - 1, (b - 1) % 2)

            nc.gpsimd.memset(ones[:], 1.0).then_inc(consts_ready, 1)
            nc.gpsimd.memset(eps[:], EPS).then_inc(consts_ready, 1)
            nc.gpsimd.memset(one_s[:], 1.0).then_inc(consts_ready, 1)
            lo_panels(0, PAN["hgrn_out"] + 1)

            pool.wait_ge(cum_ready, HG)
            pool.wait_ge(panel_done, PAN["hgrn_out"])
            with pool.Fori(0, HG) as i:
                for l, m in enumerate(LEVELS):
                    wait_apart(pool, lev_done, i * 8 + (l + 1))
                    b = blocks(cum[:, i, :], m)
                    n = S // (2 * m)
                    nc.gpsimd.tensor_tensor(blocks(zl[:, l, :], m), b, b[:, :, m - 1:m].to_broadcast([P, n, 2 * m]),
                                            ALU.subtract).then_inc(diff_ready, 1)
                pool.wait_ge(o_done, i)
                nc.gpsimd.tensor_copy(key_h[:], key[:, i, :])
                nc.gpsimd.tensor_copy(val_h[:], val[:, :, bass.ds(i * P, P)]).then_inc(heads_copied, 1)

            lo_panels(PAN["hgrn_out"] + 1, PAN["attn_out"] + 1)

            pool.wait_ge(group_free, GRP["attn_out"] + 2)
            for g in range(3):
                with pool.Fori(0, GH) as i:
                    pool.wait_ge(pv_done, i + GH * g)
                    nc.gpsimd.tensor_copy(q_h[:], aqk[:, i + GH * g, :])
                    nc.gpsimd.tensor_copy(v_h[:], av[:, g, :, bass.ds(i * P, P)]).then_inc(qv_copied, 1)

            lo_panels(PAN["attn_out"] + 1, PAN["end"])

        @block.scalar
        def _(act):
            ch = Chain(act, act_chain)

            def af(out, in_, func, **k):
                return nc.scalar.activation(out, in_, func, **k)

            def conv(p, i=None, step=2):
                s = p % 2
                if i is None:
                    act.wait_ge(raw_loaded[s], 16 * (p // 2 + 1))
                    if p >= 2:
                        act.wait_ge(panel_done, p - 1)
                else:
                    act.wait_ge(raw_loaded[s], i * (8 * step) + 16 * (p // 2 + 1))
                    act.wait_ge(panel_done, i * step + (p - 1))
                af(w_hi[:, s, :], raw[:, s, :], ACT.Copy).then_inc(hi_ready, 1)

            def norm_sums_part(n, j, i=None, step=0):
                if n:
                    act.wait_ge(h_ready, KC * (n - 1) + j + 1 if i is None else i * step + (KC * (n - 1) + j + 1))
                if n or j >= 2:
                    act.wait_ge(sum_added, KC * n + j - 1 if i is None else i * step + (KC * n + j - 1))
                hj = h[:, j, :] if i is None else h[:, i * step + j, :]
                af(sq[:, j % 2, :], hj, ACT.Square).then_inc(sq_ready, 1)

            def norm_scale(n):
                act.wait_ge(ms_ready, n + 1)
                ch.link(af(rstd[:], MS[:], ACT.Ln, bias=eps[:, 0:1], scale=1.0 / DM))
                af(rstd[:], rstd[:], ACT.Exp, scale=-0.5).then_inc(rstd_ready, 1)

            def norm_upper(m):
                for j in range(KC):
                    act.wait_ge(un_ready, KC * m + j + 1)
                    af(u_hi[:, j, :], un[:, j % 2, :], ACT.Copy).then_inc(uhi_ready, 1)

            def residual(p0, per, n):
                with act.Fori(0, 2) as i:
                    for s in range(2):
                        for t in range(per):
                            conv(p0 + per * s + t + 1, i, 2 * per)
                        for c in range(2):
                            norm_sums_part(n, 2 * s + c, i, 4)

            def ffn(f, n):
                with act.Fori(0, FT // 2) as i:
                    for s in range(2):
                        p = PAN[f"up{f}"] + s
                        conv(p + 1, i)
                        act.wait_ge(group_free, i * 2 + (GRP[f"up{f}"] + s + 1))
                        act.wait_ge(panel_done, i * 2 + (p + 1))
                        af(sq[:, s, :], pair(GRP[f"up{f}"] + s)[0][:], ACT.Silu).then_inc(sg_ready, 1)
                residual(PAN[f"down{f}"], 3, n)

            act.wait_ge(x_loaded, 16)
            act.wait_ge(consts_ready, 3)
            for j in range(KC):
                norm_sums_part(0, j)
            conv(0)
            act.wait_ge(lb_in, 2)
            af(lb[:, 0:3, :], lb[:, 0:3, :], ACT.Exp).then_inc(lb_exp, 1)
            af(spl[:, 1, :], spl[:, 1, :], ACT.Exp).then_inc(lam_exp, 1)
            norm_scale(0)
            norm_upper(0)

            with act.Fori(0, 2) as i:
                for s in range(2):
                    p = PAN["f"] + s
                    conv(p + 1, i)
                    act.wait_ge(panel_done, i * 2 + (p + 1))
                    for c in range(2):
                        af(key[:, i * 4 + (2 * s + c), :], pair(GRP["f"] + s)[c][:], ACT.Sigmoid).then_inc(fsig_ready, 1)
            act.wait_ge(group_free, GRP["q"] + 2)
            with act.Fori(0, HG) as i:
                af(cum[:, i, :], cum[:, i, :], ACT.Ln).then_inc(logf_ready, 1)
            with act.Fori(0, 2) as i:
                for s in range(2):
                    p = PAN["q"] + s
                    conv(p + 1, i)
                    act.wait_ge(panel_done, i * 2 + (p + 1))
                    af(query[:, i * 4 + 2 * s, :], pair(GRP["q"] + s)[0][:], ACT.Silu)
                    af(query[:, i * 4 + (2 * s + 1), :], pair(GRP["q"] + s)[1][:], ACT.Silu).then_inc(group_free, 1)
            with act.Fori(0, 2) as i:
                for s in range(2):
                    conv(PAN["i"] + s + 1, i)
                act.wait_ge(panel_done, i * 2 + (PAN["i"] + 2))
                for t in range(TT):
                    ins = af(val[:, t, bass.ds(i * S, S)], PB[t][:], ACT.Copy)
                    if t % 2:
                        ins.then_inc(group_free, 1)
            with act.Fori(0, 2) as i:
                for s in range(2):
                    p = PAN["g"] + s
                    conv(p + 1, i)
                    act.wait_ge(panel_done, i * 2 + (p + 1))
                    af(gate[:, i * 4 + 2 * s, :], pair(GRP["g"] + s)[0][:], ACT.Silu)
                    af(gate[:, i * 4 + (2 * s + 1), :], pair(GRP["g"] + s)[1][:], ACT.Silu).then_inc(group_free, 1)
            with act.Fori(0, HG) as i:
                ch.enter(i, 1)
                for l, m in enumerate(LEVELS):
                    act.wait_ge(diff_ready, i * len(LEVELS) + (l + 1))
                    z = blocks(zl[:, l, :], m)
                    af(z[:, :, m:2 * m], z[:, :, m:2 * m], ACT.Exp)
                    af(z[:, :, 0:m], z[:, :, 0:m], ACT.Exp, scale=-1.0).then_inc(exp_ready, 1)
                act.wait_ge(o_done, i)
                af(q_dec[:], cum[:, i, :], ACT.Exp)
                wait_apart(act, blast_ready, i + 1)
                for c in range(TT - 1):
                    af(k_end[:, c * P:(c + 1) * P], cum[:, i, c * P:(c + 1) * P], ACT.Exp,
                       bias=b_last[:, c:c + 1], scale=-1.0)
                af(e_last[:], b_last[:], ACT.Exp).then_inc(ends_ready, 1)
                act.wait_ge(ket_done, i + 1)
                af(k_endt[:].rearrange("p a b -> p (a b)"), PB[7][:, 0:3 * P], ACT.Copy).then_inc(ket_ready, 1)
                act.wait_ge(o_done, i + 1)
                af(sq[:, 0, :], OB[:], ACT.Square).then_inc(osq_ready, 1)
                act.wait_ge(oms_done, i + 1)
                ch.link(af(rstd[:], MS[:], ACT.Ln, bias=eps[:, 0:1], scale=1.0 / P))
                af(rstd[:], rstd[:], ACT.Exp, scale=-0.5).then_inc(orstd_ready, 1)
            ch.leave(HG)
            residual(PAN["hgrn_out"], 1, 1)
            norm_scale(1)
            norm_upper(1)
            ffn(0, 2)
            norm_scale(2)
            norm_upper(2)

            with act.Fori(0, AH // 2) as i:
                for s in range(2):
                    p, g = PAN["aq"] + s, GRP["aq"] + s
                    conv(p + 1, i)
                    act.wait_ge(group_free, i * 2 + (g + 2))
                    act.wait_ge(panel_done, i * 2 + (p + 1))
                    for c in range(2):
                        bank = pair(g)[c]
                        af(rot[0:64, c, :], bank[64:128, :], ACT.Copy)
                        af(rot[64:128, c, :], bank[0:64, :], ACT.Copy).then_inc(rot_ready, 1)
            with act.Fori(0, 3) as i:
                for s in range(2):
                    conv(PAN["av"] + s + 1, i)
                act.wait_ge(panel_done, i * 2 + (PAN["av"] + 2))
                for t in range(TT):
                    ins = af(av[:, i, t, :], PB[t][:], ACT.Copy)
                    if t % 2:
                        ins.then_inc(group_free, 1)
            for g in range(3):
                with act.Fori(0, GH) as i:
                    act.wait_ge(max_ready, i + (GH * g + 1))
                    for n in range(TT):
                        ins = af(s_a[:, n, :], s_a[:, n, :], ACT.Exp, bias=cols[:, 1, n:n + 1], scale=ATT_SCALE,
                                 accum_out=cols[:, 2, n:n + 1])
                        if g == 0 and n:
                            ins = af(s_b[:, n, :], s_b[:, n, :], ACT.Exp, bias=cols[:, 1, n:n + 1], scale=ATT_SCALE,
                                     accum_out=cols[:, 3, n:n + 1])
                    ins.then_inc(p_ready, 1)
                    act.wait_ge(pt_done, i + (GH * g + 1))
                    if g == 0:
                        af(pt_b[:, 1:TT, :], MS[:, P:S].rearrange("p (n c) -> p n c", c=P), ACT.Copy)
                    af(pt_a[:].rearrange("p n c -> p (n c)"), PB[7][:], ACT.Copy).then_inc(pt_ready, 1)
            act.wait_ge(rows_done, 1)
            for g in range(3):
                src = PB[g][0:GH, :]
                dst = lrow[:, g, :] if g == 0 else by_four(lrow[:, g, :])
                if g:
                    src = src.rearrange("p (r a) -> p r a", r=TT)
                ins = af(dst, src, ACT.Ln)
            ins.then_inc(row_log, 1)
            act.wait_ge(row_diff, 1)
            af(lrow[:], erow[:], ACT.Exp).then_inc(row_exp, 1)
            act.wait_ge(row_sum, 1)
            af(rstd[0:GH, :], rstd[0:GH, :], ACT.Ln).then_inc(row_logsum, 1)
            act.wait_ge(row_fac, 1)
            af(mrow[:], mrow[:], ACT.Exp).then_inc(fac_ready, 1)

            residual(PAN["attn_out"], 2, 3)
            norm_scale(3)
            norm_upper(3)
            ffn(1, 4)
            norm_scale(4)
            for j in range(KC):
                norm_sums_part(5, j)
            norm_scale(5)
            norm_upper(4)

            with act.Fori(0, 2) as i:
                for s in range(2):
                    p, g = PAN["rx"] + s, GRP["rx"] + s
                    conv(p + 1, i)
                    act.wait_ge(x4_ready, i * 4 + 2 * s)
                    act.wait_ge(panel_done, i * 2 + (p + 1))
                    af(xpad[:, 0, 3:3 + S], pair(g)[0][:], ACT.Copy).then_inc(xp_ready, 1)
                    af(xpad[:, 1, 3:3 + S], pair(g)[1][:], ACT.Copy).then_inc(xp_ready, 1)
                    act.wait_ge(xp_ready, i * 4 + (2 * s + 2))
                    act.sem_inc(group_free, 1)
            for s, (dst, bias) in enumerate(((rr, V_BR), (ii, V_BI))):
                conv(PAN["rg"] + s + 1)
                for q in range(4):
                    g = GRP["rg"] + 4 * s + q
                    act.wait_ge(gate_done, 4 * s + q + 1)
                    for c in range(2):
                        ins = af(dst[:, 2 * q + c, :], pair(g)[c][:], ACT.Sigmoid, bias=vec(bias, 2 * q + c))
                    ins.then_inc(group_free, 1)
            with act.Fori(0, KC // 2) as i:
                for s in range(2):
                    p, g = PAN["cx"] + s, GRP["cx"] + s
                    conv(p + 1, i)
                    act.wait_ge(z8_ready, i * 2 + (s + 1))
                    af(rr[:, i * 2 + s, :], sq[:, s, :], ACT.Exp, scale=-1.0).then_inc(decay_ready, 1)
                    af(sq[:, s, :], sq[:, s, :], ACT.Tanh).then_inc(decay_ready, 1)
                    act.wait_ge(group_free, i * 2 + (g + 2))
                    act.wait_ge(panel_done, i * 2 + (p + 1))
                    af(rstd[:], pair(g)[1][:], ACT.Copy).then_inc(xs_ready, 1)
            with act.Fori(0, KC // 2) as i:
                for s in range(2):
                    p, g = PAN["bg"] + s, GRP["bg"] + s
                    conv(p + 1, i)
                    act.wait_ge(m2_ready, i * 2 + (s + 1))
                    af(sq[:, s, :], x4[:, i * 2 + s, :], ACT.Sqrt).then_inc(mult_ready, 1)
                    act.wait_ge(group_free, i * 2 + (g + 2))
                    act.wait_ge(panel_done, i * 2 + (p + 1))
                    af(rstd[:], pair(g)[1][:], ACT.Sigmoid).then_inc(sgc_ready, 1)
            with act.Fori(0, KC // 2) as i:
                for s in range(2):
                    p, g = PAN["yg"] + s, GRP["yg"] + s
                    conv(p + 1, i)
                    act.wait_ge(group_free, i * 2 + (g + 2))
                    act.wait_ge(panel_done, i * 2 + (p + 1))
                    af(gel[:], pair(g)[0][:], ACT.Gelu_apprx_tanh).then_inc(gel_ready, 1)
                    af(rstd[:], pair(g)[1][:], ACT.Sigmoid).then_inc(gel_ready, 1)
            residual(PAN["rg_out"], 1, 6)
            norm_scale(6)
            norm_upper(5)
            ffn(2, 7)
            norm_scale(7)
            for q in range(4):
                act.wait_ge(side_done, q + 1)
                for c in range(2):
                    ins = af(pp[:, 2 * q + c, :], pair(GRP["ple"] + q)[c][:], ACT.Copy)
                ins.then_inc(group_free, 1)
            norm_upper(6)
            conv(PAN["gate"])
            for q in range(4):
                p, g = PAN["gate"] + q, GRP["gate"] + q
                if p + 1 < PAN["end"]:
                    conv(p + 1)
                act.wait_ge(panel_done, p + 1)
                for c in range(2):
                    act.wait_ge(h_ready, KC * 7 + 2 * q + c - 1)
                    af(un[:, c, :], pair(g)[c][:], ACT.Sigmoid).then_inc(sgate_ready, 1)
                for c in range(2):
                    norm_sums_part(8, 2 * q + c)
            norm_scale(8)

        @block.vector
        def _(dve):
            ch = Chain(dve, dve_chain)
            tt, ts, stt = nc.vector.tensor_tensor, nc.vector.tensor_scalar, nc.vector.scalar_tensor_tensor
            cp = nc.vector.tensor_copy

            def norm_sum(n, j, i=None, step=0):
                dve.wait_ge(sq_ready, KC * n + j + 1 if i is None else i * step + (KC * n + j + 1))
                if i is not None or j:
                    dve.wait_ge(sum_added, KC * n + j if i is None else i * step + (KC * n + j))
                tt(ssq[:], ssq[:], sq[:, j % 2, :], ALU.add).then_inc(sum_added, 1)

            def norm_split(n, m):
                dve.wait_ge(rstd_ready, n + 1)

                def scaled(j):
                    if j >= 2 :
                        dve.wait_ge(u_ready, KC * m + j - 1)
                    stt(un[:, j % 2, :], h[:, j, :], vec(V_NORM + KC * n, j), rstd[:], ALU.mult, ALU.mult)\
                        .then_inc(un_ready, 1)

                scaled(0)
                for j in range(KC):
                    if j + 1 < KC:
                        scaled(j + 1)
                    if n == 7 and j == 4:
                        dve.wait_ge(panel_done, PAN["gate"])
                    dve.wait_ge(uhi_ready, KC * m + j + 1)
                    tt(u_lo[:, j, :], un[:, j % 2, :], u_hi[:, j, :].bitcast(F32), ALU.subtract).then_inc(u_ready, 1)

            def norm_in_place(n):
                dve.wait_ge(rstd_ready, n + 1)
                for j in range(KC):
                    stt(h[:, j, :], h[:, j, :], vec(V_NORM + KC * n, j), rstd[:], ALU.mult, ALU.mult)\
                        .then_inc(h_ready, 1)

            def residual(p0, g0, per, r, n):
                ch.link(nc.vector.memset(ssq[:], 0.0))
                with dve.Fori(0, 2) as i:
                    for s in range(2):
                        dve.wait_ge(panel_done, i * (2 * per) + (p0 + per * (s + 1)))
                        for c in range(2):
                            hj = h[:, i * 4 + (2 * s + c), :]
                            tt(hj, hj, pair(g0 + s)[c][:], ALU.add).then_inc(h_ready, 1)
                        dve.wait_ge(h_ready, i * 4 + (KC * r + 2 * s + 2))
                        dve.sem_inc(group_free, 1)
                        for c in range(2):
                            norm_sum(n, 2 * s + c, i, 4)

            def ffn(f, r, n):
                with dve.Fori(0, FT // 2) as i:
                    ch.enter(i, 2)
                    for s in range(2):
                        g = GRP[f"up{f}"] + s
                        dve.wait_ge(sg_ready, i * 2 + (FT * f + s + 1))
                        tt(un[:, s, :], sq[:, s, :], pair(g)[1][:], ALU.mult).then_inc(group_free, 1)
                        dve.wait_ge(group_free, i * 2 + (g + 3))
                        ch.link(cp(act_hi[:, i * 2 + s, :], un[:, s, :]))
                        tt(act_lo[:, i * 2 + s, :], un[:, s, :], act_hi[:, i * 2 + s, :].bitcast(F32),
                           ALU.subtract).then_inc(act_ready, 1)
                ch.leave(FT // 2)
                if f == 2:
                    dve.wait_ge(p_loaded, 16)
                    ch.link(cp(p_hi[:], pf[:]))
                    tt(p_lo[:], pf[:], p_hi[:].bitcast(F32), ALU.subtract).then_inc(pf_ready, 1)
                residual(PAN[f"down{f}"], GRP[f"down{f}"], 3, r, n)

            dve.wait_ge(const_loaded, 80)
            cp(lmask[:], lmask_f[:]).then_inc(masks_ready, 1)
            row = [vecs[:, V_LB + KC * k:V_LB + KC * (k + 1)] for k in range(3)]
            lam = vecs[:, V_LAM:V_LAM + KC]
            ch.link(tt(lb[:, 3, :], row[0], row[1], ALU.max))
            ch.link(tt(lb[:, 3, :], lb[:, 3, :], row[2], ALU.max))
            for k in range(3):
                ins = tt(lb[:, k, :], row[k], lb[:, 3, :], ALU.subtract)
            ins.then_inc(lb_in, 1)
            ch.link(ts(spl[:, 2, :], lam, -1.0, None, ALU.mult))
            ch.link(ts(spl[:, 0, :], spl[:, 2, :], 0.0, None, ALU.max))
            tt(spl[:, 1, :], lam, spl[:, 2, :], ALU.min).then_inc(lb_in, 1)
            dve.wait_ge(x_loaded, 16)
            ch.link(nc.vector.memset(ssq[:], 0.0))
            for j in range(KC):
                norm_sum(0, j)
            dve.wait_ge(lb_exp, 1)
            ch.link(tt(lb[:, 3, :], lb[:, 0, :], lb[:, 1, :], ALU.add))
            ch.link(tt(lb[:, 3, :], lb[:, 3, :], lb[:, 2, :], ALU.add))
            ch.link(nc.vector.reciprocal(lb[:, 4, :], lb[:, 3, :]))
            ch.link(tt(lb[:, 0, :], lb[:, 0, :], lb[:, 4, :], ALU.mult))
            ch.link(ts(lb[:, 1, :], lb[:, 0, :], -1.0, 1.0, ALU.mult, ALU.add))
            dve.wait_ge(lam_exp, 1)
            ch.link(ts(spl[:, 2, :], spl[:, 1, :], 2.0, None, ALU.add))
            ch.link(nc.vector.reciprocal(spl[:, 3, :], spl[:, 2, :]))
            ch.link(tt(spl[:, 1, :], spl[:, 1, :], spl[:, 3, :], ALU.mult))
            ch.link(tt(spl[:, 2, :], spl[:, 1, :], spl[:, 1, :], ALU.mult))
            ch.link(ts(spl[:, 3, :], spl[:, 2, :], 1.0 / 19, 1.0 / 17, ALU.mult, ALU.add))
            for k in (15, 13, 11, 9, 7, 5, 3, 1):
                ch.link(tt(spl[:, 3, :], spl[:, 3, :], spl[:, 2, :], ALU.mult))
                ch.link(ts(spl[:, 3, :], spl[:, 3, :], 1.0 / k, None, ALU.add))
            ch.link(tt(spl[:, 3, :], spl[:, 3, :], spl[:, 1, :], ALU.mult))
            ch.link(stt(spl[:, 0, :], spl[:, 3, :], 2.0, spl[:, 0, :], ALU.mult, ALU.add))
            ch.link(ts(spl[:, 0, :], spl[:, 0, :], RG_C, None, ALU.mult))
            norm_split(0, 0)

            with dve.Fori(0, 2) as i:
                ch.enter(i, 4)
                for s in range(2):
                    for c in range(2):
                        k = 2 * s + c
                        dve.wait_ge(fsig_ready, i * 4 + (k + 1))
                        ch.link(ts(cum[:, i * 4 + k, :], key[:, i * 4 + k, :], lb[:, 1, bass.ds(i * 4 + k, 1)],
                                   lb[:, 0, bass.ds(i * 4 + k, 1)], ALU.mult, ALU.add))
                        ins = ts(key[:, i * 4 + k, :], cum[:, i * 4 + k, :], -1.0, 1.0, ALU.mult, ALU.add)
                    ins.then_inc(group_free, 1)
            ch.leave(2)
            dve.wait_ge(consts_ready, 3)
            with dve.Fori(0, HG) as i:
                dve.wait_ge(logf_ready, i + 1)
                for c in range(TT):
                    b = cum[:, i, c * P:(c + 1) * P]
                    ins = nc.vector.tensor_tensor_scan(b, one_s[:], b, 0.0, ALU.mult, ALU.add)
                ins.then_inc(cum_ready, 1)
            dve.wait_ge(cum_ready, HG)
            dve.wait_ge(panel_done, PAN["hgrn_out"])
            with dve.Fori(0, HG) as i:
                ch.enter(i, 5)
                cp(b_last[:], cum[:, i, P - 1:S:P]).then_inc(blast_ready, 1)

                dve.wait_ge(masks_ready, 1)

                def take_level(l):
                    dve.wait_ge(lev_done, i * 8 + (8 + l + 1))
                    bank = PB[5 + l % 2][:].rearrange("p (n c) -> p n c", c=P)
                    s3 = sc[:].rearrange("p (n c) -> p n c", c=P)
                    if l == 0:
                        tt(s3, bank, amask[:, 3:4, :].to_broadcast([P, TT, P]), ALU.mult).then_inc(lev_free, 1)
                    else:
                        wait_apart(dve, lev_free, i * 8 + (2 + l))
                        nc.vector.copy_predicated(s3, lmask[:, l:l + 1, :].to_broadcast([P, TT, P]), bank)\
                            .then_inc(lev_free, 1)

                for l, m in enumerate(LEVELS):
                    dve.wait_ge(exp_ready, i * len(LEVELS) + (l + 1))
                    z, q, k = blocks(zl[:, l, :], m), blocks(query[:, i, :], m), blocks(key[:, i, :], m)
                    tt(z[:, :, m:2 * m], z[:, :, m:2 * m], q[:, :, m:2 * m], ALU.mult)
                    tt(z[:, :, 0:m], z[:, :, 0:m], k[:, :, 0:m], ALU.mult).then_inc(z_ready, 1)
                    if l:
                        take_level(l - 1)
                dve.wait_ge(ends_ready, i + 1)
                tt(k_end[:, 0:3 * P], k_end[:, 0:3 * P], key[:, i, 0:3 * P], ALU.mult)
                tt(q_dec[:], q_dec[:], query[:, i, :], ALU.mult).then_inc(dec_ready, 1)
                take_level(6)
                dve.wait_ge(kv_done, i + 1)
                ch.link(cp(state[:, 0, :], KV[:, 0:P]))
                for c in range(1, 3):
                    ins = stt(state[:, c, :], state[:, c - 1, :], e_last[:, c:c + 1], KV[:, c * P:(c + 1) * P],
                              ALU.mult, ALU.add)
                    if c == 1:
                        ch.link(ins)
                ins.then_inc(states_ready, 1)
                take_level(7)
                dve.wait_ge(orstd_ready, i + 1)
                ch.link(stt(un[:, 0, :], OB[:], vec(V_HG, 0), rstd[:], ALU.mult, ALU.mult))
                ch.step(tt(un[:, 1, :], un[:, 0, :], gate[:, i, :], ALU.mult))
                wait_apart(dve, dve_chain, ch.now())
                ch.link(cp(o_hi[:, i, :], un[:, 1, :]))
                tt(o_lo[:, i, :], un[:, 1, :], o_hi[:, i, :].bitcast(F32), ALU.subtract).then_inc(oh_ready, 1)
            ch.leave(HG)
            residual(PAN["hgrn_out"], GRP["hgrn_out"], 1, 0, 1)
            norm_split(1, 1)
            ffn(0, 1, 2)
            norm_split(2, 2)

            dve.wait_ge(cs_loaded, 16)
            with dve.Fori(0, AH // 2) as i:
                ch.enter(i, 8)
                for s in range(2):
                    g = GRP["aq"] + s
                    for c in range(2):
                        k = 2 * s + c
                        dve.wait_ge(rot_ready, i * 4 + (k + 1))
                        ch.step(tt(un[:, c, :], pair(g)[c][:], cs[:, 0, :], ALU.mult))
                        ch.link(tt(rot[:, c, :], rot[:, c, :], cs[:, 1, :], ALU.mult))
                        ins = tt(aqk[:, i * 4 + k, :], un[:, c, :], rot[:, c, :], ALU.add)
                    ins.then_inc(group_free, 1)
            ch.leave(AH // 2)

            def spread(k):
                return amask[:, k:k + 1, :].to_broadcast([P, TT, P])

            for g in range(3):
                with dve.Fori(0, GH) as i:
                    ch.enter(i, 6 if g == 0 else 3)
                    dve.wait_ge(s_done, i + (GH * g + 1))
                    bank = PB[5][:].rearrange("p (n c) -> p n c", c=P)
                    ch.step(tt(s_a[:], bank, spread(0 if g < 2 else 2), ALU.add))
                    if g == 0:
                        prev = PB[6][:, P:S].rearrange("p (n c) -> p n c", c=P)
                        ch.step(tt(s_b[:, 1:TT, :], prev, amask[:, 1:2, :].to_broadcast([P, TT - 1, P]), ALU.add))
                    ch.settle()
                    ch.step(nc.vector.tensor_reduce(cols[:, 0, :], s_a[:], AX_X, ALU.max))
                    if g == 0:
                        ch.link(nc.vector.tensor_reduce(cols[:, 3, 1:TT], s_b[:, 1:TT, :], AX_X, ALU.max))
                        ch.step(tt(cols[:, 0, 1:TT], cols[:, 0, 1:TT], cols[:, 3, 1:TT], ALU.max))
                    ch.settle()
                    cp(mst[:, i + GH * g, :], cols[:, 0, :])
                    ts(cols[:, 1, :], cols[:, 0, :], -ATT_SCALE, None, ALU.mult).then_inc(max_ready, 1)
                    dve.wait_ge(p_ready, i + (GH * g + 1))
                    ch.link(cp(lst[:, i + GH * g, :], cols[:, 2, :]))
                    if g == 0:
                        tt(lst[:, i + GH * g, 1:TT], cols[:, 2, 1:TT], cols[:, 3, 1:TT], ALU.add)
                    dve.wait_ge(pv_done, i + (GH * g + 1))
                    if g == 0:
                        ins = cp(o_raw[:, i, :], OB[:])
                    else:
                        ins = cp(by_four(o_raw[:, i + GH * g, :]), OB[:].rearrange("p (r a) -> p r a", r=TT))
                    ins.then_inc(oraw_ready, 1)
                ch.leave(GH)
            dve.wait_ge(rows_done, 1)
            for g in range(3):
                if g == 0:
                    ch.step(ts(mrow[:, g, :], PB[5][0:GH, :], ATT_SCALE, None, ALU.mult))
                else:
                    ch.step(ts(by_four(mrow[:, g, :]), PB[5 + g][0:GH, :].rearrange("p (r a) -> p r a", r=TT),
                               ATT_SCALE, None, ALU.mult))
            ch.settle()
            dve.wait_ge(row_log, 1)
            ch.link(tt(erow[:], mrow[:], lrow[:], ALU.add))
            ch.link(tt(trow[:], erow[:, 0, :], erow[:, 1, :], ALU.max))
            ch.link(tt(trow[:], trow[:], erow[:, 2, :], ALU.max))
            for g in range(3):
                ins = tt(erow[:, g, :], erow[:, g, :], trow[:], ALU.subtract)
            ins.then_inc(row_diff, 1)
            dve.wait_ge(row_exp, 1)
            ch.link(tt(rstd[0:GH, :], lrow[:, 0, :], lrow[:, 1, :], ALU.add))
            tt(rstd[0:GH, :], rstd[0:GH, :], lrow[:, 2, :], ALU.add).then_inc(row_sum, 1)
            dve.wait_ge(row_logsum, 1)
            ch.link(tt(trow[:], trow[:], rstd[0:GH, :], ALU.add))
            for g in range(3):
                ins = tt(mrow[:, g, :], mrow[:, g, :], trow[:], ALU.subtract)
            ins.then_inc(row_fac, 1)
            with dve.Fori(0, 3) as i:
                ch.enter(i, 2 * GH)
                for k in range(GH):
                    dve.wait_ge(fac_done, i * GH + (k + 1))
                    ch.link(tt(un[:, k % 2, :], o_raw[:, i * GH + k, :], FAC[k][:], ALU.mult))
                    ch.link(cp(ao_hi[:, i * GH + k, :], un[:, k % 2, :]))
                    tt(ao_lo[:, i * GH + k, :], un[:, k % 2, :], ao_hi[:, i * GH + k, :].bitcast(F32),
                       ALU.subtract).then_inc(ao_ready, 1)
            ch.leave(3)
            residual(PAN["attn_out"], GRP["attn_out"], 2, 2, 3)
            norm_split(3, 3)
            ffn(1, 3, 4)
            norm_in_place(4)
            ch.link(nc.vector.memset(ssq[:], 0.0))
            for j in range(KC):
                norm_sum(5, j)
            ch.link(nc.vector.memset(xpad[:, :, 0:3], 0.0))
            norm_split(5, 4)

            with dve.Fori(0, 2) as i:
                ch.enter(i, 5 * 4)
                for s in range(2):
                    for c in range(2):
                        k = 2 * s + c
                        x = x4[:, i * 4 + k, :]
                        dve.wait_ge(xp_ready, i * 4 + (k + 1))
                        ch.link(ts(x, xpad[:, c, 3:3 + S], vec_i(V_C4W + 3 * KC, i, 4, k), vec_i(V_C4B, i, 4, k),
                                   ALU.mult, ALU.add))
                        for tap in range(3):
                            ch.link(stt(x, xpad[:, c, tap:tap + S], vec_i(V_C4W + tap * KC, i, 4, k), x,
                                        ALU.mult, ALU.add))
                        ch.link(cp(x4_hi[:, i * 4 + k, :], x))
                        tt(x4_lo[:, i * 4 + k, :], x, x4_hi[:, i * 4 + k, :].bitcast(F32), ALU.subtract)\
                            .then_inc(x4_ready, 1)
            ch.leave(2)
            dve.wait_ge(group_free, GRP["cx"] + 2)
            with dve.Fori(0, KC // 2) as i:
                ch.enter(i, 8)
                for s in range(2):
                    j = i * 2 + s
                    g = GRP["cx"] + s
                    ts(sq[:, s, :], rr[:, j, :], spl[:, 0, bass.ds(j, 1)], None, ALU.mult).then_inc(z8_ready, 1)
                    ch.link(tt(ii[:, j, :], ii[:, j, :], x4[:, j, :], ALU.mult))
                    dve.wait_ge(decay_ready, i * 4 + (2 * s + 2))
                    ch.link(tt(un[:, 0, :], rr[:, j, :], rr[:, j, :], ALU.mult))
                    stt(x4[:, j, :], un[:, 0, :], 1.0, sq[:, s, :], ALU.add, ALU.mult).then_inc(m2_ready, 1)
                    dve.wait_ge(xs_ready, i * 2 + (s + 1))
                    tt(xpad[:, s, 3:3 + S], pair(g)[0][:], rstd[:], ALU.mult).then_inc(group_free, 1)
                    dve.wait_ge(group_free, i * 2 + (g + 3))
                    ch.link(ts(cc[:, j, :], xpad[:, s, 3:3 + S], vec_i(V_C3W + 2 * KC, i, 2, s), None, ALU.mult))
                    for tap in range(2):
                        ins = stt(cc[:, j, :], xpad[:, s, 1 + tap:1 + tap + S], vec_i(V_C3W + tap * KC, i, 2, s),
                                  cc[:, j, :], ALU.mult, ALU.add)
                        if tap == 0:
                            ch.link(ins)
            ch.leave(KC // 2)
            ch.link(nc.vector.memset(ssq[:], 0.0))
            with dve.Fori(0, KC // 2) as i:
                ch.enter(i, 4)
                for s in range(2):
                    j = i * 2 + s
                    g = GRP["bg"] + s
                    dve.wait_ge(mult_ready, i * 2 + (s + 1))
                    ch.link(tt(ii[:, j, :], ii[:, j, :], sq[:, s, :], ALU.mult))
                    nc.vector.tensor_tensor_scan(rr[:, j, :], rr[:, j, :], ii[:, j, :], 0.0, ALU.mult, ALU.add)
                    dve.wait_ge(sgc_ready, i * 2 + (s + 1))
                    ch.link(tt(un[:, 0, :], pair(g)[0][:], cc[:, j, :], ALU.mult))
                    tt(cc[:, j, :], un[:, 0, :], rstd[:], ALU.mult).then_inc(group_free, 1)
            ch.leave(KC // 2)
            dve.wait_ge(group_free, GRP["yg"] + 2)
            with dve.Fori(0, KC // 2) as i:
                ch.enter(i, 6)
                for s in range(2):
                    j = i * 2 + s
                    g = GRP["yg"] + s
                    dve.wait_ge(gel_ready, i * 4 + (2 * s + 2))
                    tt(un[:, 0, :], gel[:], rstd[:], ALU.mult).then_inc(group_free, 1)
                    dve.wait_ge(group_free, i * 2 + (g + 3))
                    ch.link(tt(un[:, 0, :], un[:, 0, :], rr[:, j, :], ALU.mult))
                    ch.link(tt(un[:, 1, :], un[:, 0, :], cc[:, j, :], ALU.add))
                    ch.link(cp(m_hi[:, j, :], un[:, 1, :]))
                    tt(m_lo[:, j, :], un[:, 1, :], m_hi[:, j, :].bitcast(F32), ALU.subtract).then_inc(mg_ready, 1)
            ch.leave(KC // 2)
            residual(PAN["rg_out"], GRP["rg_out"], 1, 5, 6)
            norm_split(6, 5)
            ffn(2, 6, 7)
            norm_split(7, 6)
            ch.link(nc.vector.memset(ssq[:], 0.0))
            for q in range(4):
                for c in range(2):
                    j = 2 * q + c
                    dve.wait_ge(sgate_ready, j + 1)
                    ch.link(tt(un[:, c, :], un[:, c, :], pp[:, j, :], ALU.mult))
                    tt(h[:, j, :], h[:, j, :], un[:, c, :], ALU.add).then_inc(h_ready, 1)
                dve.sem_inc(group_free, 1)
                for c in range(2):
                    norm_sum(8, 2 * q + c)
            norm_in_place(8)

        @block.tensor
        def _(pe):
            def mm(out, lhsT, rhs, start=True, stop=True):
                return nc.tensor.matmul(out, lhsT, rhs, start=start, stop=stop, skip_group_check=True)

            def at(c, i, step):
                return c if i is None else i * step + c

            def panel(p, g, x_hi, x_lo, i=None, pstep=2, gstep=2, ks=tuple(range(KC)), first=True, last=True,
                      inputs=None):
                s, nk = p % 2, len(ks)
                w = [t[:, s, :].rearrange("p (k c) -> p k c", c=HALF) for t in (w_hi, w_lo)]
                pe.wait_ge(hi_ready, at(p + 1, i, pstep))
                if first:
                    pe.wait_ge(group_free, at(g + 1, i, gstep))
                for n, k in enumerate(ks):
                    if inputs is not None:
                        pe.wait_ge(inputs[0], inputs[1] + k + 1)
                    for c in range(2):
                        mm(pair(g)[c][:], w[0][:, n, c * P:(c + 1) * P], x_hi[:, k, :], first and n == 0, False)
                        mm(pair(g)[c][:], w[0][:, n, c * P:(c + 1) * P], x_lo[:, k, :], False, False)
                pe.wait_ge(lo_ready, at(p + 1, i, pstep))
                for c in range(2):
                    for n, k in enumerate(ks):
                        ins = mm(pair(g)[c][:], w[1][:, n, c * P:(c + 1) * P], x_hi[:, k, :], False,
                                 last and n == nk - 1)
                ins.then_inc(panel_done, 1)

            def project(name, n, x_hi, x_lo, inputs):
                with pe.Fori(0, n // 2) as i:
                    for s in range(2):
                        panel(PAN[name] + s, GRP[name] + s, x_hi, x_lo, i, inputs=inputs if s == 0 else None)

            def residual(name, x_hi, x_lo, cuts, inputs):
                per = len(cuts) - 1
                with pe.Fori(0, 2) as i:
                    for s in range(2):
                        for t in range(per):
                            panel(PAN[name] + per * s + t, GRP[name] + s, x_hi, x_lo, i, 2 * per, 2,
                                  tuple(range(cuts[t], cuts[t + 1])), t == 0, t == per - 1,
                                  inputs if s == 0 else None)

            def by_tokens(name, i, tile_of):
                for s in range(2):
                    p = PAN[name] + s
                    sl = p % 2
                    w = [t[:, sl, :].rearrange("p (k c) -> p k c", c=S) for t in (w_hi, w_lo)]
                    pe.wait_ge(hi_ready, at(p + 1, i, 2))
                    pe.wait_ge(lo_ready, at(p + 1, i, 2))
                    if s == 0:
                        pe.wait_ge(group_free, at(GRP[name] + 2, i, 2))
                    for t in range(TT):
                        for n in range(4):
                            k = 4 * s + n
                            for a, (x, v) in enumerate(((u_hi, w[0]), (u_lo, w[0]), (u_hi, w[1]))):
                                ins = mm(PB[t][:], tile_of(x[:, k, :], t), v[:, n, :], k == 0 and a == 0,
                                         k == KC - 1 and a == 2)
                    ins.then_inc(panel_done, 1)

            def norm(n):
                pe.wait_ge(sum_added, KC * (n + 1))
                mm(MS[:], ones[:], ssq[:]).then_inc(ms_ready, 1)

            def near(t, n):
                return t[:, n * P:(n + 1) * P]

            def far(t, n):
                return t[:, n::TT]

            def ffn(f, m):
                project(f"up{f}", FT, u_hi, u_lo, (u_ready, KC * m))
                residual(f"down{f}", act_hi, act_lo, (0, 8, 16, FT), (act_ready, FT * f))

            pe.sem_inc(group_free, 2)
            pe.sem_inc(lev_done, 8)
            pe.sem_inc(lev_free, 2)
            pe.wait_ge(consts_ready, 3)
            norm(0)
            project("f", 4, u_hi, u_lo, (u_ready, 0))
            project("q", 4, u_hi, u_lo, None)
            with pe.Fori(0, 2) as i:
                by_tokens("i", i, near)
            project("g", 4, u_hi, u_lo, None)

            pe.wait_ge(group_free, GRP["hgrn_out"] + 2)
            pe.wait_ge(const_loaded, 80)
            with pe.Fori(0, HG) as i:
                for l in range(len(LEVELS) + 1):
                    diag = l == len(LEVELS)
                    if diag:
                        pe.wait_ge(heads_copied, i + 1)
                    else:
                        pe.wait_ge(z_ready, i * len(LEVELS) + (l + 1))
                    pe.wait_ge(lev_free, i * 8 + (l + 1))
                    for c in range(TT):
                        a = key_h if diag else zl[:, l, :]
                        b = query[:, i, :] if diag else zl[:, l, :]
                        ins = mm(near(PB[5 + l % 2], c), near(a, c), near(b, c))
                    ins.then_inc(lev_done, 1)
                pe.wait_ge(dec_ready, i + 1)
                for c in range(TT - 1):
                    ins = nc.tensor.transpose(near(PB[7], c), near(k_end, c), ident[:])
                ins.then_inc(ket_done, 1)
                pe.wait_ge(ket_ready, i + 1)
                for c in range(TT - 1):
                    ins = mm(near(KV, c), k_endt[:, c, :], val_h[:, c, :])
                ins.then_inc(kv_done, 1)
                pe.wait_ge(states_ready, i + 1)
                pe.wait_ge(lev_free, i * 8 + 10)
                for c in range(TT):
                    ins = mm(near(OB, c), val_h[:, c, :], near(sc, c), True, c == 0)
                    if c:
                        ins = mm(near(OB, c), state[:, c - 1, :], near(q_dec, c), False, True)
                ins.then_inc(o_done, 1)
                pe.wait_ge(osq_ready, i + 1)
                mm(MS[:], ones[:], sq[:, 0, :]).then_inc(oms_done, 1)

            residual("hgrn_out", o_hi, o_lo, (0, KC), (oh_ready, 0))
            norm(1)
            ffn(0, 1)
            norm(2)
            project("aq", 2 * AH // 2, u_hi, u_lo, (u_ready, KC * 2))
            for g in range(3):
                tile_of = far if g else near
                by_tokens_at = g
                for s in range(2):
                    p = PAN["av"] + 2 * g + s
                    w = [t[:, p % 2, :].rearrange("p (k c) -> p k c", c=S) for t in (w_hi, w_lo)]
                    pe.wait_ge(hi_ready, p + 1)
                    pe.wait_ge(lo_ready, p + 1)
                    if s == 0:
                        pe.wait_ge(group_free, GRP["av"] + 2 * g + 2)
                    for t in range(TT):
                        for n in range(4):
                            k = 4 * s + n
                            for a, (x, v) in enumerate(((u_hi, w[0]), (u_lo, w[0]), (u_hi, w[1]))):
                                ins = mm(PB[t][:], tile_of(x[:, k, :], t), v[:, n, :], k == 0 and a == 0,
                                         k == KC - 1 and a == 2)
                    ins.then_inc(panel_done, 1)

            for g in range(3):
                tile_of = far if g else near
                with pe.Fori(0, GH) as i:
                    hd = i + GH * g
                    pe.wait_ge(qv_copied, i + (GH * g + 1))
                    for n in range(TT):
                        ins = mm(near(PB[5], n), tile_of(q_h, n), tile_of(aqk[:, hd + AH, :], n))
                        if g == 0 and n:
                            ins = mm(near(PB[6], n), near(q_h, n), near(aqk[:, hd + AH, :], n - 1))
                    ins.then_inc(s_done, 1)
                    pe.wait_ge(p_ready, i + (GH * g + 1))
                    for n in range(TT):
                        ins = nc.tensor.transpose(near(PB[7], n), s_a[:, n, :], ident[:])
                        if g == 0 and n:
                            ins = nc.tensor.transpose(near(MS, n), s_b[:, n, :], ident[:])
                    ins.then_inc(pt_done, 1)
                    pe.wait_ge(pt_ready, i + (GH * g + 1))
                    pe.wait_ge(oraw_ready, hd)
                    for n in range(TT):
                        ins = mm(near(OB, n), v_h[:, n, :], pt_a[:, n, :], True, g > 0 or n == 0)
                        if g == 0 and n:
                            ins = mm(near(OB, n), v_h[:, n - 1, :], pt_b[:, n, :], False, True)
                    ins.then_inc(pv_done, 1)
            pe.wait_ge(oraw_ready, AH)
            for src, bank in ((lst, 0), (mst, 5)):
                for g in range(3):
                    for n in range(TT):
                        ins = nc.tensor.transpose(PB[bank + g][0:GH, n * P:(n + 1) * P],
                                                  src[:, GH * g:GH * (g + 1), n], ident[:])
            ins.then_inc(rows_done, 1)
            pe.wait_ge(fac_ready, 1)
            with pe.Fori(0, 3) as i:
                pe.wait_ge(ao_ready, i * GH)
                for k in range(GH):
                    mm(FAC[k][:], sel[:, k, :], mrow[:, i, :]).then_inc(fac_done, 1)
            residual("attn_out", ao_hi, ao_lo, (0, 6, AH), (ao_ready, 0))
            norm(3)
            ffn(1, 3)
            norm(4)
            norm(5)
            project("rx", 4, u_hi, u_lo, (u_ready, KC * 4))
            for s in range(2):
                p = PAN["rg"] + s
                w = [t[:, p % 2, :].rearrange("p (k c) -> p k c", c=HALF) for t in (w_hi, w_lo)]
                pe.wait_ge(lo_ready, p + 1)
                for q in range(4):
                    g = GRP["rg"] + 4 * s + q
                    pe.wait_ge(group_free, g + 1)
                    pe.wait_ge(x4_ready, 2 * q + 2)
                    for c in range(2):
                        for n in range(2):
                            k = 2 * q + n
                            for a, (v, x) in enumerate(((w[0], x4_hi), (w[0], x4_lo), (w[1], x4_hi))):
                                ins = mm(pair(g)[c][:], v[:, k, c * P:(c + 1) * P], x[:, k, :],
                                         n == 0 and a == 0, n == 1 and a == 2)
                    ins.then_inc(gate_done, 1)
                pe.wait_ge(gate_done, 4 * s + 4)
                pe.sem_inc(panel_done, 1)
            project("cx", KC, u_hi, u_lo, None)
            project("bg", KC, u_hi, u_lo, None)
            project("yg", KC, u_hi, u_lo, None)
            residual("rg_out", m_hi, m_lo, (0, KC), (mg_ready, 0))
            norm(6)
            ffn(2, 5)
            norm(7)
            p = PAN["ple"]
            w = [t[:, p % 2, :].rearrange("p (k c) -> p k c", c=DM) for t in (w_hi, w_lo)]
            pe.wait_ge(lo_ready, p + 1)
            pe.wait_ge(pf_ready, 1)
            for q in range(4):
                g = GRP["ple"] + q
                pe.wait_ge(group_free, g + 1)
                for c in range(2):
                    j = 2 * q + c
                    for k in range(2):
                        for a, (v, x) in enumerate(((w[0], p_hi), (w[0], p_lo), (w[1], p_hi))):
                            ins = mm(pair(g)[c][:], v[:, k, j * P:(j + 1) * P], x[:, k, :],
                                     k == 0 and a == 0, k == 1 and a == 2)
                ins.then_inc(side_done, 1)
            pe.wait_ge(side_done, 4)
            pe.sem_inc(panel_done, 1)
            project("gate", 4, u_hi, u_lo, (u_ready, KC * 6))
            norm(8)


def _tiles(v):
    return np.asarray(v).reshape(-1, P).T


def _panel(w, ks, cols):
    t = np.asarray(w).reshape(-1, P, w.shape[-1])[list(ks)][:, :, cols]
    t = t.transpose(1, 0, 2).reshape(P, -1)
    return np.pad(t, ((0, 0), (0, PANEL - t.shape[1])))


def _panels(i):
    def cols(*starts):
        return np.concatenate([np.arange(c, c + P) for c in starts])

    def whole(w, first, n):
        return [_panel(w, range(KC), cols(first + 256 * k, first + 256 * k + P)) for k in range(n)]

    def paired(w, a, b, n):
        return [_panel(w, range(KC), cols(a + P * k, b + P * k)) for k in range(n)]

    def by_tokens(w, first, n):
        return [_panel(w, range(4 * s, 4 * s + 4), np.arange(first + S * k, first + S * (k + 1)))
                for k in range(n) for s in range(2)]

    def cut(w, cuts):
        return [_panel(w, range(a, b), cols(256 * k, 256 * k + P))
                for k in range(4) for a, b in zip(cuts, cuts[1:])]

    def ffn(w_in, w_down):
        return paired(w_in, 0, DFF, FT), cut(w_down, (0, 8, 16, FT))

    hin, qkv, w2 = i["hgrn_w_in"][0], i["attn_w_qkv"][0], i["w_in_2"][0]
    aw = AH * P
    up0, down0 = ffn(i["ffn_w_in"][0], i["ffn_w_down"][0])
    up1, down1 = ffn(i["ffn_w_in"][1], i["ffn_w_down"][1])
    up2, down2 = ffn(i["w_gate_up_2"][0], i["w_down_2"][0])
    out = whole(hin, DM, 4) + whole(hin, 0, 4) + by_tokens(hin, 2 * DM, 2) + whole(hin, 3 * DM, 4)
    out += whole(i["hgrn_w_out"][0], 0, 4) + up0 + down0
    out += whole(qkv, 0, 12) + by_tokens(qkv, 2 * aw, 3) + cut(i["attn_w_out"][0], (0, 6, 12)) + up1 + down1
    out += whole(w2, 0, 4)
    out += [_panel(i[k][0].reshape(DM, 256), range(KC), np.arange(256)) for k in ("w_rg_r_2", "w_rg_i_2")]
    out += paired(w2, 3 * DM, 4 * DM, KC) + paired(w2, 2 * DM, 6 * DM, KC) + paired(w2, DM, 5 * DM, KC)
    out += whole(i["w_out_2"][0], 0, 4) + up2 + down2
    out += [_panel(i["w_ple_2"][0], range(2), np.arange(DM))] + whole(i["w_ple_gate_2"][0], 0, 4)
    assert len(out) == PAN["end"]
    return np.stack(out)


def _vecs(i):
    v = [i["norm_mix"][0], i["norm_ffn"][0], i["norm_mix"][1], i["norm_ffn"][1], i["final_norm"],
         i["g_mix_2"][0], i["g_ffn_2"][0], i["g_ple_2"][0], i["g_final_2"],
         *i["hgrn_lb_logits"], i["hgrn_out_norm"][0], *i["conv4_w_2"][0], i["conv4_b_2"][0],
         i["b_rg_r_2"][0].reshape(-1), i["b_rg_i_2"][0].reshape(-1), i["lru_lambda_2"][0], *i["conv3_w_2"][0]]
    return np.concatenate([_tiles(a) for a in v], axis=1)


def _constants():
    inv = 1.0 / (np.float32(10000.0) ** (np.arange(0, P, 2, dtype=np.float32) / np.float32(P)))
    ang = inv.astype(np.float32)[:, None] * np.arange(S, dtype=np.float32)[None, :]
    cos, sin = np.cos(ang), np.sin(ang)
    cs = np.stack([np.concatenate([cos, cos]), np.concatenate([-sin, sin])], axis=1)
    a, b = np.meshgrid(np.arange(P), np.arange(P), indexing="ij")
    lm = [(a // (2 * m) == b // (2 * m)) & (a % (2 * m) < m) & (b % (2 * m) >= m) for m in LEVELS]
    lmask = np.stack([*lm, a == b], axis=1).astype(np.float32)
    am = [b <= a, b >= a, (b <= a) & (b % 4 == a % 4)]
    amask = np.stack([np.where(m, 0.0, MASKED) for m in am] + [lm[0].astype(np.float64)], axis=1)
    sel = np.zeros((GH, GH, P), np.float32)
    for k in range(GH):
        sel[k, k] = 1.0
    return np.eye(P, dtype=np.float32), cs.astype(np.float32), lmask, amask.astype(np.float32), sel


def kernel(**inputs):
    import concourse.bacc as _bacc
    from concourse.bass_utils import run_bass_kernel_spmd as _run

    i = {k: np.asarray(v) for k, v in inputs.items()}
    ident, cs, lmask, amask, sel = _constants()
    arrays = {
        "wall": _panels(i), "x_t": np.ascontiguousarray(i["x"][0].T), "p_t": np.ascontiguousarray(i["p_2"][0, 0].T),
        "vecs_in": np.ascontiguousarray(_vecs(i)), "ident_in": ident, "cs_in": cs, "lmask_in": lmask,
        "amask_in": amask, "sel_in": sel,
    }
    nc = _bacc.Bacc("TRN2", target_bir_lowering=False, num_devices=1)
    args = [nc.dram_tensor(k, a.shape, mybir.dt.from_np(a.dtype), kind="ExternalInput").ap()
            for k, a in arrays.items()]
    out = nc.dram_tensor("out_t", (DM, S), F32, kind="ExternalOutput").ap()
    build(nc, *args, out)
    r = _run(nc, [arrays], core_ids=[0])
    return np.ascontiguousarray(r.results[0]["out_t"].T)[None]
```

```python
from contextlib import ExitStack

import numpy as np

import concourse.bass as bass
from concourse import mybir

F32 = mybir.dt.float32
F32R = mybir.dt.float32r
U8 = mybir.dt.uint8
ALU = mybir.AluOpType
ACT = mybir.ActivationFunctionType
AX_X = mybir.AxisListType.X

P = 128
S = 512
DM = 1024
KC = DM // P
DFF = 2816
FT = DFF // P
TT = S // P
HG = 8
AH = 12
GH = 4
PLE = 256
PANEL = 2048
HALF = PANEL // KC
LEVELS = (64, 32, 16, 8, 4, 2, 1)
RING = 4
EPS = 1e-6
ATT_SCALE = 128 ** -0.5
MASKED = -1e30
RG_C = 8.0

V_NORM = 0
V_LB = V_NORM + 9 * KC
V_HG = V_LB + 3 * KC
V_C4W = V_HG + 1
V_C4B = V_C4W + 4 * KC
V_BR = V_C4B + KC
V_BI = V_BR + KC
V_LAM = V_BI + KC
V_C3W = V_LAM + KC
V_ALL = V_C3W + 3 * KC


def panel_plan():
    at, first = 0, {}
    for name, n in (("f", 4), ("q", 4), ("i", 4), ("g", 4), ("hgrn_out", 4),
                    ("up0", FT), ("down0", 12),
                    ("a0", 6), ("a1", 6), ("a2", 6), ("attn_out", 8),
                    ("up1", FT), ("down1", 12),
                    ("rx", 4), ("rg", 2), ("cx", 8), ("bg", 8), ("yg", 8), ("rg_out", 4),
                    ("up2", FT), ("down2", 12), ("ple", 1), ("gate", 4)):
        first[name] = at
        at += n
    first["end"] = at
    return first


def group_plan():
    at, first = 0, {}
    for name, n in (("f", 4), ("q", 4), ("i", 4), ("g", 4), ("hgrn_out", 4),
                    ("up0", FT), ("down0", 4),
                    ("a0", 6), ("a1", 6), ("a2", 6), ("attn_out", 4),
                    ("up1", FT), ("down1", 4),
                    ("rx", 4), ("rg", 8), ("cx", 8), ("bg", 8), ("yg", 8), ("rg_out", 4),
                    ("up2", FT), ("down2", 4), ("ple", 4), ("gate", 4)):
        first[name] = at
        at += n
    return first


PAN = panel_plan()
GRP = group_plan()


class Chain:

    def __init__(self, eng, sem):
        self.eng, self.sem, self.base, self.k, self.i, self.per = eng, sem, 0, 0, None, 0

    def now(self):
        return self.base + self.k if self.i is None else self.per * self.i + (self.base + self.k)

    def step(self, ins):
        ins.then_inc(self.sem, 1)
        self.k += 1

    def settle(self):
        self.eng.wait_ge(self.sem, self.now())

    def link(self, ins):
        self.step(ins)
        self.settle()

    def enter(self, i, per):
        self.base += self.k
        self.k, self.i, self.per = 0, i, per

    def leave(self, n):
        assert self.k == self.per, f"{self.k} steps in the body, {self.per} stated"
        self.base += self.per * n
        self.k, self.i = 0, None


def build(nc, wall, x_t, p_t, vecs_d, ident_d, cs_d, lmask_d, amask_d, sel_d, out_t):
    with ExitStack() as ctx:
        UNIT = 4 * S

        def sb(name, shape, dt=F32):
            return ctx.enter_context(nc.sbuf_tensor(name, shape, dt))

        def sem(name):
            return ctx.enter_context(nc.semaphore(name))

        h = sb("h", [P, KC, S])
        raw = sb("raw", [P, 2, PANEL])
        w_hi = sb("w_hi", [P, 2, PANEL], F32R)
        w_lo = sb("w_lo", [P, 2, PANEL], F32R)
        sq = sb("sq", [P, 2, S])
        un = sb("un", [P, 2, S])
        ssq = sb("ssq", [P, S])
        rstd = sb("rstd", [P, S])
        ones = sb("ones", [P, P])
        ident = sb("ident", [P, P])
        vecs = sb("vecs", [P, V_ALL])
        eps = sb("eps", [P, 1])
        lb = sb("lb", [P, 6, KC])
        spl = sb("spl", [P, 6, KC])
        lmask = sb("lmask", [P, len(LEVELS) + 1, P], U8)
        amask = sb("amask", [P, 4, P])
        sel = sb("sel", [GH, GH, P])
        mst = sb("mst", [P, AH, TT])
        lst = sb("lst", [P, AH, TT])
        cols = sb("cols", [P, 8, TT])

        k_endt = sb("k_endt", [P, 3, P])
        state = sb("state", [P, 3, P])
        b_last = sb("b_last", [P, TT])
        e_last = sb("e_last", [P, TT])

        region = {}
        region["u"] = (nc.sbuf_base + 31) // 32 * 32
        sb("region_u", [P, 2 * KC * S])
        region["a"] = (nc.sbuf_base + 31) // 32 * 32
        sb("region_a", [P, 2 * FT * S])

        def place(name, where, unit, shape, dt=F32):
            return nc.alloc_sbuf_tensor_at(name, shape, dt, offset=region[where] + int(unit * UNIT))

        u_hi = place("u_hi", "u", 0, [P, KC, S], F32R)
        u_lo = place("u_lo", "u", KC, [P, KC, S], F32R)
        act_hi = place("act_hi", "a", 0, [P, FT, S], F32R)
        act_lo = place("act_lo", "a", FT, [P, FT, S], F32R)
        query = place("query", "a", 0, [P, HG, S])
        key = place("key", "a", 8, [P, HG, S])
        o_hi = place("o_hi", "a", 0, [P, HG, S], F32R)
        o_lo = place("o_lo", "a", 8, [P, HG, S], F32R)
        cum = place("cum", "a", 16, [P, HG, S])
        val = place("val", "a", 24, [P, TT, DM])
        gate = place("gate", "a", 32, [P, 4, S])
        lmask_f = place("lmask_f", "a", 41, [P, len(LEVELS) + 1, P])
        one_s = place("one_s", "a", 40, [P, P])
        zl = place("zl", "a", 36, [P, RING, S])
        q_dec = place("q_dec", "a", 40, [P, S])
        k_end = place("k_end", "a", 41, [P, S])
        scores = [place("scores0", "a", 42, [P, S]), place("scores1", "a", 43, [P, S])]
        aqk = place("aqk", "a", 0, [P, 2 * AH, S])
        av = place("av", "a", 24, [P, 3, TT, S])
        o_raw = place("o_raw", "a", 0, [P, AH, S])
        ao_hi = place("ao_hi", "a", 12, [P, AH, S], F32R)
        ao_lo = place("ao_lo", "a", 24, [P, AH, S], F32R)
        cs = place("cs", "a", 36, [P, 2, S])
        rot = place("rot", "a", 38, [P, 2, S])
        s_ab = [place("s_a", "a", 40, [P, TT, P]), place("s_b", "a", 41, [P, TT, P])]
        pt_ab = [place("pt_a", "a", 42, [P, TT, P]), place("pt_b", "a", 43, [P, TT, P])]
        mrow = place("mrow", "u", 6, [GH, 3, S])
        lrow = place("lrow", "u", 9, [GH, 3, S])
        erow = place("erow", "u", 12, [GH, 3, S])
        trow = place("trow", "u", 15, [GH, S])
        x4 = place("x4", "a", 0, [P, KC, S])
        x4_hi = place("x4_hi", "a", 8, [P, KC, S], F32R)
        x4_lo = place("x4_lo", "a", 16, [P, KC, S], F32R)
        rr = place("rr", "a", 24, [P, KC, S])
        ii = place("ii", "a", 32, [P, KC, S])
        m_hi = place("m_hi", "a", 0, [P, KC, S], F32R)
        cc = place("cc", "a", 8, [P, KC, S])
        m_lo = place("m_lo", "a", 16, [P, KC, S], F32R)
        xpad = place("xpad", "a", 40, [P, 2, S + 8])
        gel = place("gel", "a", 42.5, [P, S])
        pf = place("pf", "u", 0, [P, 2, S])
        p_hi = place("p_hi", "u", 12, [P, 2, S], F32R)
        p_lo = place("p_lo", "u", 14, [P, 2, S], F32R)
        pp = place("pp", "a", 0, [P, KC, S])

        PB = [ctx.enter_context(nc.psum_tensor(f"bank{i}", [P, S], F32)) for i in range(8)]
        MS = PB[4]
        HB = PB[7]
        FAC = [PB[5], PB[6], PB[7], PB[3]]

        def pair(g):
            return PB[2 * (g % 2)], PB[2 * (g % 2) + 1]

        raw_loaded = [sem("raw_loaded0"), sem("raw_loaded1")]
        x_loaded = sem("x_loaded")
        p_loaded = sem("p_loaded")
        const_loaded = sem("const_loaded")
        cs_loaded = sem("cs_loaded")
        out_stored = sem("out_stored")
        hi_ready = sem("hi_ready")
        lo_ready = sem("lo_ready")
        panel_done = sem("panel_done")
        group_free = sem("group_free")
        consts_ready = sem("consts_ready")
        waits_apart = sem("waits_apart")
        act_chain = sem("act_chain")
        dve_chain = sem("dve_chain")
        masks_ready = sem("masks_ready")
        h_ready = sem("h_ready")
        sq_ready = sem("sq_ready")
        sum_added = sem("sum_added")
        ms_ready = sem("ms_ready")
        rstd_ready = sem("rstd_ready")
        un_ready = sem("un_ready")
        uhi_ready = sem("uhi_ready")
        u_ready = sem("u_ready")
        sg_ready = sem("sg_ready")
        act_ready = sem("act_ready")
        fsig_ready = sem("fsig_ready")
        logf_ready = sem("logf_ready")
        cum_ready = sem("cum_ready")
        diff_ready = sem("diff_ready")
        exp_ready = sem("exp_ready")
        z_ready = sem("z_ready")
        lev_done = sem("lev_done")
        lev_free = sem("lev_free")
        blast_ready = sem("blast_ready")
        ends_ready = sem("ends_ready")
        dec_ready = sem("dec_ready")
        ket_done = sem("ket_done")
        ket_ready = sem("ket_ready")
        kv_done = sem("kv_done")
        states_ready = sem("states_ready")
        o_done = sem("o_done")
        osq_ready = sem("osq_ready")
        oms_done = sem("oms_done")
        orstd_ready = sem("orstd_ready")
        on_ready = sem("on_ready")
        oh_ready = sem("oh_ready")
        rot_ready = sem("rot_ready")
        v_ready = sem("v_ready")
        qk_ready = sem("qk_ready")
        s_done = sem("s_done")
        max_ready = sem("max_ready")
        p_ready = sem("p_ready")
        pt_done = sem("pt_done")
        pt_ready = sem("pt_ready")
        pv_done = sem("pv_done")
        oraw_ready = sem("oraw_ready")
        rows_done = sem("rows_done")
        row_log = sem("row_log")
        row_diff = sem("row_diff")
        row_exp = sem("row_exp")
        row_sum = sem("row_sum")
        row_logsum = sem("row_logsum")
        row_fac = sem("row_fac")
        fac_ready = sem("fac_ready")
        fac_done = sem("fac_done")
        ao_ready = sem("ao_ready")
        xp_ready = sem("xp_ready")
        x4_ready = sem("x4_ready")
        z8_ready = sem("z8_ready")
        decay_ready = sem("decay_ready")
        m2_ready = sem("m2_ready")
        mult_ready = sem("mult_ready")
        xs_ready = sem("xs_ready")
        sgc_ready = sem("sgc_ready")
        gel_ready = sem("gel_ready")
        mg_ready = sem("mg_ready")
        lam_exp = sem("lam_exp")
        lb_exp = sem("lb_exp")
        lb_in = sem("lb_in")
        pf_ready = sem("pf_ready")
        sgate_ready = sem("sgate_ready")
        gate_done = sem("gate_done")
        side_done = sem("side_done")

        def wait_apart(eng, s, value):
            eng.wait_ge(s, value)
            eng.sem_inc(waits_apart, 1)

        def vec(first, j):
            return vecs[:, first + j:first + j + 1]

        def vec_i(first, i, step, s):
            return vecs[:, bass.ds(i * step + (first + s), 1)]

        def before_level(h, l):
            n = len(LEVELS) * h + l - RING
            return 8 * (n // len(LEVELS)) + n % len(LEVELS) + 1

        def level_tile(h, l):
            return zl[:, (len(LEVELS) * h + l) % RING, :]

        A1 = PAN["a1"]
        HEAD_STEPS = {A1: (None, (0,)), A1 + 1: (0, (1,)), A1 + 2: (1, (2,)), A1 + 3: (2, (3,)), A1 + 4: (3, ()),
                      A1 + 6: (None, (4,)), A1 + 7: (4, (5,)), A1 + 8: (5, (6,)), A1 + 9: (6, (7,)),
                      A1 + 10: (7, (8,)), A1 + 11: (8, (9, 10))}
        HEAD_TAIL = ((9, (11,)), (10, ()), (11, ()))

        def score_bank(hd):
            return PB[5] if hd < GH else PB[5 + hd % 2]

        def turn_bank(hd):
            return PB[7] if hd < GH or hd % 2 == 0 else MS

        def buf(hd):
            return 0 if hd < GH else hd % 2

        def blocks(t, m):
            return t.rearrange("p (n c) -> p n c", c=2 * m)

        def by_four(t):
            return t.rearrange("p (a r) -> p r a", r=TT)

        block = ctx.enter_context(nc.Block())

        @block.sync
        def _(sp):
            def load_panels(a, b):
                n = (b - a) // 2
                with sp.Fori(0, n) as i:
                    for s in range(2):
                        sp.wait_ge(lo_ready, i * 2 + (a + s - 1))
                        sp.dma_start(raw[:, (a + s) % 2, :], wall[i * 2 + (a + s)]).then_inc(raw_loaded[(a + s) % 2], 16)
                if (b - a) % 2:
                    sp.wait_ge(lo_ready, b - 2)
                    sp.dma_start(raw[:, (b - 1) % 2, :], wall[b - 1]).then_inc(raw_loaded[(b - 1) % 2], 16)

            x_v = x_t.rearrange("(k p) s -> p k s", p=P)
            sp.dma_start(h[:], x_v).then_inc(x_loaded, 16)
            for s in range(2):
                sp.dma_start(raw[:, s, :], wall[s]).then_inc(raw_loaded[s], 16)
            sp.dma_start(vecs[:], vecs_d).then_inc(const_loaded, 16)
            sp.dma_start(ident[:], ident_d).then_inc(const_loaded, 16)
            sp.dma_start(amask[:], amask_d).then_inc(const_loaded, 16)
            sp.dma_start(lmask_f[:], lmask_d).then_inc(const_loaded, 16)
            sp.dma_start(sel[:], sel_d).then_inc(const_loaded, 16)
            load_panels(2, PAN["a0"] + 2)
            sp.wait_ge(panel_done, PAN["a0"])
            sp.dma_start(cs[:], cs_d).then_inc(cs_loaded, 16)
            load_panels(PAN["a0"] + 2, PAN["down2"] + 2)
            sp.wait_ge(panel_done, PAN["down2"])
            sp.dma_start(pf[:], p_t.rearrange("(k p) s -> p k s", p=P)).then_inc(p_loaded, 16)
            load_panels(PAN["down2"] + 2, PAN["end"])
            out_v = out_t.rearrange("(k p) s -> p k s", p=P)
            for j in range(0, KC, 2):
                sp.wait_ge(h_ready, 8 * KC + j + 2)
                sp.dma_start(out_v[:, j:j + 2, :], h[:, j:j + 2, :]).then_inc(out_stored, 16)
            sp.wait_ge(out_stored, 16 * KC // 2)

        @block.gpsimd
        def _(pool):
            def lo(p, s, i=None):
                q = p if i is None else i * 2 + p
                pool.wait_ge(hi_ready, q + 1)
                nc.gpsimd.tensor_tensor(w_lo[:, s, :], raw[:, s, :], w_hi[:, s, :].bitcast(F32),
                                        ALU.subtract).then_inc(lo_ready, 1)

            def lo_panels(a, b):
                n = (b - a) // 2
                with pool.Fori(0, n) as i:
                    for s in range(2):
                        lo(a + s, (a + s) % 2, i)
                if (b - a) % 2:
                    lo(b - 1, (b - 1) % 2)

            nc.gpsimd.memset(ones[:], 1.0).then_inc(consts_ready, 1)
            nc.gpsimd.memset(eps[:], EPS).then_inc(consts_ready, 1)
            nc.gpsimd.memset(one_s[:], 1.0).then_inc(consts_ready, 1)
            lo_panels(0, PAN["g"] + 2)

            def differences(h, levels):
                for l in levels:
                    m = LEVELS[l]
                    n = S // (2 * m)
                    b = blocks(cum[:, h, :], m)
                    pool.wait_ge(cum_ready, h + 1)
                    if (h, l) >= (0, RING):
                        pool.wait_ge(lev_done, before_level(h, l))
                    nc.gpsimd.tensor_tensor(blocks(level_tile(h, l), m), b,
                                            b[:, :, m - 1:m].to_broadcast([P, n, 2 * m]),
                                            ALU.subtract).then_inc(diff_ready, 1)

            differences(0, range(RING))
            for hd in range(HG):
                differences(hd, range(RING, len(LEVELS)))
                if hd % 2 == 0 and hd < 6:
                    p = PAN["g"] + hd // 2 + 2
                    lo(p, p % 2)
                pool.wait_ge(ends_ready, hd + 1)
                nc.gpsimd.tensor_tensor(k_end[:, 0:3 * P], k_end[:, 0:3 * P], key[:, hd, 0:3 * P], ALU.mult)
                nc.gpsimd.tensor_tensor(q_dec[:], q_dec[:], query[:, hd, :], ALU.mult).then_inc(dec_ready, 1)
                if hd + 1 < HG:
                    differences(hd + 1, range(RING))

            lo_panels(PAN["hgrn_out"] + 1, PAN["end"])


        @block.scalar
        def _(act):
            ch = Chain(act, act_chain)

            def af(out, in_, func, **k):
                return nc.scalar.activation(out, in_, func, **k)

            def conv(p, i=None, step=2):
                s = p % 2
                if i is None:
                    act.wait_ge(raw_loaded[s], 16 * (p // 2 + 1))
                    if p >= 2:
                        act.wait_ge(panel_done, p - 1)
                else:
                    act.wait_ge(raw_loaded[s], i * (8 * step) + 16 * (p // 2 + 1))
                    act.wait_ge(panel_done, i * step + (p - 1))
                af(w_hi[:, s, :], raw[:, s, :], ACT.Copy).then_inc(hi_ready, 1)

            def norm_sums_part(n, j, i=None, step=0):
                if n:
                    act.wait_ge(h_ready, KC * (n - 1) + j + 1 if i is None else i * step + (KC * (n - 1) + j + 1))
                if n or j >= 2:
                    act.wait_ge(sum_added, KC * n + j - 1 if i is None else i * step + (KC * n + j - 1))
                hj = h[:, j, :] if i is None else h[:, i * step + j, :]
                af(sq[:, j % 2, :], hj, ACT.Square).then_inc(sq_ready, 1)

            def norm_scale(n):
                act.wait_ge(ms_ready, n + 1)
                ch.link(af(rstd[:], MS[:], ACT.Ln, bias=eps[:, 0:1], scale=1.0 / DM))
                af(rstd[:], rstd[:], ACT.Exp, scale=-0.5).then_inc(rstd_ready, 1)

            def norm_upper(m):
                for j in range(KC):
                    act.wait_ge(un_ready, KC * m + j + 1)
                    af(u_hi[:, j, :], un[:, j % 2, :], ACT.Copy).then_inc(uhi_ready, 1)

            def residual(p0, per, n):
                with act.Fori(0, 2) as i:
                    for s in range(2):
                        for t in range(per):
                            conv(p0 + per * s + t + 1, i, 2 * per)
                        for c in range(2):
                            norm_sums_part(n, 2 * s + c, i, 4)

            def ffn(f, n):
                with act.Fori(0, FT // 2) as i:
                    for s in range(2):
                        p = PAN[f"up{f}"] + s
                        conv(p + 1, i)
                        act.wait_ge(group_free, i * 2 + (GRP[f"up{f}"] + s + 1))
                        act.wait_ge(panel_done, i * 2 + (p + 1))
                        af(sq[:, s, :], pair(GRP[f"up{f}"] + s)[0][:], ACT.Silu).then_inc(sg_ready, 1)
                residual(PAN[f"down{f}"], 3, n)

            act.wait_ge(x_loaded, 16)
            act.wait_ge(consts_ready, 3)
            for j in range(KC):
                norm_sums_part(0, j)
            conv(0)
            act.wait_ge(lb_in, 2)
            af(lb[:, 0:3, :], lb[:, 0:3, :], ACT.Exp).then_inc(lb_exp, 1)
            af(spl[:, 1, :], spl[:, 1, :], ACT.Exp).then_inc(lam_exp, 1)
            norm_scale(0)
            norm_upper(0)

            with act.Fori(0, 2) as i:
                for s in range(2):
                    p = PAN["f"] + s
                    conv(p + 1, i)
                    act.wait_ge(panel_done, i * 2 + (p + 1))
                    for c in range(2):
                        af(key[:, i * 4 + (2 * s + c), :], pair(GRP["f"] + s)[c][:], ACT.Sigmoid).then_inc(fsig_ready, 1)
            act.wait_ge(group_free, GRP["q"] + 2)
            with act.Fori(0, HG) as i:
                af(cum[:, i, :], cum[:, i, :], ACT.Ln).then_inc(logf_ready, 1)
            with act.Fori(0, 2) as i:
                for s in range(2):
                    p = PAN["q"] + s
                    conv(p + 1, i)
                    act.wait_ge(panel_done, i * 2 + (p + 1))
                    af(query[:, i * 4 + 2 * s, :], pair(GRP["q"] + s)[0][:], ACT.Silu)
                    af(query[:, i * 4 + (2 * s + 1), :], pair(GRP["q"] + s)[1][:], ACT.Silu).then_inc(group_free, 1)
            with act.Fori(0, 2) as i:
                for s in range(2):
                    conv(PAN["i"] + s + 1, i)
                act.wait_ge(panel_done, i * 2 + (PAN["i"] + 2))
                for t in range(TT):
                    ins = af(val[:, t, bass.ds(i * S, S)], PB[t][:], ACT.Copy)
                    if t % 2:
                        ins.then_inc(group_free, 1)
            def decays(hd, levels):
                for l in levels:
                    m = LEVELS[l]
                    act.wait_ge(diff_ready, len(LEVELS) * hd + l + 1)
                    z = blocks(level_tile(hd, l), m)
                    af(z[:, :, m:2 * m], z[:, :, m:2 * m], ACT.Exp)
                    af(z[:, :, 0:m], z[:, :, 0:m], ACT.Exp, scale=-1.0).then_inc(exp_ready, 1)

            def keys_by_token(hd):
                act.wait_ge(ket_done, hd + 1)
                af(k_endt[:].rearrange("p a b -> p (a b)"), HB[:, 0:3 * P], ACT.Copy).then_inc(ket_ready, 1)

            def squares(hd):
                act.wait_ge(o_done, hd + 1)
                af(sq[:, 0, :], HB[:], ACT.Square).then_inc(osq_ready, 1)

            def ends(hd):
                act.wait_ge(blast_ready, hd + 1)
                if hd:
                    act.wait_ge(o_done, hd)
                af(q_dec[:], cum[:, hd, :], ACT.Exp)
                for c in range(TT - 1):
                    af(k_end[:, c * P:(c + 1) * P], cum[:, hd, c * P:(c + 1) * P], ACT.Exp,
                       bias=b_last[:, c:c + 1], scale=-1.0)
                af(e_last[:], b_last[:], ACT.Exp).then_inc(ends_ready, 1)

            def root(hd):
                act.wait_ge(oms_done, hd + 1)
                ch.link(af(rstd[:], MS[:], ACT.Ln, bias=eps[:, 0:1], scale=1.0 / P))
                af(rstd[:], rstd[:], ACT.Exp, scale=-0.5).then_inc(orstd_ready, 1)

            conv(PAN["g"] + 1)
            decays(0, range(RING))
            for hd in range(HG):
                if hd:
                    keys_by_token(hd - 1)
                decays(hd, range(RING, len(LEVELS)))
                if hd % 2 == 0:
                    q = hd // 2
                    p, g = PAN["g"] + q, GRP["g"] + q
                    act.wait_ge(panel_done, p + 1)
                    if q >= 2:
                        act.wait_ge(oh_ready, 2 * q - 2)
                    for c in range(2):
                        ins = af(gate[:, (2 * q + c) % 4, :], pair(g)[c][:], ACT.Silu)
                    ins.then_inc(group_free, 1)
                    if hd < 6:
                        conv(p + 2)
                if hd:
                    squares(hd - 1)
                ends(hd)
                if hd:
                    root(hd - 1)
                if hd + 1 < HG:
                    decays(hd + 1, range(RING))
            keys_by_token(HG - 1)
            squares(HG - 1)
            root(HG - 1)
            residual(PAN["hgrn_out"], 1, 1)
            norm_scale(1)
            norm_upper(1)
            ffn(0, 2)
            norm_scale(2)
            norm_upper(2)

            def exps(hd):
                act.wait_ge(max_ready, hd + 1)
                r = 4 * (hd % 2)
                for n in range(TT):
                    s_n = s_ab[buf(hd)][:, n, :]
                    ins = af(s_n, s_n, ACT.Exp, bias=cols[:, r + 1, n:n + 1], scale=ATT_SCALE,
                             accum_out=cols[:, r + 2, n:n + 1])
                    if hd < GH and n:
                        ins = af(s_ab[1][:, n, :], s_ab[1][:, n, :], ACT.Exp, bias=cols[:, r + 1, n:n + 1],
                                 scale=ATT_SCALE, accum_out=cols[:, r + 3, n:n + 1])
                ins.then_inc(p_ready, 1)

            def turned(hd):
                act.wait_ge(pt_done, hd + 1)
                if hd < GH:
                    af(pt_ab[1][:, 1:TT, :], MS[:, P:S].rearrange("p (n c) -> p n c", c=P), ACT.Copy)
                af(pt_ab[buf(hd)][:].rearrange("p n c -> p (n c)"), turn_bank(hd)[:], ACT.Copy).then_inc(pt_ready, 1)

            for g in range(3):
                for t in range(6):
                    p, grp = PAN[f"a{g}"] + t, GRP[f"a{g}"] + t
                    conv(p + 1)
                    for hd in HEAD_STEPS.get(p - 1, (None, ()))[1]:
                        exps(hd)
                    act.wait_ge(panel_done, p + 1)
                    back = HEAD_STEPS.get(p, (None, ()))[0]
                    if back is not None:
                        turned(back)
                    if t < 4:
                        act.wait_ge(qk_ready, 4 * g + t)
                        for c in range(2):
                            bank = pair(grp)[c]
                            af(rot[0:64, c, :], bank[64:128, :], ACT.Copy)
                            af(rot[64:128, c, :], bank[0:64, :], ACT.Copy).then_inc(rot_ready, 1)
                    elif t == 5:
                        for c in range(TT):
                            ins = af(av[:, g, c, :], PB[c][:], ACT.Copy)
                            if c % 2:
                                ins.then_inc(group_free, 1)
                        act.wait_ge(group_free, grp + 3)
                        act.sem_inc(v_ready, 1)
            last = HEAD_STEPS[PAN["a2"] + 5][1]
            for (back, scored), hd in zip(HEAD_TAIL, last):
                exps(hd)
            for back, scored in HEAD_TAIL:
                turned(back)
                for hd in scored:
                    exps(hd)
            act.wait_ge(rows_done, 1)
            for g in range(3):
                src = PB[g][0:GH, :]
                dst = lrow[:, g, :] if g == 0 else by_four(lrow[:, g, :])
                if g:
                    src = src.rearrange("p (r a) -> p r a", r=TT)
                ins = af(dst, src, ACT.Ln)
            ins.then_inc(row_log, 1)
            act.wait_ge(row_diff, 1)
            af(lrow[:], erow[:], ACT.Exp).then_inc(row_exp, 1)
            act.wait_ge(row_sum, 1)
            af(rstd[0:GH, :], rstd[0:GH, :], ACT.Ln).then_inc(row_logsum, 1)
            act.wait_ge(row_fac, 1)
            af(mrow[:], mrow[:], ACT.Exp).then_inc(fac_ready, 1)

            residual(PAN["attn_out"], 2, 3)
            norm_scale(3)
            norm_upper(3)
            ffn(1, 4)
            norm_scale(4)
            for j in range(KC):
                norm_sums_part(5, j)
            norm_scale(5)
            norm_upper(4)

            with act.Fori(0, 2) as i:
                for s in range(2):
                    p, g = PAN["rx"] + s, GRP["rx"] + s
                    conv(p + 1, i)
                    act.wait_ge(x4_ready, i * 4 + 2 * s)
                    act.wait_ge(panel_done, i * 2 + (p + 1))
                    af(xpad[:, 0, 3:3 + S], pair(g)[0][:], ACT.Copy).then_inc(xp_ready, 1)
                    af(xpad[:, 1, 3:3 + S], pair(g)[1][:], ACT.Copy).then_inc(xp_ready, 1)
                    act.wait_ge(xp_ready, i * 4 + (2 * s + 2))
                    act.sem_inc(group_free, 1)
            for s, (dst, bias) in enumerate(((rr, V_BR), (ii, V_BI))):
                conv(PAN["rg"] + s + 1)
                for q in range(4):
                    g = GRP["rg"] + 4 * s + q
                    act.wait_ge(gate_done, 4 * s + q + 1)
                    for c in range(2):
                        ins = af(dst[:, 2 * q + c, :], pair(g)[c][:], ACT.Sigmoid, bias=vec(bias, 2 * q + c))
                    ins.then_inc(group_free, 1)
            with act.Fori(0, KC // 2) as i:
                for s in range(2):
                    p, g = PAN["cx"] + s, GRP["cx"] + s
                    conv(p + 1, i)
                    act.wait_ge(z8_ready, i * 2 + (s + 1))
                    af(rr[:, i * 2 + s, :], sq[:, s, :], ACT.Exp, scale=-1.0).then_inc(decay_ready, 1)
                    af(sq[:, s, :], sq[:, s, :], ACT.Tanh).then_inc(decay_ready, 1)
                    act.wait_ge(group_free, i * 2 + (g + 2))
                    act.wait_ge(panel_done, i * 2 + (p + 1))
                    af(rstd[:], pair(g)[1][:], ACT.Copy).then_inc(xs_ready, 1)
            with act.Fori(0, KC // 2) as i:
                for s in range(2):
                    p, g = PAN["bg"] + s, GRP["bg"] + s
                    conv(p + 1, i)
                    act.wait_ge(m2_ready, i * 2 + (s + 1))
                    af(sq[:, s, :], x4[:, i * 2 + s, :], ACT.Sqrt).then_inc(mult_ready, 1)
                    act.wait_ge(group_free, i * 2 + (g + 2))
                    act.wait_ge(panel_done, i * 2 + (p + 1))
                    af(rstd[:], pair(g)[1][:], ACT.Sigmoid).then_inc(sgc_ready, 1)
            with act.Fori(0, KC // 2) as i:
                for s in range(2):
                    p, g = PAN["yg"] + s, GRP["yg"] + s
                    conv(p + 1, i)
                    act.wait_ge(group_free, i * 2 + (g + 2))
                    act.wait_ge(panel_done, i * 2 + (p + 1))
                    af(gel[:], pair(g)[0][:], ACT.Gelu_apprx_tanh).then_inc(gel_ready, 1)
                    af(rstd[:], pair(g)[1][:], ACT.Sigmoid).then_inc(gel_ready, 1)
            residual(PAN["rg_out"], 1, 6)
            norm_scale(6)
            norm_upper(5)
            ffn(2, 7)
            norm_scale(7)
            for q in range(4):
                act.wait_ge(side_done, q + 1)
                for c in range(2):
                    ins = af(pp[:, 2 * q + c, :], pair(GRP["ple"] + q)[c][:], ACT.Copy)
                ins.then_inc(group_free, 1)
            norm_upper(6)
            conv(PAN["gate"])
            for q in range(4):
                p, g = PAN["gate"] + q, GRP["gate"] + q
                if p + 1 < PAN["end"]:
                    conv(p + 1)
                act.wait_ge(panel_done, p + 1)
                for c in range(2):
                    act.wait_ge(h_ready, KC * 7 + 2 * q + c - 1)
                    af(un[:, c, :], pair(g)[c][:], ACT.Sigmoid).then_inc(sgate_ready, 1)
                for c in range(2):
                    norm_sums_part(8, 2 * q + c)
            norm_scale(8)

        @block.vector
        def _(dve):
            ch = Chain(dve, dve_chain)
            tt, ts, stt = nc.vector.tensor_tensor, nc.vector.tensor_scalar, nc.vector.scalar_tensor_tensor
            cp = nc.vector.tensor_copy

            def norm_sum(n, j, i=None, step=0):
                dve.wait_ge(sq_ready, KC * n + j + 1 if i is None else i * step + (KC * n + j + 1))
                if i is not None or j:
                    dve.wait_ge(sum_added, KC * n + j if i is None else i * step + (KC * n + j))
                tt(ssq[:], ssq[:], sq[:, j % 2, :], ALU.add).then_inc(sum_added, 1)

            def norm_split(n, m):
                dve.wait_ge(rstd_ready, n + 1)

                def scaled(j):
                    if j >= 2 :
                        dve.wait_ge(u_ready, KC * m + j - 1)
                    stt(un[:, j % 2, :], h[:, j, :], vec(V_NORM + KC * n, j), rstd[:], ALU.mult, ALU.mult)\
                        .then_inc(un_ready, 1)

                scaled(0)
                for j in range(KC):
                    if j + 1 < KC:
                        scaled(j + 1)
                    if n == 7 and j == 4:
                        dve.wait_ge(panel_done, PAN["gate"])
                    dve.wait_ge(uhi_ready, KC * m + j + 1)
                    tt(u_lo[:, j, :], un[:, j % 2, :], u_hi[:, j, :].bitcast(F32), ALU.subtract).then_inc(u_ready, 1)

            def norm_in_place(n):
                dve.wait_ge(rstd_ready, n + 1)
                for j in range(KC):
                    stt(h[:, j, :], h[:, j, :], vec(V_NORM + KC * n, j), rstd[:], ALU.mult, ALU.mult)\
                        .then_inc(h_ready, 1)

            def residual(p0, g0, per, r, n):
                ch.link(nc.vector.memset(ssq[:], 0.0))
                with dve.Fori(0, 2) as i:
                    for s in range(2):
                        dve.wait_ge(panel_done, i * (2 * per) + (p0 + per * (s + 1)))
                        for c in range(2):
                            hj = h[:, i * 4 + (2 * s + c), :]
                            tt(hj, hj, pair(g0 + s)[c][:], ALU.add).then_inc(h_ready, 1)
                        dve.wait_ge(h_ready, i * 4 + (KC * r + 2 * s + 2))
                        dve.sem_inc(group_free, 1)
                        for c in range(2):
                            norm_sum(n, 2 * s + c, i, 4)

            def ffn(f, r, n):
                with dve.Fori(0, FT // 2) as i:
                    ch.enter(i, 2)
                    for s in range(2):
                        g = GRP[f"up{f}"] + s
                        dve.wait_ge(sg_ready, i * 2 + (FT * f + s + 1))
                        tt(un[:, s, :], sq[:, s, :], pair(g)[1][:], ALU.mult).then_inc(group_free, 1)
                        dve.wait_ge(group_free, i * 2 + (g + 3))
                        ch.link(cp(act_hi[:, i * 2 + s, :], un[:, s, :]))
                        tt(act_lo[:, i * 2 + s, :], un[:, s, :], act_hi[:, i * 2 + s, :].bitcast(F32),
                           ALU.subtract).then_inc(act_ready, 1)
                ch.leave(FT // 2)
                if f == 2:
                    dve.wait_ge(p_loaded, 16)
                    ch.link(cp(p_hi[:], pf[:]))
                    tt(p_lo[:], pf[:], p_hi[:].bitcast(F32), ALU.subtract).then_inc(pf_ready, 1)
                residual(PAN[f"down{f}"], GRP[f"down{f}"], 3, r, n)

            dve.wait_ge(const_loaded, 80)
            cp(lmask[:], lmask_f[:]).then_inc(masks_ready, 1)
            row = [vecs[:, V_LB + KC * k:V_LB + KC * (k + 1)] for k in range(3)]
            lam = vecs[:, V_LAM:V_LAM + KC]
            ch.link(tt(lb[:, 3, :], row[0], row[1], ALU.max))
            ch.link(tt(lb[:, 3, :], lb[:, 3, :], row[2], ALU.max))
            for k in range(3):
                ins = tt(lb[:, k, :], row[k], lb[:, 3, :], ALU.subtract)
            ins.then_inc(lb_in, 1)
            ch.link(ts(spl[:, 2, :], lam, -1.0, None, ALU.mult))
            ch.link(ts(spl[:, 0, :], spl[:, 2, :], 0.0, None, ALU.max))
            tt(spl[:, 1, :], lam, spl[:, 2, :], ALU.min).then_inc(lb_in, 1)
            dve.wait_ge(x_loaded, 16)
            ch.link(nc.vector.memset(ssq[:], 0.0))
            for j in range(KC):
                norm_sum(0, j)
            dve.wait_ge(lb_exp, 1)
            ch.link(tt(lb[:, 3, :], lb[:, 0, :], lb[:, 1, :], ALU.add))
            ch.link(tt(lb[:, 3, :], lb[:, 3, :], lb[:, 2, :], ALU.add))
            ch.link(nc.vector.reciprocal(lb[:, 4, :], lb[:, 3, :]))
            ch.link(tt(lb[:, 0, :], lb[:, 0, :], lb[:, 4, :], ALU.mult))
            ch.link(ts(lb[:, 1, :], lb[:, 0, :], -1.0, 1.0, ALU.mult, ALU.add))
            dve.wait_ge(lam_exp, 1)
            ch.link(ts(spl[:, 2, :], spl[:, 1, :], 2.0, None, ALU.add))
            ch.link(nc.vector.reciprocal(spl[:, 3, :], spl[:, 2, :]))
            ch.link(tt(spl[:, 1, :], spl[:, 1, :], spl[:, 3, :], ALU.mult))
            ch.link(tt(spl[:, 2, :], spl[:, 1, :], spl[:, 1, :], ALU.mult))
            ch.link(ts(spl[:, 3, :], spl[:, 2, :], 1.0 / 19, 1.0 / 17, ALU.mult, ALU.add))
            for k in (15, 13, 11, 9, 7, 5, 3, 1):
                ch.link(tt(spl[:, 3, :], spl[:, 3, :], spl[:, 2, :], ALU.mult))
                ch.link(ts(spl[:, 3, :], spl[:, 3, :], 1.0 / k, None, ALU.add))
            ch.link(tt(spl[:, 3, :], spl[:, 3, :], spl[:, 1, :], ALU.mult))
            ch.link(stt(spl[:, 0, :], spl[:, 3, :], 2.0, spl[:, 0, :], ALU.mult, ALU.add))
            ch.link(ts(spl[:, 0, :], spl[:, 0, :], RG_C, None, ALU.mult))
            norm_split(0, 0)

            with dve.Fori(0, 2) as i:
                ch.enter(i, 4)
                for s in range(2):
                    for c in range(2):
                        k = 2 * s + c
                        dve.wait_ge(fsig_ready, i * 4 + (k + 1))
                        ch.link(ts(cum[:, i * 4 + k, :], key[:, i * 4 + k, :], lb[:, 1, bass.ds(i * 4 + k, 1)],
                                   lb[:, 0, bass.ds(i * 4 + k, 1)], ALU.mult, ALU.add))
                        ins = ts(key[:, i * 4 + k, :], cum[:, i * 4 + k, :], -1.0, 1.0, ALU.mult, ALU.add)
                    ins.then_inc(group_free, 1)
            ch.leave(2)
            dve.wait_ge(consts_ready, 3)
            with dve.Fori(0, HG) as i:
                dve.wait_ge(logf_ready, i + 1)
                for c in range(TT):
                    b = cum[:, i, c * P:(c + 1) * P]
                    ins = nc.vector.tensor_tensor_scan(b, one_s[:], b, 0.0, ALU.mult, ALU.add)
                ins.then_inc(cum_ready, 1)
            def decayed(hd, levels):
                for l in levels:
                    m = LEVELS[l]
                    dve.wait_ge(exp_ready, len(LEVELS) * hd + l + 1)
                    z, q, k = (blocks(t, m) for t in (level_tile(hd, l), query[:, hd, :], key[:, hd, :]))
                    tt(z[:, :, m:2 * m], z[:, :, m:2 * m], q[:, :, m:2 * m], ALU.mult)
                    tt(z[:, :, 0:m], z[:, :, 0:m], k[:, :, 0:m], ALU.mult).then_inc(z_ready, 1)

            def take_level(hd, l):
                n = 8 * hd + l
                dve.wait_ge(lev_done, n + 1)
                bank = PB[5 + l % 2][:].rearrange("p (n c) -> p n c", c=P)
                s3 = scores[hd % 2][:].rearrange("p (n c) -> p n c", c=P)
                if l == 0:
                    ins = tt(s3, bank, amask[:, 3:4, :].to_broadcast([P, TT, P]), ALU.mult)
                else:
                    dve.wait_ge(lev_free, n)
                    ins = nc.vector.copy_predicated(s3, lmask[:, l:l + 1, :].to_broadcast([P, TT, P]), bank)
                ins.then_inc(lev_free, 1)

            def chunk_states(hd):
                dve.wait_ge(kv_done, hd + 1)
                ch.link(cp(state[:, 0, :], HB[:, 0:P]))
                for c in range(1, 3):
                    ins = stt(state[:, c, :], state[:, c - 1, :], e_last[:, c:c + 1], HB[:, c * P:(c + 1) * P],
                              ALU.mult, ALU.add)
                    if c == 1:
                        ch.link(ins)
                ins.then_inc(states_ready, 1)

            def head_out(hd):
                dve.wait_ge(orstd_ready, hd + 1)
                stt(un[:, 0, :], HB[:], vec(V_HG, 0), rstd[:], ALU.mult, ALU.mult).then_inc(on_ready, 1)
                dve.wait_ge(on_ready, hd + 1)
                ch.link(tt(un[:, 1, :], un[:, 0, :], gate[:, hd % 4, :], ALU.mult))
                ch.link(cp(o_hi[:, hd, :], un[:, 1, :]))
                tt(o_lo[:, hd, :], un[:, 1, :], o_hi[:, hd, :].bitcast(F32), ALU.subtract).then_inc(oh_ready, 1)

            dve.wait_ge(masks_ready, 1)
            decayed(0, range(RING))
            for hd in range(HG):
                if hd:
                    dve.wait_ge(ends_ready, hd)
                cp(b_last[:], cum[:, hd, P - 1:S:P]).then_inc(blast_ready, 1)
                take_level(hd, 0)
                decayed(hd, (4,))
                take_level(hd, 1)
                if hd:
                    chunk_states(hd - 1)
                decayed(hd, (5,))
                take_level(hd, 2)
                decayed(hd, (6,))
                for l in range(3, 8):
                    take_level(hd, l)
                if hd:
                    head_out(hd - 1)
                if hd + 1 < HG:
                    decayed(hd + 1, range(RING))
            chunk_states(HG - 1)
            head_out(HG - 1)
            residual(PAN["hgrn_out"], GRP["hgrn_out"], 1, 0, 1)
            norm_split(1, 1)
            ffn(0, 1, 2)
            norm_split(2, 2)

            def rotate(g, t):
                grp = GRP[f"a{g}"] + t
                for c in range(2):
                    j = (t // 2) * AH + GH * g + 2 * (t % 2) + c
                    dve.wait_ge(rot_ready, 2 * (4 * g + t) + c + 1)
                    ch.step(tt(un[:, c, :], pair(grp)[c][:], cs[:, 0, :], ALU.mult))
                    ch.link(tt(rot[:, c, :], rot[:, c, :], cs[:, 1, :], ALU.mult))
                    ins = tt(aqk[:, j, :], un[:, c, :], rot[:, c, :], ALU.add)
                ins.then_inc(qk_ready, 1)
                dve.wait_ge(qk_ready, 4 * g + t + 1)
                dve.sem_inc(group_free, 1)

            def spread(k, n=TT):
                return amask[:, k:k + 1, :].to_broadcast([P, n, P])

            def maxima(hd):
                r = 4 * (hd % 2)
                s_h = s_ab[buf(hd)]
                dve.wait_ge(s_done, hd + 1)
                bank = score_bank(hd)[:].rearrange("p (n c) -> p n c", c=P)
                ch.step(tt(s_h[:], bank, spread(0 if hd < 2 * GH else 2), ALU.add))
                if hd < GH:
                    prev = PB[6][:, P:S].rearrange("p (n c) -> p n c", c=P)
                    ch.step(tt(s_ab[1][:, 1:TT, :], prev, spread(1, TT - 1), ALU.add))
                ch.settle()
                ch.step(nc.vector.tensor_reduce(cols[:, r, :], s_h[:], AX_X, ALU.max))
                if hd < GH:
                    ch.link(nc.vector.tensor_reduce(cols[:, r + 3, 1:TT], s_ab[1][:, 1:TT, :], AX_X, ALU.max))
                    ch.step(tt(cols[:, r, 1:TT], cols[:, r, 1:TT], cols[:, r + 3, 1:TT], ALU.max))
                ch.settle()
                cp(mst[:, hd, :], cols[:, r, :])
                ts(cols[:, r + 1, :], cols[:, r, :], -ATT_SCALE, None, ALU.mult).then_inc(max_ready, 1)

            def sums(hd):
                r = 4 * (hd % 2)
                dve.wait_ge(p_ready, hd + 1)
                ch.link(cp(lst[:, hd, :], cols[:, r + 2, :]))
                if hd < GH:
                    ch.link(tt(lst[:, hd, 1:TT], cols[:, r + 2, 1:TT], cols[:, r + 3, 1:TT], ALU.add))

            def head_out(hd):
                dve.wait_ge(pv_done, hd + 1)
                if hd < GH:
                    ins = cp(o_raw[:, hd, :], turn_bank(hd)[:])
                else:
                    ins = cp(by_four(o_raw[:, hd, :]), turn_bank(hd)[:].rearrange("p (r a) -> p r a", r=TT))
                ins.then_inc(oraw_ready, 1)

            def heads_step(back, scored):
                if back is not None:
                    sums(back)
                for hd in scored:
                    maxima(hd)
                if back is not None:
                    head_out(back)

            dve.wait_ge(cs_loaded, 16)
            for g in range(3):
                for t in range(6):
                    if t < 4:
                        rotate(g, t)
                    heads_step(*HEAD_STEPS.get(PAN[f"a{g}"] + t, (None, ())))
            for back, scored in HEAD_TAIL:
                heads_step(back, scored)
            dve.wait_ge(rows_done, 1)
            for g in range(3):
                if g == 0:
                    ch.step(ts(mrow[:, g, :], PB[5][0:GH, :], ATT_SCALE, None, ALU.mult))
                else:
                    ch.step(ts(by_four(mrow[:, g, :]), PB[5 + g][0:GH, :].rearrange("p (r a) -> p r a", r=TT),
                               ATT_SCALE, None, ALU.mult))
            ch.settle()
            dve.wait_ge(row_log, 1)
            ch.link(tt(erow[:], mrow[:], lrow[:], ALU.add))
            ch.link(tt(trow[:], erow[:, 0, :], erow[:, 1, :], ALU.max))
            ch.link(tt(trow[:], trow[:], erow[:, 2, :], ALU.max))
            for g in range(3):
                ins = tt(erow[:, g, :], erow[:, g, :], trow[:], ALU.subtract)
            ins.then_inc(row_diff, 1)
            dve.wait_ge(row_exp, 1)
            ch.link(tt(rstd[0:GH, :], lrow[:, 0, :], lrow[:, 1, :], ALU.add))
            tt(rstd[0:GH, :], rstd[0:GH, :], lrow[:, 2, :], ALU.add).then_inc(row_sum, 1)
            dve.wait_ge(row_logsum, 1)
            ch.link(tt(trow[:], trow[:], rstd[0:GH, :], ALU.add))
            for g in range(3):
                ins = tt(mrow[:, g, :], mrow[:, g, :], trow[:], ALU.subtract)
            ins.then_inc(row_fac, 1)
            with dve.Fori(0, 3) as i:
                ch.enter(i, 2 * GH)
                for k in range(GH):
                    dve.wait_ge(fac_done, i * GH + (k + 1))
                    ch.link(tt(un[:, k % 2, :], o_raw[:, i * GH + k, :], FAC[k][:], ALU.mult))
                    ch.link(cp(ao_hi[:, i * GH + k, :], un[:, k % 2, :]))
                    tt(ao_lo[:, i * GH + k, :], un[:, k % 2, :], ao_hi[:, i * GH + k, :].bitcast(F32),
                       ALU.subtract).then_inc(ao_ready, 1)
            ch.leave(3)
            residual(PAN["attn_out"], GRP["attn_out"], 2, 2, 3)
            norm_split(3, 3)
            ffn(1, 3, 4)
            norm_in_place(4)
            ch.link(nc.vector.memset(ssq[:], 0.0))
            for j in range(KC):
                norm_sum(5, j)
            ch.link(nc.vector.memset(xpad[:, :, 0:3], 0.0))
            norm_split(5, 4)

            with dve.Fori(0, 2) as i:
                ch.enter(i, 5 * 4)
                for s in range(2):
                    for c in range(2):
                        k = 2 * s + c
                        x = x4[:, i * 4 + k, :]
                        dve.wait_ge(xp_ready, i * 4 + (k + 1))
                        ch.link(ts(x, xpad[:, c, 3:3 + S], vec_i(V_C4W + 3 * KC, i, 4, k), vec_i(V_C4B, i, 4, k),
                                   ALU.mult, ALU.add))
                        for tap in range(3):
                            ch.link(stt(x, xpad[:, c, tap:tap + S], vec_i(V_C4W + tap * KC, i, 4, k), x,
                                        ALU.mult, ALU.add))
                        ch.link(cp(x4_hi[:, i * 4 + k, :], x))
                        tt(x4_lo[:, i * 4 + k, :], x, x4_hi[:, i * 4 + k, :].bitcast(F32), ALU.subtract)\
                            .then_inc(x4_ready, 1)
            ch.leave(2)
            dve.wait_ge(group_free, GRP["cx"] + 2)
            with dve.Fori(0, KC // 2) as i:
                ch.enter(i, 8)
                for s in range(2):
                    j = i * 2 + s
                    g = GRP["cx"] + s
                    ts(sq[:, s, :], rr[:, j, :], spl[:, 0, bass.ds(j, 1)], None, ALU.mult).then_inc(z8_ready, 1)
                    ch.link(tt(ii[:, j, :], ii[:, j, :], x4[:, j, :], ALU.mult))
                    dve.wait_ge(decay_ready, i * 4 + (2 * s + 2))
                    ch.link(tt(un[:, 0, :], rr[:, j, :], rr[:, j, :], ALU.mult))
                    stt(x4[:, j, :], un[:, 0, :], 1.0, sq[:, s, :], ALU.add, ALU.mult).then_inc(m2_ready, 1)
                    dve.wait_ge(xs_ready, i * 2 + (s + 1))
                    tt(xpad[:, s, 3:3 + S], pair(g)[0][:], rstd[:], ALU.mult).then_inc(group_free, 1)
                    dve.wait_ge(group_free, i * 2 + (g + 3))
                    ch.link(ts(cc[:, j, :], xpad[:, s, 3:3 + S], vec_i(V_C3W + 2 * KC, i, 2, s), None, ALU.mult))
                    for tap in range(2):
                        ins = stt(cc[:, j, :], xpad[:, s, 1 + tap:1 + tap + S], vec_i(V_C3W + tap * KC, i, 2, s),
                                  cc[:, j, :], ALU.mult, ALU.add)
                        if tap == 0:
                            ch.link(ins)
            ch.leave(KC // 2)
            ch.link(nc.vector.memset(ssq[:], 0.0))
            with dve.Fori(0, KC // 2) as i:
                ch.enter(i, 4)
                for s in range(2):
                    j = i * 2 + s
                    g = GRP["bg"] + s
                    dve.wait_ge(mult_ready, i * 2 + (s + 1))
                    ch.link(tt(ii[:, j, :], ii[:, j, :], sq[:, s, :], ALU.mult))
                    nc.vector.tensor_tensor_scan(rr[:, j, :], rr[:, j, :], ii[:, j, :], 0.0, ALU.mult, ALU.add)
                    dve.wait_ge(sgc_ready, i * 2 + (s + 1))
                    ch.link(tt(un[:, 0, :], pair(g)[0][:], cc[:, j, :], ALU.mult))
                    tt(cc[:, j, :], un[:, 0, :], rstd[:], ALU.mult).then_inc(group_free, 1)
            ch.leave(KC // 2)
            dve.wait_ge(group_free, GRP["yg"] + 2)
            with dve.Fori(0, KC // 2) as i:
                ch.enter(i, 6)
                for s in range(2):
                    j = i * 2 + s
                    g = GRP["yg"] + s
                    dve.wait_ge(gel_ready, i * 4 + (2 * s + 2))
                    tt(un[:, 0, :], gel[:], rstd[:], ALU.mult).then_inc(group_free, 1)
                    dve.wait_ge(group_free, i * 2 + (g + 3))
                    ch.link(tt(un[:, 0, :], un[:, 0, :], rr[:, j, :], ALU.mult))
                    ch.link(tt(un[:, 1, :], un[:, 0, :], cc[:, j, :], ALU.add))
                    ch.link(cp(m_hi[:, j, :], un[:, 1, :]))
                    tt(m_lo[:, j, :], un[:, 1, :], m_hi[:, j, :].bitcast(F32), ALU.subtract).then_inc(mg_ready, 1)
            ch.leave(KC // 2)
            residual(PAN["rg_out"], GRP["rg_out"], 1, 5, 6)
            norm_split(6, 5)
            ffn(2, 6, 7)
            norm_split(7, 6)
            ch.link(nc.vector.memset(ssq[:], 0.0))
            for q in range(4):
                for c in range(2):
                    j = 2 * q + c
                    dve.wait_ge(sgate_ready, j + 1)
                    ch.link(tt(un[:, c, :], un[:, c, :], pp[:, j, :], ALU.mult))
                    tt(h[:, j, :], h[:, j, :], un[:, c, :], ALU.add).then_inc(h_ready, 1)
                dve.sem_inc(group_free, 1)
                for c in range(2):
                    norm_sum(8, 2 * q + c)
            norm_in_place(8)

        @block.tensor
        def _(pe):
            def mm(out, lhsT, rhs, start=True, stop=True):
                return nc.tensor.matmul(out, lhsT, rhs, start=start, stop=stop, skip_group_check=True)

            def at(c, i, step):
                return c if i is None else i * step + c

            def panel(p, g, x_hi, x_lo, i=None, pstep=2, gstep=2, ks=tuple(range(KC)), first=True, last=True,
                      inputs=None):
                s, nk = p % 2, len(ks)
                w = [t[:, s, :].rearrange("p (k c) -> p k c", c=HALF) for t in (w_hi, w_lo)]
                pe.wait_ge(hi_ready, at(p + 1, i, pstep))
                if first:
                    pe.wait_ge(group_free, at(g + 1, i, gstep))
                for n, k in enumerate(ks):
                    if inputs is not None:
                        pe.wait_ge(inputs[0], inputs[1] + k + 1)
                    for c in range(2):
                        mm(pair(g)[c][:], w[0][:, n, c * P:(c + 1) * P], x_hi[:, k, :], first and n == 0, False)
                        mm(pair(g)[c][:], w[0][:, n, c * P:(c + 1) * P], x_lo[:, k, :], False, False)
                pe.wait_ge(lo_ready, at(p + 1, i, pstep))
                for c in range(2):
                    for n, k in enumerate(ks):
                        ins = mm(pair(g)[c][:], w[1][:, n, c * P:(c + 1) * P], x_hi[:, k, :], False,
                                 last and n == nk - 1)
                ins.then_inc(panel_done, 1)

            def project(name, n, x_hi, x_lo, inputs):
                with pe.Fori(0, n // 2) as i:
                    for s in range(2):
                        panel(PAN[name] + s, GRP[name] + s, x_hi, x_lo, i, inputs=inputs if s == 0 else None)

            def residual(name, x_hi, x_lo, cuts, inputs):
                per = len(cuts) - 1
                with pe.Fori(0, 2) as i:
                    for s in range(2):
                        for t in range(per):
                            panel(PAN[name] + per * s + t, GRP[name] + s, x_hi, x_lo, i, 2 * per, 2,
                                  tuple(range(cuts[t], cuts[t + 1])), t == 0, t == per - 1,
                                  inputs if s == 0 else None)

            def by_tokens(name, i, tile_of):
                for s in range(2):
                    p = PAN[name] + s
                    sl = p % 2
                    w = [t[:, sl, :].rearrange("p (k c) -> p k c", c=S) for t in (w_hi, w_lo)]
                    pe.wait_ge(hi_ready, at(p + 1, i, 2))
                    pe.wait_ge(lo_ready, at(p + 1, i, 2))
                    if s == 0:
                        pe.wait_ge(group_free, at(GRP[name] + 2, i, 2))
                    for t in range(TT):
                        for n in range(4):
                            k = 4 * s + n
                            for a, (x, v) in enumerate(((u_hi, w[0]), (u_lo, w[0]), (u_hi, w[1]))):
                                ins = mm(PB[t][:], tile_of(x[:, k, :], t), v[:, n, :], k == 0 and a == 0,
                                         k == KC - 1 and a == 2)
                    ins.then_inc(panel_done, 1)

            def norm(n):
                pe.wait_ge(sum_added, KC * (n + 1))
                mm(MS[:], ones[:], ssq[:]).then_inc(ms_ready, 1)

            def near(t, n):
                return t[:, n * P:(n + 1) * P]

            def far(t, n):
                return t[:, n::TT]

            def ffn(f, m):
                project(f"up{f}", FT, u_hi, u_lo, (u_ready, KC * m))
                residual(f"down{f}", act_hi, act_lo, (0, 8, 16, FT), (act_ready, FT * f))

            pe.sem_inc(group_free, 2)
            pe.wait_ge(consts_ready, 3)
            norm(0)
            project("f", 4, u_hi, u_lo, (u_ready, 0))
            project("q", 4, u_hi, u_lo, None)
            with pe.Fori(0, 2) as i:
                by_tokens("i", i, near)

            def level(hd, l):
                n = 8 * hd + l
                if l < len(LEVELS):
                    pe.wait_ge(z_ready, len(LEVELS) * hd + l + 1)
                if n >= 2:
                    pe.wait_ge(lev_free, n - 1)
                a, b = (level_tile(hd, l),) * 2 if l < len(LEVELS) else (key[:, hd, :], query[:, hd, :])
                for c in range(TT):
                    ins = mm(near(PB[5 + l % 2], c), near(a, c), near(b, c))
                ins.then_inc(lev_done, 1)

            def keys_by_token(hd):
                pe.wait_ge(dec_ready, hd + 1)
                if hd:
                    pe.wait_ge(on_ready, hd)
                for c in range(TT - 1):
                    ins = nc.tensor.transpose(near(HB, c), near(k_end, c), ident[:])
                ins.then_inc(ket_done, 1)

            def chunk_states(hd):
                pe.wait_ge(ket_ready, hd + 1)
                for c in range(TT - 1):
                    ins = mm(near(HB, c), k_endt[:, c, :], near(val[:, c, :], hd))
                ins.then_inc(kv_done, 1)

            def outputs(hd):
                pe.wait_ge(states_ready, hd + 1)
                pe.wait_ge(lev_free, 8 * hd + 8)
                for c in range(TT):
                    ins = mm(near(HB, c), near(val[:, c, :], hd), near(scores[hd % 2], c), True, c == 0)
                    if c:
                        ins = mm(near(HB, c), state[:, c - 1, :], near(q_dec, c), False, True)
                ins.then_inc(o_done, 1)

            def mean_squares(hd):
                pe.wait_ge(osq_ready, hd + 1)
                mm(MS[:], ones[:], sq[:, 0, :]).then_inc(oms_done, 1)

            AFTER_LEVEL = (1, 3, 4)

            def gate_part(q, half):
                p, g = PAN["g"] + q, GRP["g"] + q
                w = [t[:, p % 2, :].rearrange("p (k c) -> p k c", c=HALF) for t in (w_hi, w_lo)]
                pe.wait_ge(lo_ready, p + 1)
                if half == 0:
                    pe.wait_ge(group_free, g + 1)
                for k in range(4 * half, 4 * half + 4):
                    for c in range(2):
                        for a, (v, x) in enumerate(((w[0], u_hi), (w[0], u_lo), (w[1], u_hi))):
                            ins = mm(pair(g)[c][:], v[:, k, c * P:(c + 1) * P], x[:, k, :], k == 0 and a == 0,
                                     k == KC - 1 and a == 2)
                if half:
                    ins.then_inc(panel_done, 1)

            panel(PAN["g"], GRP["g"], u_hi, u_lo)
            pe.wait_ge(const_loaded, 80)
            for hd in range(HG):
                for l in range(len(LEVELS) + 1):
                    level(hd, l)
                    if hd and l in AFTER_LEVEL:
                        (chunk_states, outputs, mean_squares)[AFTER_LEVEL.index(l)](hd - 1)
                if hd < 6:
                    gate_part(1 + hd // 2, hd % 2)
                keys_by_token(hd)
            chunk_states(HG - 1)
            outputs(HG - 1)
            mean_squares(HG - 1)

            residual("hgrn_out", o_hi, o_lo, (0, KC), (oh_ready, 0))
            norm(1)
            ffn(0, 1)
            norm(2)
            def value_panels(g):
                tile_of = far if g else near
                for s in range(2):
                    p = PAN[f"a{g}"] + 4 + s
                    w = [t[:, p % 2, :].rearrange("p (k c) -> p k c", c=S) for t in (w_hi, w_lo)]
                    pe.wait_ge(hi_ready, p + 1)
                    pe.wait_ge(lo_ready, p + 1)
                    if s == 0:
                        pe.wait_ge(group_free, GRP[f"a{g}"] + 6)
                    for t in range(TT):
                        for n in range(4):
                            k = 4 * s + n
                            for a, (x, v) in enumerate(((u_hi, w[0]), (u_lo, w[0]), (u_hi, w[1]))):
                                ins = mm(PB[t][:], tile_of(x[:, k, :], t), v[:, n, :], k == 0 and a == 0,
                                         k == KC - 1 and a == 2)
                    ins.then_inc(panel_done, 1)
                    if g:
                        heads_step(*HEAD_STEPS.get(p, (None, ())))

            def heads_step(back, scored):
                if back is not None:
                    turn(back)
                for hd in scored:
                    score(hd)
                if back is not None:
                    weigh(back)

            def score(hd):
                tile_of = far if hd >= GH else near
                pe.wait_ge(qk_ready, 4 * (hd // GH + 1))
                if hd:
                    pe.wait_ge(max_ready, hd if hd <= GH else hd - 1)
                q, k = aqk[:, hd, :], aqk[:, AH + hd, :]
                for n in range(TT):
                    ins = mm(near(score_bank(hd), n), tile_of(q, n), tile_of(k, n))
                    if hd < GH and n:
                        ins = mm(near(PB[6], n), near(q, n), near(k, n - 1))
                ins.then_inc(s_done, 1)

            def turn(hd):
                pe.wait_ge(p_ready, hd + 1)
                if hd:
                    pe.wait_ge(oraw_ready, hd if hd <= GH else max(GH, hd - 1))
                for n in range(TT):
                    ins = nc.tensor.transpose(near(turn_bank(hd), n), s_ab[buf(hd)][:, n, :], ident[:])
                    if hd < GH and n:
                        ins = nc.tensor.transpose(near(MS, n), s_ab[1][:, n, :], ident[:])
                ins.then_inc(pt_done, 1)

            def weigh(hd):
                g, c = hd // GH, (hd % GH) * P
                pe.wait_ge(v_ready, g + 1)
                pe.wait_ge(pt_ready, hd + 1)
                for n in range(TT):
                    ins = mm(near(turn_bank(hd), n), av[:, g, n, c:c + P], pt_ab[buf(hd)][:, n, :], True, g > 0 or n == 0)
                    if g == 0 and n:
                        ins = mm(near(turn_bank(hd), n), av[:, g, n - 1, c:c + P], pt_ab[1][:, n, :], False, True)
                ins.then_inc(pv_done, 1)

            project("a0", 4, u_hi, u_lo, (u_ready, KC * 2))
            value_panels(0)
            for g in (1, 2):
                for t in range(4):
                    p = PAN[f"a{g}"] + t
                    panel(p, GRP[f"a{g}"] + t, u_hi, u_lo)
                    heads_step(*HEAD_STEPS.get(p, (None, ())))
                value_panels(g)
            for back, scored in HEAD_TAIL:
                heads_step(back, scored)
            pe.wait_ge(group_free, GRP["attn_out"] + 2)
            pe.wait_ge(oraw_ready, AH)
            for src, bank in ((lst, 0), (mst, 5)):
                for g in range(3):
                    for n in range(TT):
                        ins = nc.tensor.transpose(PB[bank + g][0:GH, n * P:(n + 1) * P],
                                                  src[:, GH * g:GH * (g + 1), n], ident[:])
            ins.then_inc(rows_done, 1)
            pe.wait_ge(fac_ready, 1)
            with pe.Fori(0, 3) as i:
                pe.wait_ge(ao_ready, i * GH)
                for k in range(GH):
                    mm(FAC[k][:], sel[:, k, :], mrow[:, i, :]).then_inc(fac_done, 1)
            residual("attn_out", ao_hi, ao_lo, (0, 6, AH), (ao_ready, 0))
            norm(3)
            ffn(1, 3)
            norm(4)
            norm(5)
            project("rx", 4, u_hi, u_lo, (u_ready, KC * 4))
            for s in range(2):
                p = PAN["rg"] + s
                w = [t[:, p % 2, :].rearrange("p (k c) -> p k c", c=HALF) for t in (w_hi, w_lo)]
                pe.wait_ge(lo_ready, p + 1)
                for q in range(4):
                    g = GRP["rg"] + 4 * s + q
                    pe.wait_ge(group_free, g + 1)
                    pe.wait_ge(x4_ready, 2 * q + 2)
                    for c in range(2):
                        for n in range(2):
                            k = 2 * q + n
                            for a, (v, x) in enumerate(((w[0], x4_hi), (w[0], x4_lo), (w[1], x4_hi))):
                                ins = mm(pair(g)[c][:], v[:, k, c * P:(c + 1) * P], x[:, k, :],
                                         n == 0 and a == 0, n == 1 and a == 2)
                    ins.then_inc(gate_done, 1)
                pe.wait_ge(gate_done, 4 * s + 4)
                pe.sem_inc(panel_done, 1)
            project("cx", KC, u_hi, u_lo, None)
            project("bg", KC, u_hi, u_lo, None)
            project("yg", KC, u_hi, u_lo, None)
            residual("rg_out", m_hi, m_lo, (0, KC), (mg_ready, 0))
            norm(6)
            ffn(2, 5)
            norm(7)
            p = PAN["ple"]
            w = [t[:, p % 2, :].rearrange("p (k c) -> p k c", c=DM) for t in (w_hi, w_lo)]
            pe.wait_ge(lo_ready, p + 1)
            pe.wait_ge(pf_ready, 1)
            for q in range(4):
                g = GRP["ple"] + q
                pe.wait_ge(group_free, g + 1)
                for c in range(2):
                    j = 2 * q + c
                    for k in range(2):
                        for a, (v, x) in enumerate(((w[0], p_hi), (w[0], p_lo), (w[1], p_hi))):
                            ins = mm(pair(g)[c][:], v[:, k, j * P:(j + 1) * P], x[:, k, :],
                                     k == 0 and a == 0, k == 1 and a == 2)
                ins.then_inc(side_done, 1)
            pe.wait_ge(side_done, 4)
            pe.sem_inc(panel_done, 1)
            project("gate", 4, u_hi, u_lo, (u_ready, KC * 6))
            norm(8)


def _tiles(v):
    return np.asarray(v).reshape(-1, P).T


def _panel(w, ks, cols):
    t = np.asarray(w).reshape(-1, P, w.shape[-1])[list(ks)][:, :, cols]
    t = t.transpose(1, 0, 2).reshape(P, -1)
    return np.pad(t, ((0, 0), (0, PANEL - t.shape[1])))


def _panels(i):
    def cols(*starts):
        return np.concatenate([np.arange(c, c + P) for c in starts])

    def whole(w, first, n):
        return [_panel(w, range(KC), cols(first + 256 * k, first + 256 * k + P)) for k in range(n)]

    def paired(w, a, b, n):
        return [_panel(w, range(KC), cols(a + P * k, b + P * k)) for k in range(n)]

    def by_tokens(w, first, n):
        return [_panel(w, range(4 * s, 4 * s + 4), np.arange(first + S * k, first + S * (k + 1)))
                for k in range(n) for s in range(2)]

    def cut(w, cuts):
        return [_panel(w, range(a, b), cols(256 * k, 256 * k + P))
                for k in range(4) for a, b in zip(cuts, cuts[1:])]

    def ffn(w_in, w_down):
        return paired(w_in, 0, DFF, FT), cut(w_down, (0, 8, 16, FT))

    hin, qkv, w2 = i["hgrn_w_in"][0], i["attn_w_qkv"][0], i["w_in_2"][0]
    aw, gw = AH * P, GH * P
    attn_in = [panel for g in range(3)
               for panel in whole(qkv, g * gw, 2) + whole(qkv, aw + g * gw, 2) + by_tokens(qkv, 2 * aw + g * gw, 1)]
    up0, down0 = ffn(i["ffn_w_in"][0], i["ffn_w_down"][0])
    up1, down1 = ffn(i["ffn_w_in"][1], i["ffn_w_down"][1])
    up2, down2 = ffn(i["w_gate_up_2"][0], i["w_down_2"][0])
    out = whole(hin, DM, 4) + whole(hin, 0, 4) + by_tokens(hin, 2 * DM, 2) + whole(hin, 3 * DM, 4)
    out += whole(i["hgrn_w_out"][0], 0, 4) + up0 + down0
    out += attn_in + cut(i["attn_w_out"][0], (0, 6, 12)) + up1 + down1
    out += whole(w2, 0, 4)
    out += [_panel(i[k][0].reshape(DM, 256), range(KC), np.arange(256)) for k in ("w_rg_r_2", "w_rg_i_2")]
    out += paired(w2, 3 * DM, 4 * DM, KC) + paired(w2, 2 * DM, 6 * DM, KC) + paired(w2, DM, 5 * DM, KC)
    out += whole(i["w_out_2"][0], 0, 4) + up2 + down2
    out += [_panel(i["w_ple_2"][0], range(2), np.arange(DM))] + whole(i["w_ple_gate_2"][0], 0, 4)
    assert len(out) == PAN["end"]
    return np.stack(out)


def _vecs(i):
    v = [i["norm_mix"][0], i["norm_ffn"][0], i["norm_mix"][1], i["norm_ffn"][1], i["final_norm"],
         i["g_mix_2"][0], i["g_ffn_2"][0], i["g_ple_2"][0], i["g_final_2"],
         *i["hgrn_lb_logits"], i["hgrn_out_norm"][0], *i["conv4_w_2"][0], i["conv4_b_2"][0],
         i["b_rg_r_2"][0].reshape(-1), i["b_rg_i_2"][0].reshape(-1), i["lru_lambda_2"][0], *i["conv3_w_2"][0]]
    return np.concatenate([_tiles(a) for a in v], axis=1)


def _constants():
    inv = 1.0 / (np.float32(10000.0) ** (np.arange(0, P, 2, dtype=np.float32) / np.float32(P)))
    ang = inv.astype(np.float32)[:, None] * np.arange(S, dtype=np.float32)[None, :]
    cos, sin = np.cos(ang), np.sin(ang)
    cs = np.stack([np.concatenate([cos, cos]), np.concatenate([-sin, sin])], axis=1)
    a, b = np.meshgrid(np.arange(P), np.arange(P), indexing="ij")
    lm = [(a // (2 * m) == b // (2 * m)) & (a % (2 * m) < m) & (b % (2 * m) >= m) for m in LEVELS]
    lmask = np.stack([*lm, a == b], axis=1).astype(np.float32)
    am = [b <= a, b >= a, (b <= a) & (b % 4 == a % 4)]
    amask = np.stack([np.where(m, 0.0, MASKED) for m in am] + [lm[0].astype(np.float64)], axis=1)
    sel = np.zeros((GH, GH, P), np.float32)
    for k in range(GH):
        sel[k, k] = 1.0
    return np.eye(P, dtype=np.float32), cs.astype(np.float32), lmask, amask.astype(np.float32), sel


def kernel(**inputs):
    import concourse.bacc as _bacc
    from concourse.bass_utils import run_bass_kernel_spmd as _run

    i = {k: np.asarray(v) for k, v in inputs.items()}
    ident, cs, lmask, amask, sel = _constants()
    arrays = {
        "wall": _panels(i), "x_t": np.ascontiguousarray(i["x"][0].T), "p_t": np.ascontiguousarray(i["p_2"][0, 0].T),
        "vecs_in": np.ascontiguousarray(_vecs(i)), "ident_in": ident, "cs_in": cs, "lmask_in": lmask,
        "amask_in": amask, "sel_in": sel,
    }
    nc = _bacc.Bacc("TRN2", target_bir_lowering=False, num_devices=1)
    args = [nc.dram_tensor(k, a.shape, mybir.dt.from_np(a.dtype), kind="ExternalInput").ap()
            for k, a in arrays.items()]
    out = nc.dram_tensor("out_t", (DM, S), F32, kind="ExternalOutput").ap()
    build(nc, *args, out)
    r = _run(nc, [arrays], core_ids=[0])
    return np.ascontiguousarray(r.results[0]["out_t"].T)[None]
```

```python
from contextlib import ExitStack

import numpy as np

import concourse.bass as bass
from concourse import mybir

F32 = mybir.dt.float32
F32R = mybir.dt.float32r
U8 = mybir.dt.uint8
ALU = mybir.AluOpType
ACT = mybir.ActivationFunctionType
AX_X = mybir.AxisListType.X

P = 128
S = 512
DM = 1024
KC = DM // P
DFF = 2816
FT = DFF // P
TT = S // P
HG = 8
AH = 12
GH = 4
PLE = 256
PANEL = 2048
HALF = PANEL // KC
LEVELS = (64, 32, 16, 8, 4, 2, 1)
RING = 4
EPS = 1e-6
ATT_SCALE = 128 ** -0.5
MASKED = -1e30
RG_C = 8.0

V_NORM = 0
V_LB = V_NORM + 9 * KC
V_HG = V_LB + 3 * KC
V_C4W = V_HG + 1
V_C4B = V_C4W + 4 * KC
V_BR = V_C4B + KC
V_BI = V_BR + KC
V_LAM = V_BI + KC
V_C3W = V_LAM + KC
V_ALL = V_C3W + 3 * KC


def panel_plan():
    at, first = 0, {}
    for name, n in (("f", 4), ("q", 4), ("i", 4), ("g", 4), ("hgrn_out", 4),
                    ("up0", FT), ("down0", 12),
                    ("a0", 6), ("a1", 4), ("a2", 4), ("v1", 2), ("v2", 2), ("attn_out", 8),
                    ("up1", FT), ("down1", 12),
                    ("rx", 4), ("cx", 8), ("rg", 2), ("bg", 8), ("yg", 8), ("rg_out", 4),
                    ("up2", FT), ("down2", 12), ("gate", 4), ("ple", 1)):
        first[name] = at
        at += n
    first["end"] = at
    return first


def group_plan():
    at, first = 0, {}
    for name, n in (("f", 4), ("q", 4), ("i", 4), ("g", 4), ("hgrn_out", 4),
                    ("up0", FT), ("down0", 4),
                    ("a0", 6), ("a1", 4), ("a2", 4), ("v1", 2), ("v2", 2), ("attn_out", 4),
                    ("up1", FT), ("down1", 4),
                    ("rx", 4), ("cx", 8), ("rg", 8), ("bg", 8), ("yg", 8), ("rg_out", 4),
                    ("up2", FT), ("down2", 4), ("gate", 4), ("ple", 4)):
        first[name] = at
        at += n
    return first


SQ0 = [KC * m for m in range(5)] + [KC * (m + 1) for m in range(5, 8)]
GAIN = [V_NORM + KC * m for m in range(5)] + [V_NORM + KC * (m + 1) for m in range(5, 8)]
TWIN = 4
OUT_SPLIT = 5

PAN = panel_plan()
GRP = group_plan()


class Chain:

    def __init__(self, eng, sem):
        self.eng, self.sem, self.base, self.k, self.i, self.per = eng, sem, 0, 0, None, 0

    def now(self):
        return self.base + self.k if self.i is None else self.per * self.i + (self.base + self.k)

    def step(self, ins):
        ins.then_inc(self.sem, 1)
        self.k += 1

    def settle(self):
        self.eng.wait_ge(self.sem, self.now())

    def link(self, ins):
        self.step(ins)
        self.settle()

    def enter(self, i, per):
        self.base += self.k
        self.k, self.i, self.per = 0, i, per

    def leave(self, n):
        assert self.k == self.per, f"{self.k} steps in the body, {self.per} stated"
        self.base += self.per * n
        self.k, self.i = 0, None


def build(nc, wall, x_t, p_t, vecs_d, ident_d, cs_d, lmask_d, amask_d, sel_d, out_t):
    with ExitStack() as ctx:
        UNIT = 4 * S

        def sb(name, shape, dt=F32):
            return ctx.enter_context(nc.sbuf_tensor(name, shape, dt))

        def sem(name):
            return ctx.enter_context(nc.semaphore(name))

        h = sb("h", [P, KC, S])
        raw = sb("raw", [P, 2, PANEL])
        w_hi = sb("w_hi", [P, 2, PANEL], F32R)
        w_lo = sb("w_lo", [P, 2, PANEL], F32R)
        sq = sb("sq", [P, 2, S])
        un = sb("un", [P, 2, S])
        ssq = sb("ssq", [P, S])
        ssq2 = sb("ssq2", [P, S])
        rstd = sb("rstd", [P, S])
        rstd2 = sb("rstd2", [P, S])
        rcol = sb("rcol", [P, 2 * TT])
        ones = sb("ones", [P, P])
        ident = sb("ident", [P, P])
        vecs = sb("vecs", [P, V_ALL])
        eps = sb("eps", [P, 1])
        lb = sb("lb", [P, 6, KC])
        spl = sb("spl", [P, 6, KC])
        lmask = sb("lmask", [P, len(LEVELS) + 1, P], U8)
        amask = sb("amask", [P, 4, P])
        sel = sb("sel", [GH, GH, P])
        mst = sb("mst", [P, AH, TT])
        lst = sb("lst", [P, AH, TT])
        cols = sb("cols", [P, 8, TT])

        k_endt, state = (t[:, 0:3 * P].rearrange("p (c d) -> p c d", d=P) for t in (ssq, ssq2))
        b_last = sb("b_last", [P, TT])
        e_last = sb("e_last", [P, TT])

        region = {}
        region["u"] = (nc.sbuf_base + 31) // 32 * 32
        sb("region_u", [P, 2 * KC * S])
        region["a"] = (nc.sbuf_base + 31) // 32 * 32
        sb("region_a", [P, 2 * FT * S])

        def place(name, where, unit, shape, dt=F32):
            return nc.alloc_sbuf_tensor_at(name, shape, dt, offset=region[where] + int(unit * UNIT))

        u_hi = place("u_hi", "u", 0, [P, KC, S], F32R)
        u_lo = place("u_lo", "u", KC, [P, KC, S], F32R)
        act_hi = place("act_hi", "a", 0, [P, FT, S], F32R)
        act_lo = place("act_lo", "a", FT, [P, FT, S], F32R)
        query = place("query", "a", 0, [P, HG, S])
        key = place("key", "a", 8, [P, HG, S])
        o_hi = place("o_hi", "a", 0, [P, HG, S], F32R)
        o_lo = place("o_lo", "a", 8, [P, HG, S], F32R)
        cum = place("cum", "a", 16, [P, HG, S])
        val = place("val", "a", 24, [P, TT, DM])
        gate = place("gate", "a", 32, [P, 4, S])
        lmask_f = place("lmask_f", "a", 41, [P, len(LEVELS) + 1, P])
        one_s = place("one_s", "a", 40, [P, P])
        zl = place("zl", "a", 36, [P, RING, S])
        q_dec = place("q_dec", "a", 40, [P, S])
        k_end = place("k_end", "a", 41, [P, S])
        scores = [place("scores0", "a", 42, [P, S]), place("scores1", "a", 43, [P, S])]
        aqk = place("aqk", "a", 0, [P, 2 * AH, S])
        av = place("av", "a", 24, [P, 3, TT, S])
        o_raw = place("o_raw", "a", 0, [P, AH, S])
        ao_hi = place("ao_hi", "a", 12, [P, AH, S], F32R)
        ao_lo = place("ao_lo", "a", 24, [P, AH, S], F32R)
        cs = place("cs", "a", 36, [P, 2, S])
        rot = place("rot", "a", 38, [P, 2, S])
        s_ab = [place("s_a", "a", 40, [P, TT, P]), place("s_b", "a", 41, [P, TT, P])]
        pt_a = place("pt_a", "a", 42, [P, TT, P])
        pt_b = place("pt_b", "a", 43, [P, TT, P])
        mrow = place("mrow", "a", 12, [GH, 3, S])
        lrow = place("lrow", "a", 12, [GH, 3, S])
        erow = place("erow", "a", 36, [GH, 3, S])
        trow = place("trow", "a", 39, [GH, S])
        x4 = place("x4", "a", 0, [P, KC, S])
        x4_hi = place("x4_hi", "a", 8, [P, KC, S], F32R)
        x4_lo = place("x4_lo", "a", 16, [P, KC, S], F32R)
        rr = place("rr", "a", 24, [P, KC, S])
        cc = place("cc", "a", 32, [P, KC, S])
        m2 = place("m2", "a", 8, [P, KC, S])
        m_hi = place("m_hi", "a", 8, [P, KC, S], F32R)
        m_lo = place("m_lo", "a", 16, [P, KC, S], F32R)
        xpad = place("xpad", "a", 40, [P, 2, S + 8])
        gel = place("gel", "a", 42.25, [P, S])
        sq8 = place("sq8", "u", 0, [P, KC, S])
        sgate = place("sgate", "a", 0, [P, KC, S])
        pf = place("pf", "a", 8, [P, 2, S])
        p_hi = place("p_hi", "a", 10, [P, 2, S], F32R)
        p_lo = place("p_lo", "a", 12, [P, 2, S], F32R)

        PB = [ctx.enter_context(nc.psum_tensor(f"bank{i}", [P, S], F32)) for i in range(8)]
        MS = PB[4]
        HB = PB[7]

        def pair(g):
            return PB[2 * (g % 2)], PB[2 * (g % 2) + 1]

        raw_loaded = [sem("raw_loaded0"), sem("raw_loaded1")]
        x_loaded = [sem(f"x_loaded{j}") for j in range(KC // 2)]
        vecs_loaded = sem("vecs_loaded")
        p_loaded = sem("p_loaded")
        const_loaded = sem("const_loaded")
        cs_loaded = sem("cs_loaded")
        out_stored = sem("out_stored")
        hi_ready = sem("hi_ready")
        lo_ready = sem("lo_ready")
        panel_done = sem("panel_done")
        group_free = sem("group_free")
        consts_ready = sem("consts_ready")
        waits_apart = sem("waits_apart")
        act_chain = sem("act_chain")
        dve_chain = sem("dve_chain")
        masks_ready = sem("masks_ready")
        h_ready = sem("h_ready")
        sq_ready = sem("sq_ready")
        sum_added = sem("sum_added")
        ms_ready = sem("ms_ready")
        rstd_ready = sem("rstd_ready")
        un_ready = sem("un_ready")
        uhi_ready = sem("uhi_ready")
        u_ready = sem("u_ready")
        sgin_ready = sem("sgin_ready")
        sg_ready = sem("sg_ready")
        r4_ready = sem("r4_ready")
        t5_ready = sem("t5_ready")
        r5_ready = sem("r5_ready")
        fin_ready = sem("fin_ready")
        qin_ready = sem("qin_ready")
        gin_ready = sem("gin_ready")
        forget_ready = sem("forget_ready")
        tok_done = sem("tok_done")
        pin_ready = sem("pin_ready")
        bin_ready = sem("bin_ready")
        yin_ready = sem("yin_ready")
        act_ready = sem("act_ready")
        fsig_ready = sem("fsig_ready")
        logf_ready = sem("logf_ready")
        cum_ready = sem("cum_ready")
        diff_ready = sem("diff_ready")
        exp_ready = sem("exp_ready")
        z_ready = sem("z_ready")
        lev_done = sem("lev_done")
        lev_free = sem("lev_free")
        blast_ready = sem("blast_ready")
        ends_ready = sem("ends_ready")
        dec_ready = sem("dec_ready")
        ket_done = sem("ket_done")
        ket_ready = sem("ket_ready")
        kv_done = sem("kv_done")
        states_ready = sem("states_ready")
        o_done = sem("o_done")
        osq_ready = sem("osq_ready")
        oms_done = sem("oms_done")
        orstd_ready = sem("orstd_ready")
        on_ready = sem("on_ready")
        oh_ready = sem("oh_ready")
        rot_ready = sem("rot_ready")
        v_ready = sem("v_ready")
        qk_ready = sem("qk_ready")
        s_done = sem("s_done")
        max_ready = sem("max_ready")
        p_ready = sem("p_ready")
        pt_done = sem("pt_done")
        pt_ready = sem("pt_ready")
        pv_done = sem("pv_done")
        oraw_ready = sem("oraw_ready")
        mrows_done = sem("mrows_done")
        mrow_ready = sem("mrow_ready")
        sums_ready = sem("sums_ready")
        lrows_done = sem("lrows_done")
        lrow_ready = sem("lrow_ready")
        row_diff = sem("row_diff")
        row_exp = sem("row_exp")
        row_sum = sem("row_sum")
        row_inv = sem("row_inv")
        fac_ready = sem("fac_ready")
        fac_done = sem("fac_done")
        prod_ready = sem("prod_ready")
        aohi_ready = sem("aohi_ready")
        ao_ready = sem("ao_ready")
        x4_ready = sem("x4_ready")
        z8_ready = sem("z8_ready")
        decay_ready = sem("decay_ready")
        m2_ready = sem("m2_ready")
        mult_ready = sem("mult_ready")
        mult_used = sem("mult_used")
        ig_ready = sem("ig_ready")
        xi_ready = sem("xi_ready")
        xs_ready = sem("xs_ready")
        sgc_ready = sem("sgc_ready")
        gel_ready = sem("gel_ready")
        mg_ready = sem("mg_ready")
        lam_exp = sem("lam_exp")
        lb_exp = sem("lb_exp")
        lb_in = sem("lb_in")
        pf_ready = sem("pf_ready")
        sgate_ready = sem("sgate_ready")
        gate_done = sem("gate_done")
        side_done = sem("side_done")
        gained = sem("gained")
        out_ready = sem("out_ready")
        out_ready_pool = sem("out_ready_pool")

        def wait_apart(eng, s, value):
            eng.wait_ge(s, value)
            eng.sem_inc(waits_apart, 1)

        def vec(first, j):
            return vecs[:, first + j:first + j + 1]

        def vec_i(first, i, step, s):
            return vecs[:, bass.ds(i * step + (first + s), 1)]

        def before_level(h, l):
            n = len(LEVELS) * h + l - RING
            return 8 * (n // len(LEVELS)) + n % len(LEVELS) + 1

        def level_tile(h, l):
            return zl[:, (len(LEVELS) * h + l) % RING, :]

        def score_bank(hd):
            return PB[5] if hd < GH else PB[5 + hd % 2]

        def turn_bank(hd):
            return PB[7] if hd < GH or hd % 2 == 0 else MS

        def weigh_bank(hd):
            return PB[7] if hd < GH else PB[(4, 5, 6, 7, 2, 3, 2, 3)[hd - GH]]

        def factor_bank(hd):
            return PB[(5, 6, 7, 4)[hd % 4]]

        def scores_of(hd):
            return s_ab[0 if hd < GH else hd % 2]

        def turned_scores(hd):
            return pt_a[:] if hd < GH else aqk[:, AH + hd, :].rearrange("p (n c) -> p n c", c=P)

        def rows_of(bank, g):
            src = bank[0:GH, :]
            return src.rearrange("p (r a) -> p r a", r=TT) if g else src

        def row_out(t, g):
            return by_four(t[:, g, :]) if g else t[:, g, :]

        def blocks(t, m):
            return t.rearrange("p (n c) -> p n c", c=2 * m)

        def by_four(t):
            return t.rearrange("p (a r) -> p r a", r=TT)

        block = ctx.enter_context(nc.Block())

        @block.sync
        def _(sp):
            def load_panels(a, b):
                n = (b - a) // 2
                with sp.Fori(0, n) as i:
                    for s in range(2):
                        sp.wait_ge(lo_ready, i * 2 + (a + s - 1))
                        sp.dma_start(raw[:, (a + s) % 2, :], wall[i * 2 + (a + s)]).then_inc(raw_loaded[(a + s) % 2], 16)
                if (b - a) % 2:
                    sp.wait_ge(lo_ready, b - 2)
                    sp.dma_start(raw[:, (b - 1) % 2, :], wall[b - 1]).then_inc(raw_loaded[(b - 1) % 2], 16)

            x_v = x_t.rearrange("(k p) s -> p k s", p=P)
            sp.dma_start(raw[:, 0, :], wall[0]).then_inc(raw_loaded[0], 16)
            sp.dma_start(vecs[:], vecs_d).then_inc(vecs_loaded, 16)
            for j in range(KC // 2):
                sp.dma_start(h[:, 2 * j:2 * j + 2, :], x_v[:, 2 * j:2 * j + 2, :]).then_inc(x_loaded[j], 16)
            sp.dma_start(raw[:, 1, :], wall[1]).then_inc(raw_loaded[1], 16)
            sp.dma_start(ident[:], ident_d).then_inc(const_loaded, 16)
            sp.dma_start(amask[:], amask_d).then_inc(const_loaded, 16)
            sp.dma_start(lmask_f[:], lmask_d).then_inc(const_loaded, 16)
            sp.dma_start(sel[:], sel_d).then_inc(const_loaded, 16)
            load_panels(2, PAN["a0"] + 2)
            sp.wait_ge(panel_done, PAN["a0"])
            sp.dma_start(cs[:], cs_d).then_inc(cs_loaded, 16)
            load_panels(PAN["a0"] + 2, PAN["gate"] + 2)
            sp.wait_ge(panel_done, PAN["gate"])
            sp.dma_start(pf[:], p_t.rearrange("(k p) s -> p k s", p=P)).then_inc(p_loaded, 16)
            load_panels(PAN["gate"] + 2, PAN["end"])
            out_v = out_t.rearrange("(k p) s -> p k s", p=P)
            stores = ((out_ready, 0, 2), (out_ready_pool, 5, 6), (out_ready, 2, 4), (out_ready_pool, 6, 7),
                      (out_ready, 4, 5), (out_ready_pool, 7, 8))
            for ready, a, b in stores:
                sp.wait_ge(ready, b - (OUT_SPLIT if a >= OUT_SPLIT else 0))
                sp.dma_start(out_v[:, a:b, :], h[:, a:b, :]).then_inc(out_stored, 16)
            sp.wait_ge(out_stored, 16 * len(stores))

        @block.gpsimd
        def _(pool):
            def lo(p, s, i=None):
                q = p if i is None else i * 2 + p
                pool.wait_ge(hi_ready, q + 1)
                nc.gpsimd.tensor_tensor(w_lo[:, s, :], raw[:, s, :], w_hi[:, s, :].bitcast(F32),
                                        ALU.subtract).then_inc(lo_ready, 1)

            def lo_panels(a, b):
                n = (b - a) // 2
                with pool.Fori(0, n) as i:
                    for s in range(2):
                        lo(a + s, (a + s) % 2, i)
                if (b - a) % 2:
                    lo(b - 1, (b - 1) % 2)

            nc.gpsimd.memset(ones[:], 1.0).then_inc(consts_ready, 1)
            nc.gpsimd.memset(one_s[:], 1.0).then_inc(consts_ready, 1)
            lo_panels(0, PAN["g"] + 2)

            def differences(h, levels):
                for l in levels:
                    m = LEVELS[l]
                    n = S // (2 * m)
                    b = blocks(cum[:, h, :], m)
                    pool.wait_ge(cum_ready, h + 1)
                    if (h, l) >= (0, RING):
                        pool.wait_ge(lev_done, before_level(h, l))
                    nc.gpsimd.tensor_tensor(blocks(level_tile(h, l), m), b,
                                            b[:, :, m - 1:m].to_broadcast([P, n, 2 * m]),
                                            ALU.subtract).then_inc(diff_ready, 1)

            differences(0, range(RING))
            for hd in range(HG):
                differences(hd, range(RING, len(LEVELS)))
                if hd % 2:
                    p = PAN["g"] + hd // 2 + 2
                    lo(p, p % 2)
                pool.wait_ge(ends_ready, hd + 1)
                nc.gpsimd.tensor_tensor(k_end[:, 0:3 * P], k_end[:, 0:3 * P], key[:, hd, 0:3 * P], ALU.mult)
                nc.gpsimd.tensor_tensor(q_dec[:], q_dec[:], query[:, hd, :], ALU.mult).then_inc(dec_ready, 1)
                if hd + 1 < HG:
                    differences(hd + 1, range(RING))

            lo_panels(PAN["hgrn_out"] + 2, PAN["end"])
            for j in range(1, KC - 2):
                pool.wait_ge(sq_ready, SQ0[7] + j + 1)
                if j > 1:
                    pool.wait_ge(sum_added, SQ0[7] + j - 1)
                nc.gpsimd.tensor_tensor(ssq[:], ssq[:] if j > 1 else sq8[:, 0, :], sq8[:, j, :], ALU.add)\
                    .then_inc(sum_added, 1)
            pool.wait_ge(gained, KC)
            pool.wait_ge(rstd_ready, 8)
            for j in range(OUT_SPLIT, KC):
                nc.gpsimd.tensor_tensor(h[:, j, :], h[:, j, :], rstd[:], ALU.mult).then_inc(out_ready_pool, 1)


        @block.scalar
        def _(act):
            ch = Chain(act, act_chain)

            def af(out, in_, func, **k):
                return nc.scalar.activation(out, in_, func, **k)

            def conv(p, i=None, step=2):
                s = p % 2
                if i is None:
                    act.wait_ge(raw_loaded[s], 16 * (p // 2 + 1))
                    if p >= 2:
                        act.wait_ge(panel_done, p - 1)
                else:
                    act.wait_ge(raw_loaded[s], i * (8 * step) + 16 * (p // 2 + 1))
                    act.wait_ge(panel_done, i * step + (p - 1))
                af(w_hi[:, s, :], raw[:, s, :], ACT.Copy).then_inc(hi_ready, 1)

            def squares(m, j):
                if m == 7:
                    af(sq8[:, j, :], h[:, j, :], ACT.Square).then_inc(sq_ready, 1)
                    return
                for a in range(2 if m == TWIN else 1):
                    n = SQ0[m] + (2 * j + a if m == TWIN else j)
                    if n >= 2:
                        act.wait_ge(sum_added, n - 1)
                    k = {"scale": vec(GAIN[m], j)} if a else {}
                    af(sq[:, n % 2, :], h[:, j, :], ACT.Square, **k).then_inc(sq_ready, 1)

            def upper(m, j):
                act.wait_ge(un_ready, KC * m + j + 1)
                af(u_hi[:, j, :], un[:, j % 2, :], ACT.Copy).then_inc(uhi_ready, 1)

            def norm_scale(m):
                act.wait_ge(ms_ready, m + 1)
                if m == TWIN:
                    ch.link(af(rstd2[:], MS[:], ACT.Ln, bias=eps[:, 0:1], scale=1.0 / DM))
                    af(rstd2[:], rstd2[:], ACT.Exp, scale=-0.5).then_inc(r4_ready, 1)
                    act.wait_ge(t5_ready, 1)
                    ch.link(af(rstd[:], sq[:, 0, :], ACT.Ln, bias=eps[:, 0:1], scale=1.0 / DM))
                    af(rstd[:], rstd[:], ACT.Exp, scale=-0.5).then_inc(r5_ready, 1)
                    return
                ch.step(af(rstd[:], MS[:], ACT.Ln, bias=eps[:, 0:1], scale=1.0 / DM))
                if m in (0, 2):
                    ch.step(af(rcol[:], PB[5][:, 0:2 * TT], ACT.Ln, bias=eps[:, 0:1], scale=1.0 / DM))
                ch.settle()
                af(rstd[:], rstd[:], ACT.Exp, scale=-0.5).then_inc(rstd_ready, 1)
                if m in (0, 2):
                    ch.link(af(rcol[:], rcol[:], ACT.Exp, scale=-0.5))

            def residual(p0, per, m):
                for q in range(4):
                    for t in range(per - 1):
                        conv(p0 + per * q + t + 2)
                    for j in (2 * q, 2 * q + 1):
                        upper(m, j)
                    conv(p0 + per * (q + 1) + 1)
                    for j in (2 * q, 2 * q + 1):
                        squares(m, j)

            def ffn(f, m):
                norm_scale(m)
                with act.Fori(0, FT // 2) as i:
                    for s in range(2):
                        act.wait_ge(sgin_ready, i * 2 + (FT * f + s + 1))
                        af(sq[:, s, :], sq[:, s, :], ACT.Silu).then_inc(sg_ready, 1)
                        conv(PAN[f"up{f}"] + s + 2, i)
                residual(PAN[f"down{f}"], 3, m + 1)

            act.wait_ge(consts_ready, 2)
            ch.link(af(eps[:], ones[:, 0:1], ACT.Copy, scale=EPS))
            conv(0)
            for q in range(4):
                for j in (2 * q, 2 * q + 1):
                    upper(0, j)
                for j in (2 * q, 2 * q + 1):
                    squares(0, j)
            act.wait_ge(lb_in, 2)
            af(lb[:, 0:3, :], lb[:, 0:3, :], ACT.Exp).then_inc(lb_exp, 1)
            af(spl[:, 1, :], spl[:, 1, :], ACT.Exp).then_inc(lam_exp, 1)
            conv(1)
            norm_scale(0)

            for t in range(4):
                for c in range(2):
                    j = 2 * t + c
                    act.wait_ge(fin_ready, j + 1)
                    af(key[:, j, :], key[:, j, :], ACT.Sigmoid).then_inc(fsig_ready, 1)
                conv(PAN["f"] + t + 2)
            for t in range(4):
                for c in range(2):
                    j = 2 * t + c
                    act.wait_ge(qin_ready, j + 1)
                    af(query[:, j, :], query[:, j, :], ACT.Silu)
                for j in (2 * t, 2 * t + 1):
                    act.wait_ge(forget_ready, j + 1)
                    af(cum[:, j, :], cum[:, j, :], ACT.Ln).then_inc(logf_ready, 1)
                conv(PAN["q"] + t + 2)

            def by_tokens(p0, g, n_th, col, tile):
                conv(p0 + 2)
                for t in range(TT):
                    act.wait_ge(tok_done, TT * n_th + t + 1)
                    ins = af(tile(t), PB[t][:], ACT.Copy, scale=rcol[:, col + t:col + t + 1])
                    if t % 2:
                        ins.then_inc(group_free, 1)
                conv(p0 + 3)

            for t in range(2):
                by_tokens(PAN["i"] + 2 * t, GRP["i"] + 2 * t, t, 0, lambda c: val[:, c, t * S:(t + 1) * S])
            def decays(hd, levels):
                for l in levels:
                    m = LEVELS[l]
                    act.wait_ge(diff_ready, len(LEVELS) * hd + l + 1)
                    z = blocks(level_tile(hd, l), m)
                    af(z[:, :, m:2 * m], z[:, :, m:2 * m], ACT.Exp)
                    af(z[:, :, 0:m], z[:, :, 0:m], ACT.Exp, scale=-1.0).then_inc(exp_ready, 1)

            def keys_by_token(hd):
                act.wait_ge(ket_done, hd + 1)
                af(ssq[:, 0:3 * P], HB[:, 0:3 * P], ACT.Copy).then_inc(ket_ready, 1)

            def head_squares(hd):
                act.wait_ge(o_done, hd + 1)
                af(sq[:, 0, :], HB[:], ACT.Square).then_inc(osq_ready, 1)

            def ends(hd):
                act.wait_ge(blast_ready, hd + 1)
                if hd:
                    act.wait_ge(o_done, hd)
                af(q_dec[:], cum[:, hd, :], ACT.Exp)
                for c in range(TT - 1):
                    af(k_end[:, c * P:(c + 1) * P], cum[:, hd, c * P:(c + 1) * P], ACT.Exp,
                       bias=b_last[:, c:c + 1], scale=-1.0)
                af(e_last[:], b_last[:], ACT.Exp).then_inc(ends_ready, 1)

            def root(hd):
                act.wait_ge(oms_done, hd + 1)
                ch.link(af(rstd2[:], MS[:], ACT.Ln, bias=eps[:, 0:1], scale=1.0 / P))
                af(rstd2[:], rstd2[:], ACT.Exp, scale=-0.5).then_inc(orstd_ready, 1)

            decays(0, range(RING))
            for hd in range(HG):
                if hd:
                    keys_by_token(hd - 1)
                if hd % 2:
                    conv(PAN["g"] + hd // 2 + 2)
                decays(hd, range(RING, len(LEVELS)))
                if hd:
                    head_squares(hd - 1)
                ends(hd)
                if hd % 2:
                    for j in (hd - 1, hd):
                        act.wait_ge(gin_ready, j + 1)
                        af(gate[:, j % 4, :], gate[:, j % 4, :], ACT.Silu)
                if hd:
                    root(hd - 1)
                if hd + 1 < HG:
                    decays(hd + 1, range(RING))
            keys_by_token(HG - 1)
            head_squares(HG - 1)
            root(HG - 1)
            residual(PAN["hgrn_out"], 1, 1)
            ffn(0, 1)

            def exps(hd):
                act.wait_ge(max_ready, hd + 1)
                r = 4 * (hd % 2)
                for n in range(TT):
                    s_n = scores_of(hd)[:, n, :]
                    ins = af(s_n, s_n, ACT.Exp, bias=cols[:, r + 1, n:n + 1], scale=ATT_SCALE,
                             accum_out=cols[:, r + 2, n:n + 1])
                    if hd < GH and n:
                        ins = af(s_ab[1][:, n, :], s_ab[1][:, n, :], ACT.Exp, bias=cols[:, r + 1, n:n + 1],
                                 scale=ATT_SCALE, accum_out=cols[:, r + 3, n:n + 1])
                ins.then_inc(p_ready, 1)

            def turned(hd):
                act.wait_ge(pt_done, hd + 1)
                if hd < GH:
                    af(pt_b[:, 1:TT, :], MS[:, P:S].rearrange("p (n c) -> p n c", c=P), ACT.Copy)
                af(turned_scores(hd), turn_bank(hd)[:].rearrange("p (n c) -> p n c", c=P), ACT.Copy)\
                    .then_inc(pt_ready, 1)

            def halves(g, t):
                for c in range(2):
                    bank = pair(GRP[f"a{g}"] + t)[c]
                    act.wait_ge(qk_ready, 4 * g + t)
                    af(rot[0:64, c, :], bank[64:128, :], ACT.Copy)
                    af(rot[64:128, c, :], bank[0:64, :], ACT.Copy).then_inc(rot_ready, 1)

            def values(g, c):
                act.wait_ge(tok_done, TT * (2 + g) + c + 1)
                k = (TT if g else 0) + c
                ins = af(av[:, g, c, :], PB[c][:], ACT.Copy, scale=rcol[:, k:k + 1])
                if c % 2:
                    ins.then_inc(group_free, 1)
                if c == TT - 1:
                    act.wait_ge(group_free, GRP[f"v{g}" if g else "a1"] + (4 if g else 2))
                    act.sem_inc(v_ready, 1)

            def attended(hd):
                act.wait_ge(pv_done, hd + 1)
                af(by_four(o_raw[:, hd, :]), weigh_bank(hd)[:].rearrange("p (r a) -> p r a", r=TT), ACT.Copy)\
                    .then_inc(oraw_ready, 1)

            def weighted_upper(hd):
                act.wait_ge(prod_ready, hd + 1)
                af(ao_hi[:, hd, :], un[:, hd % 2, :], ACT.Copy).then_inc(aohi_ready, 1)

            norm_scale(2)
            for t in range(4):
                act.wait_ge(panel_done, PAN["a0"] + t + 1)
                halves(0, t)
                conv(PAN["a0"] + t + 2)
            conv(PAN["a0"] + 6)
            for c in range(TT):
                values(0, c)
            conv(PAN["a0"] + 7)
            for g in (1, 2):
                for t in range(4):
                    p, hd = PAN[f"a{g}"] + t, 4 * (g - 1) + t
                    act.wait_ge(panel_done, p + 1)
                    if hd:
                        turned(hd - 1)
                    halves(g, t)
                    conv(p + 2)
                    exps(hd)
            conv(PAN["v1"] + 2)
            turned(7)
            exps(8)
            exps(9)
            values(1, 0)
            turned(8)
            values(1, 1)
            turned(9)
            values(1, 2)
            values(1, 3)
            conv(PAN["v1"] + 3)
            exps(10)
            exps(11)
            act.wait_ge(row_diff, 1)
            af(erow[:], erow[:], ACT.Exp).then_inc(row_exp, 1)
            turned(10)
            turned(11)
            conv(PAN["v2"] + 2)
            attended(4)
            act.wait_ge(row_sum, 1)
            ch.link(af(trow[:], trow[:], ACT.Ln))
            af(trow[:], trow[:], ACT.Exp, scale=-1.0).then_inc(row_inv, 1)
            for hd in (5, 6, 7):
                attended(hd)
            for c in range(TT):
                values(2, c)
            conv(PAN["v2"] + 3)
            for hd in (0, 1):
                weighted_upper(hd)
            for hd in (8, 9):
                attended(hd)
            for hd in range(2, 6):
                weighted_upper(hd)
            for hd in (10, 11):
                attended(hd)
            for hd in range(6, AH):
                weighted_upper(hd)
            residual(PAN["attn_out"], 2, 3)
            ffn(1, 3)

            norm_scale(TWIN)
            for t in range(4):
                conv(PAN["rx"] + t + 2)
            with act.Fori(0, KC // 2) as i:
                for s in range(2):
                    p, g = PAN["cx"] + s, GRP["cx"] + s
                    act.wait_ge(panel_done, i * 2 + (p + 1))
                    act.wait_ge(group_free, i * 2 + (g + 1))
                    af(sq[:, s, :], pair(g)[1][:], ACT.Copy).then_inc(xs_ready, 1)
                    conv(p + 2, i)
            act.wait_ge(group_free, GRP["rg"] + 2)
            for s in range(2):
                for q in range(4):
                    g = GRP["rg"] + 4 * s + q
                    act.wait_ge(gate_done, 4 * s + q + 1)
                    for c in range(2):
                        j = 2 * q + c
                        if s == 0:
                            ins = af(rr[:, j, :], pair(g)[c][:], ACT.Sigmoid, bias=vec(V_BR, j))
                        else:
                            if j >= 2:
                                act.wait_ge(xi_ready, j - 1)
                            af(un[:, c, :], pair(g)[c][:], ACT.Sigmoid, bias=vec(V_BI, j)).then_inc(ig_ready, 1)
                    if s == 0:
                        ins.then_inc(group_free, 1)
                    else:
                        act.wait_ge(ig_ready, 2 * q + 2)
                        act.sem_inc(group_free, 1)
                conv(PAN["rg"] + s + 2)
            with act.Fori(0, KC // 2) as i:
                for s in range(2):
                    act.wait_ge(z8_ready, i * 2 + (s + 1))
                    af(rr[:, i * 2 + s, :], sq[:, s, :], ACT.Exp, scale=-1.0).then_inc(decay_ready, 1)
                    af(sq[:, s, :], sq[:, s, :], ACT.Tanh).then_inc(decay_ready, 1)
                    act.wait_ge(bin_ready, i * 2 + (s + 1))
                    af(un[:, s, :], un[:, s, :], ACT.Sigmoid).then_inc(sgc_ready, 1)
                    conv(PAN["bg"] + s + 2, i)
            act.wait_ge(m2_ready, KC)
            with act.Fori(0, KC // 2) as i:
                for s in range(2):
                    act.wait_ge(mult_used, i * 2 + s)
                    af(gel[:], m2[:, i * 2 + s, :], ACT.Sqrt).then_inc(mult_ready, 1)
                    act.wait_ge(yin_ready, i * 4 + (2 * s + 2))
                    af(sq[:, s, :], sq[:, s, :], ACT.Gelu_apprx_tanh).then_inc(gel_ready, 1)
                    af(un[:, s, :], un[:, s, :], ACT.Sigmoid).then_inc(gel_ready, 1)
                    conv(PAN["yg"] + s + 2, i)
            residual(PAN["rg_out"], 1, 5)
            ffn(2, 5)
            norm_scale(6)
            for q in range(4):
                for c in range(2):
                    j = 2 * q + c
                    act.wait_ge(pin_ready, j + 1)
                    af(sgate[:, j, :], sgate[:, j, :], ACT.Sigmoid).then_inc(sgate_ready, 1)
                if PAN["gate"] + q + 2 < PAN["end"]:
                    conv(PAN["gate"] + q + 2)
            for j in range(KC):
                act.wait_ge(h_ready, KC * 7 + j + 1)
                squares(7, j)
            norm_scale(7)

        @block.vector
        def _(dve):
            ch = Chain(dve, dve_chain)
            tt, ts, stt = nc.vector.tensor_tensor, nc.vector.tensor_scalar, nc.vector.scalar_tensor_tensor
            cp = nc.vector.tensor_copy

            def un_tile(m, j):
                if j >= 2:
                    dve.wait_ge(u_ready, KC * m + j - 1)
                gain2 = (vec(GAIN[m] + KC, j), ALU.mult, ALU.mult) if m == TWIN else (None, ALU.mult)
                ts(un[:, j % 2, :], h[:, j, :], vec(GAIN[m], j), *gain2).then_inc(un_ready, 1)

            def lower(m, j):
                dve.wait_ge(uhi_ready, KC * m + j + 1)
                tt(u_lo[:, j, :], un[:, j % 2, :], u_hi[:, j, :].bitcast(F32), ALU.subtract).then_inc(u_ready, 1)

            def sums(m, j):
                for a in range(2 if m == TWIN else 1):
                    n = SQ0[m] + (2 * j + a if m == TWIN else j)
                    total = ssq2 if a else ssq
                    dve.wait_ge(sq_ready, n + 1)
                    if j == 0:
                        ins = cp(total[:], sq[:, n % 2, :])
                    else:
                        dve.wait_ge(sum_added, n)
                        ins = tt(total[:], total[:], sq[:, n % 2, :], ALU.add)
                    ins.then_inc(sum_added, 1)

            def residual(p0, g0, per, r, m):
                for q in range(4):
                    dve.wait_ge(panel_done, p0 + per * (q + 1))
                    for c in range(2):
                        j = 2 * q + c
                        tt(h[:, j, :], h[:, j, :], pair(g0 + q)[c][:], ALU.add).then_inc(h_ready, 1)
                        dve.wait_ge(h_ready, KC * r + j + 1)
                        un_tile(m, j)
                    dve.sem_inc(group_free, 1)
                    for c in range(2):
                        lower(m, 2 * q + c)
                    for c in range(2):
                        sums(m, 2 * q + c)

            def scaled_pair(g, tiles, ready, before):
                for c in range(2):
                    tt(tiles[c], pair(g)[c][:], rstd[:], ALU.mult).then_inc(ready, 1)
                dve.wait_ge(ready, before + 2)
                dve.sem_inc(group_free, 1)

            def ffn(f, r, m):
                dve.wait_ge(rstd_ready, m + 1)
                with dve.Fori(0, FT // 2) as i:
                    ch.enter(i, 4)
                    for s in range(2):
                        g = GRP[f"up{f}"] + s
                        dve.wait_ge(panel_done, i * 2 + (PAN[f"up{f}"] + s + 1))
                        tt(sq[:, s, :], pair(g)[0][:], rstd[:], ALU.mult).then_inc(sgin_ready, 1)
                        tt(un[:, s, :], pair(g)[1][:], rstd[:], ALU.mult).then_inc(group_free, 1)
                        dve.wait_ge(group_free, i * 2 + (g + 3))
                        dve.wait_ge(sg_ready, i * 2 + (FT * f + s + 1))
                        ch.link(tt(un[:, s, :], un[:, s, :], sq[:, s, :], ALU.mult))
                        ch.link(cp(act_hi[:, i * 2 + s, :], un[:, s, :]))
                        tt(act_lo[:, i * 2 + s, :], un[:, s, :], act_hi[:, i * 2 + s, :].bitcast(F32),
                           ALU.subtract).then_inc(act_ready, 1)
                ch.leave(FT // 2)
                residual(PAN[f"down{f}"], GRP[f"down{f}"], 3, r, m + 1)

            dve.wait_ge(vecs_loaded, 16)
            for q in range(5):
                if q:
                    for j in (2 * q - 2, 2 * q - 1):
                        lower(0, j)
                if q < 4:
                    dve.wait_ge(x_loaded[q], 16)
                    for j in (2 * q, 2 * q + 1):
                        un_tile(0, j)
                if q:
                    for j in (2 * q - 2, 2 * q - 1):
                        sums(0, j)
            row = [vecs[:, V_LB + KC * k:V_LB + KC * (k + 1)] for k in range(3)]
            lam = vecs[:, V_LAM:V_LAM + KC]
            ch.link(tt(lb[:, 3, :], row[0], row[1], ALU.max))
            ch.link(tt(lb[:, 3, :], lb[:, 3, :], row[2], ALU.max))
            for k in range(3):
                ins = tt(lb[:, k, :], row[k], lb[:, 3, :], ALU.subtract)
            ins.then_inc(lb_in, 1)
            ch.link(ts(spl[:, 2, :], lam, -1.0, None, ALU.mult))
            ch.link(ts(spl[:, 0, :], spl[:, 2, :], 0.0, None, ALU.max))
            tt(spl[:, 1, :], lam, spl[:, 2, :], ALU.min).then_inc(lb_in, 1)
            dve.wait_ge(lb_exp, 1)
            ch.link(tt(lb[:, 3, :], lb[:, 0, :], lb[:, 1, :], ALU.add))
            ch.link(tt(lb[:, 3, :], lb[:, 3, :], lb[:, 2, :], ALU.add))
            ch.link(nc.vector.reciprocal(lb[:, 4, :], lb[:, 3, :]))
            ch.link(tt(lb[:, 0, :], lb[:, 0, :], lb[:, 4, :], ALU.mult))
            ch.link(ts(lb[:, 1, :], lb[:, 0, :], -1.0, 1.0, ALU.mult, ALU.add))
            dve.wait_ge(lam_exp, 1)
            ch.link(ts(spl[:, 2, :], spl[:, 1, :], 2.0, None, ALU.add))
            ch.link(nc.vector.reciprocal(spl[:, 3, :], spl[:, 2, :]))
            ch.link(tt(spl[:, 1, :], spl[:, 1, :], spl[:, 3, :], ALU.mult))
            ch.link(tt(spl[:, 2, :], spl[:, 1, :], spl[:, 1, :], ALU.mult))
            ch.link(ts(spl[:, 3, :], spl[:, 2, :], 1.0 / 19, 1.0 / 17, ALU.mult, ALU.add))
            for k in (15, 13, 11, 9, 7, 5, 3, 1):
                ch.link(tt(spl[:, 3, :], spl[:, 3, :], spl[:, 2, :], ALU.mult))
                ch.link(ts(spl[:, 3, :], spl[:, 3, :], 1.0 / k, None, ALU.add))
            ch.link(tt(spl[:, 3, :], spl[:, 3, :], spl[:, 1, :], ALU.mult))
            ch.link(stt(spl[:, 0, :], spl[:, 3, :], 2.0, spl[:, 0, :], ALU.mult, ALU.add))
            ch.link(ts(spl[:, 0, :], spl[:, 0, :], RG_C, None, ALU.mult))
            dve.wait_ge(const_loaded, 64)
            cp(lmask[:], lmask_f[:]).then_inc(masks_ready, 1)

            dve.wait_ge(rstd_ready, 1)
            for t in range(4):
                dve.wait_ge(panel_done, PAN["f"] + t + 1)
                scaled_pair(GRP["f"] + t, (key[:, 2 * t, :], key[:, 2 * t + 1, :]), fin_ready, 2 * t)
                for j in (2 * t, 2 * t + 1):
                    dve.wait_ge(fsig_ready, j + 1)
                    ch.link(ts(cum[:, j, :], key[:, j, :], lb[:, 1, j:j + 1], lb[:, 0, j:j + 1], ALU.mult, ALU.add))
                    ts(key[:, j, :], cum[:, j, :], -1.0, 1.0, ALU.mult, ALU.add).then_inc(forget_ready, 1)
            for t in range(4):
                dve.wait_ge(panel_done, PAN["q"] + t + 1)
                scaled_pair(GRP["q"] + t, (query[:, 2 * t, :], query[:, 2 * t + 1, :]), qin_ready, 2 * t)
                for j in (2 * t, 2 * t + 1):
                    dve.wait_ge(logf_ready, j + 1)
                    for c in range(TT):
                        b = cum[:, j, c * P:(c + 1) * P]
                        ins = nc.vector.tensor_tensor_scan(b, one_s[:], b, 0.0, ALU.mult, ALU.add)
                    ins.then_inc(cum_ready, 1)
            dve.wait_ge(cum_ready, HG)
            def decayed(hd, levels):
                for l in levels:
                    m = LEVELS[l]
                    dve.wait_ge(exp_ready, len(LEVELS) * hd + l + 1)
                    z, q, k = (blocks(t, m) for t in (level_tile(hd, l), query[:, hd, :], key[:, hd, :]))
                    tt(z[:, :, m:2 * m], z[:, :, m:2 * m], q[:, :, m:2 * m], ALU.mult)
                    tt(z[:, :, 0:m], z[:, :, 0:m], k[:, :, 0:m], ALU.mult).then_inc(z_ready, 1)

            def take_level(hd, l):
                n = 8 * hd + l
                dve.wait_ge(lev_done, n + 1)
                bank = PB[5 + l % 2][:].rearrange("p (n c) -> p n c", c=P)
                s3 = scores[hd % 2][:].rearrange("p (n c) -> p n c", c=P)
                if l == 0:
                    ins = tt(s3, bank, amask[:, 3:4, :].to_broadcast([P, TT, P]), ALU.mult)
                else:
                    dve.wait_ge(lev_free, n)
                    ins = nc.vector.copy_predicated(s3, lmask[:, l:l + 1, :].to_broadcast([P, TT, P]), bank)
                ins.then_inc(lev_free, 1)

            def chunk_states(hd):
                dve.wait_ge(kv_done, hd + 1)
                ch.link(cp(state[:, 0, :], HB[:, 0:P]))
                for c in range(1, 3):
                    ins = stt(state[:, c, :], state[:, c - 1, :], e_last[:, c:c + 1], HB[:, c * P:(c + 1) * P],
                              ALU.mult, ALU.add)
                    if c == 1:
                        ch.link(ins)
                ins.then_inc(states_ready, 1)

            def head_out(hd):
                dve.wait_ge(orstd_ready, hd + 1)
                stt(un[:, 0, :], HB[:], vec(V_HG, 0), rstd2[:], ALU.mult, ALU.mult).then_inc(on_ready, 1)
                dve.wait_ge(on_ready, hd + 1)
                ch.link(tt(un[:, 1, :], un[:, 0, :], gate[:, hd % 4, :], ALU.mult))
                ch.link(cp(o_hi[:, hd, :], un[:, 1, :]))
                tt(o_lo[:, hd, :], un[:, 1, :], o_hi[:, hd, :].bitcast(F32), ALU.subtract).then_inc(oh_ready, 1)

            dve.wait_ge(masks_ready, 1)
            decayed(0, range(RING))
            for hd in range(HG):
                if hd:
                    dve.wait_ge(ends_ready, hd)
                cp(b_last[:], cum[:, hd, P - 1:S:P]).then_inc(blast_ready, 1)
                take_level(hd, 0)
                take_level(hd, 1)
                if hd:
                    chunk_states(hd - 1)
                decayed(hd, (4,))
                take_level(hd, 2)
                decayed(hd, (5,))
                take_level(hd, 3)
                if hd % 2:
                    g = GRP["g"] + hd // 2
                    dve.wait_ge(panel_done, PAN["g"] + hd // 2 + 1)
                    scaled_pair(g, (gate[:, (hd - 1) % 4, :], gate[:, hd % 4, :]), gin_ready, hd - 1)
                decayed(hd, (6,))
                for l in range(4, 8):
                    take_level(hd, l)
                if hd:
                    head_out(hd - 1)
                if hd + 1 < HG:
                    decayed(hd + 1, range(RING))
            chunk_states(HG - 1)
            head_out(HG - 1)
            residual(PAN["hgrn_out"], GRP["hgrn_out"], 1, 0, 1)
            ffn(0, 1, 1)

            def rotate(g, t):
                grp = GRP[f"a{g}"] + t
                for c in range(2):
                    j = (t // 2) * AH + GH * g + 2 * (t % 2) + c
                    dve.wait_ge(rot_ready, 2 * (4 * g + t) + c + 1)
                    ch.step(tt(un[:, c, :], pair(grp)[c][:], cs[:, 0, :], ALU.mult))
                    ch.link(tt(rot[:, c, :], rot[:, c, :], cs[:, 1, :], ALU.mult))
                    ins = tt(aqk[:, j, :], un[:, c, :], rot[:, c, :], ALU.add)
                ins.then_inc(qk_ready, 1)
                dve.wait_ge(qk_ready, 4 * g + t + 1)
                dve.sem_inc(group_free, 1)

            def spread(k, n=TT):
                return amask[:, k:k + 1, :].to_broadcast([P, n, P])

            def maxima(hd):
                r = 4 * (hd % 2)
                s_h = scores_of(hd)
                dve.wait_ge(s_done, hd + 1)
                bank = score_bank(hd)[:].rearrange("p (n c) -> p n c", c=P)
                ch.step(tt(s_h[:], bank, spread(0 if hd < 2 * GH else 2), ALU.add))
                if hd < GH:
                    prev = PB[6][:, P:S].rearrange("p (n c) -> p n c", c=P)
                    ch.step(tt(s_ab[1][:, 1:TT, :], prev, spread(1, TT - 1), ALU.add))
                ch.settle()
                ch.step(nc.vector.tensor_reduce(cols[:, r, :], s_h[:], AX_X, ALU.max))
                if hd < GH:
                    ch.link(nc.vector.tensor_reduce(cols[:, r + 3, 1:TT], s_ab[1][:, 1:TT, :], AX_X, ALU.max))
                    ch.step(tt(cols[:, r, 1:TT], cols[:, r, 1:TT], cols[:, r + 3, 1:TT], ALU.max))
                ch.settle()
                cp(mst[:, hd, :], cols[:, r, :])
                ts(cols[:, r + 1, :], cols[:, r, :], -ATT_SCALE, None, ALU.mult).then_inc(max_ready, 1)

            def head_sums(hd):
                r = 4 * (hd % 2)
                dve.wait_ge(p_ready, hd + 1)
                ch.link(cp(lst[:, hd, :], cols[:, r + 2, :]))
                if hd < GH:
                    ch.link(tt(lst[:, hd, 1:TT], cols[:, r + 2, 1:TT], cols[:, r + 3, 1:TT], ALU.add))

            def attended(hd):
                dve.wait_ge(pv_done, hd + 1)
                cp(o_raw[:, hd, :], weigh_bank(hd)[:]).then_inc(oraw_ready, 1)

            dve.wait_ge(cs_loaded, 16)
            dve.wait_ge(rstd_ready, 3)
            for a in range(2):
                ins = tt(cs[:, a, :], cs[:, a, :], rstd[:], ALU.mult)
            ch.link(ins)
            for t in range(4):
                rotate(0, t)
            for g in (1, 2):
                for t in range(4):
                    hd = 4 * (g - 1) + t
                    rotate(g, t)
                    if hd:
                        head_sums(hd - 1)
                    maxima(hd)
                    if 0 < hd <= GH:
                        attended(hd - 1)
            head_sums(7)
            maxima(8)
            maxima(9)
            head_sums(8)
            maxima(10)
            head_sums(9)
            maxima(11)
            dve.wait_ge(mrows_done, 1)
            for g in range(3):
                ch.step(ts(row_out(mrow, g), rows_of(PB[5 + g], g), ATT_SCALE, None, ALU.mult))
            ch.settle()
            dve.sem_inc(mrow_ready, 1)
            ch.link(tt(trow[:], mrow[:, 0, :], mrow[:, 1, :], ALU.max))
            ch.link(tt(trow[:], trow[:], mrow[:, 2, :], ALU.max))
            for g in range(3):
                ins = tt(erow[:, g, :], mrow[:, g, :], trow[:], ALU.subtract)
            ins.then_inc(row_diff, 1)
            head_sums(10)
            head_sums(11)
            dve.sem_inc(sums_ready, 1)
            dve.wait_ge(row_exp, 1)
            dve.wait_ge(lrows_done, 1)
            for g in range(3):
                tt(row_out(lrow, g), rows_of(PB[5 + g], g), row_out(erow, g), ALU.mult).then_inc(lrow_ready, 1)
            dve.wait_ge(lrow_ready, 3)
            ch.link(tt(trow[:], lrow[:, 0, :], lrow[:, 1, :], ALU.add))
            tt(trow[:], trow[:], lrow[:, 2, :], ALU.add).then_inc(row_sum, 1)
            dve.wait_ge(row_inv, 1)
            for g in range(3):
                tt(erow[:, g, :], erow[:, g, :], trow[:], ALU.mult).then_inc(fac_ready, 1)

            def weighted(hd):
                dve.wait_ge(fac_done, hd + 1)
                dve.wait_ge(oraw_ready, hd + 1)
                if hd >= 2:
                    dve.wait_ge(ao_ready, hd - 1)
                tt(un[:, hd % 2, :], o_raw[:, hd, :], factor_bank(hd)[:], ALU.mult).then_inc(prod_ready, 1)

            for first in (0, 6):
                weighted(first)
                for hd in range(first, first + 6):
                    if hd + 1 < first + 6:
                        weighted(hd + 1)
                    dve.wait_ge(aohi_ready, hd + 1)
                    tt(ao_lo[:, hd, :], un[:, hd % 2, :], ao_hi[:, hd, :].bitcast(F32), ALU.subtract)\
                        .then_inc(ao_ready, 1)
            residual(PAN["attn_out"], GRP["attn_out"], 2, 2, 3)
            ffn(1, 3, 3)

            dve.wait_ge(r4_ready, 1)
            ch.link(tt(sq[:, 0, :], rstd2[:], rstd2[:], ALU.mult))
            tt(sq[:, 0, :], sq[:, 0, :], PB[5][:], ALU.mult).then_inc(t5_ready, 1)
            ch.link(nc.vector.memset(xpad[:, :, 0:3], 0.0))
            dve.wait_ge(r5_ready, 1)
            ch.link(tt(rstd[:], rstd[:], rstd2[:], ALU.mult))
            dve.sem_inc(rstd_ready, 1)
            for t in range(4):
                dve.wait_ge(panel_done, PAN["rx"] + t + 1)
                for c in range(2):
                    ch.step(tt(xpad[:, c, 3:3 + S], pair(GRP["rx"] + t)[c][:], rstd[:], ALU.mult))
                ch.settle()
                dve.sem_inc(group_free, 1)
                for c in range(2):
                    ch.step(ts(x4[:, 2 * t + c, :], xpad[:, c, 3:3 + S], vec(V_C4W + 3 * KC, 2 * t + c),
                               vec(V_C4B, 2 * t + c), ALU.mult, ALU.add))
                for tap in range(3):
                    ch.settle()
                    for c in range(2):
                        x = x4[:, 2 * t + c, :]
                        ch.step(stt(x, xpad[:, c, tap:tap + S], vec(V_C4W + tap * KC, 2 * t + c), x,
                                    ALU.mult, ALU.add))
                ch.settle()
                for j in (2 * t, 2 * t + 1):
                    ch.step(cp(x4_hi[:, j, :], x4[:, j, :]))
                ch.settle()
                for j in (2 * t, 2 * t + 1):
                    tt(x4_lo[:, j, :], x4[:, j, :], x4_hi[:, j, :].bitcast(F32), ALU.subtract).then_inc(x4_ready, 1)
            for j in range(KC):
                stt(h[:, j, :], h[:, j, :], vec(GAIN[TWIN], j), rstd2[:], ALU.mult, ALU.mult).then_inc(h_ready, 1)
            dve.wait_ge(h_ready, 5 * KC)
            ch.link(tt(rstd2[:], rstd[:], rstd[:], ALU.mult))
            with dve.Fori(0, KC // 2) as i:
                ch.enter(i, 8)
                for s in range(2):
                    j = i * 2 + s
                    g = GRP["cx"] + s
                    dve.wait_ge(xs_ready, i * 2 + (s + 1))
                    ch.link(tt(xpad[:, s, 3:3 + S], pair(g)[0][:], sq[:, s, :], ALU.mult))
                    dve.sem_inc(group_free, 1)
                    ch.link(tt(xpad[:, s, 3:3 + S], xpad[:, s, 3:3 + S], rstd2[:], ALU.mult))
                    ch.link(ts(cc[:, j, :], xpad[:, s, 3:3 + S], vec_i(V_C3W + 2 * KC, i, 2, s), None, ALU.mult))
                    for tap in range(2):
                        ins = stt(cc[:, j, :], xpad[:, s, 1 + tap:1 + tap + S], vec_i(V_C3W + tap * KC, i, 2, s),
                                  cc[:, j, :], ALU.mult, ALU.add)
                        if tap == 0:
                            ch.link(ins)
            ch.leave(KC // 2)
            for j in range(KC):
                dve.wait_ge(ig_ready, j + 1)
                tt(x4[:, j, :], x4[:, j, :], un[:, j % 2, :], ALU.mult).then_inc(xi_ready, 1)
            dve.wait_ge(xi_ready, KC)
            dve.wait_ge(group_free, GRP["bg"] + 2)
            with dve.Fori(0, KC // 2) as i:
                ch.enter(i, 6)
                for s in range(2):
                    j = i * 2 + s
                    g = GRP["bg"] + s
                    ts(sq[:, s, :], rr[:, j, :], spl[:, 0, bass.ds(j, 1)], None, ALU.mult).then_inc(z8_ready, 1)
                    dve.wait_ge(panel_done, i * 2 + (PAN["bg"] + s + 1))
                    tt(un[:, s, :], pair(g)[1][:], rstd[:], ALU.mult).then_inc(bin_ready, 1)
                    tt(gel[:], pair(g)[0][:], rstd[:], ALU.mult).then_inc(group_free, 1)
                    dve.wait_ge(group_free, i * 2 + (g + 3))
                    ch.link(tt(cc[:, j, :], cc[:, j, :], gel[:], ALU.mult))
                    dve.wait_ge(decay_ready, i * 4 + (2 * s + 2))
                    ch.link(tt(gel[:], rr[:, j, :], rr[:, j, :], ALU.mult))
                    stt(m2[:, j, :], gel[:], 1.0, sq[:, s, :], ALU.add, ALU.mult).then_inc(m2_ready, 1)
                    dve.wait_ge(m2_ready, i * 2 + (s + 1))
                    dve.wait_ge(sgc_ready, i * 2 + (s + 1))
                    ch.link(tt(cc[:, j, :], cc[:, j, :], un[:, s, :], ALU.mult))
            ch.leave(KC // 2)
            with dve.Fori(0, KC // 2) as i:
                ch.enter(i, 10)
                for s in range(2):
                    j = i * 2 + s
                    g = GRP["yg"] + s
                    dve.wait_ge(mult_ready, i * 2 + (s + 1))
                    tt(x4[:, j, :], x4[:, j, :], gel[:], ALU.mult).then_inc(mult_used, 1)
                    dve.wait_ge(mult_used, i * 2 + (s + 1))
                    ch.step(nc.vector.tensor_tensor_scan(rr[:, j, :], rr[:, j, :], x4[:, j, :], 0.0, ALU.mult, ALU.add))
                    dve.wait_ge(panel_done, i * 2 + (PAN["yg"] + s + 1))
                    tt(sq[:, s, :], pair(g)[0][:], rstd[:], ALU.mult).then_inc(yin_ready, 1)
                    tt(un[:, s, :], pair(g)[1][:], rstd[:], ALU.mult).then_inc(yin_ready, 1)
                    dve.wait_ge(yin_ready, i * 4 + (2 * s + 2))
                    dve.sem_inc(group_free, 1)
                    dve.wait_ge(gel_ready, i * 4 + (2 * s + 2))
                    ch.link(tt(un[:, s, :], sq[:, s, :], un[:, s, :], ALU.mult))
                    ch.link(tt(un[:, s, :], un[:, s, :], rr[:, j, :], ALU.mult))
                    ch.link(tt(un[:, s, :], un[:, s, :], cc[:, j, :], ALU.add))
                    ch.link(cp(m_hi[:, j, :], un[:, s, :]))
                    tt(m_lo[:, j, :], un[:, s, :], m_hi[:, j, :].bitcast(F32), ALU.subtract).then_inc(mg_ready, 1)
            ch.leave(KC // 2)
            residual(PAN["rg_out"], GRP["rg_out"], 1, 5, 5)
            ffn(2, 6, 5)
            dve.wait_ge(rstd_ready, 7)
            for q in range(4):
                dve.wait_ge(panel_done, PAN["gate"] + q + 1)
                scaled_pair(GRP["gate"] + q, (sgate[:, 2 * q, :], sgate[:, 2 * q + 1, :]), pin_ready, 2 * q)
                if q == 1:
                    dve.wait_ge(p_loaded, 16)
                    ch.link(cp(p_hi[:], pf[:]))
                    tt(p_lo[:], pf[:], p_hi[:].bitcast(F32), ALU.subtract).then_inc(pf_ready, 1)
            for q in range(4):
                dve.wait_ge(side_done, q + 1)
                dve.wait_ge(sgate_ready, 2 * q + 2)
                for c in range(2):
                    j = 2 * q + c
                    ch.link(tt(un[:, c, :], sgate[:, j, :], pair(GRP["ple"] + q)[c][:], ALU.mult))
                    if c:
                        dve.sem_inc(group_free, 1)
                    tt(h[:, j, :], h[:, j, :], un[:, c, :], ALU.add).then_inc(h_ready, 1)
            for j in reversed(range(KC)):
                dve.wait_ge(sq_ready, SQ0[7] + j + 1)
                ts(h[:, j, :], h[:, j, :], vec(GAIN[7], j), None, ALU.mult).then_inc(gained, 1)
            dve.wait_ge(gained, KC)
            dve.wait_ge(rstd_ready, 8)
            for j in range(OUT_SPLIT):
                tt(h[:, j, :], h[:, j, :], rstd[:], ALU.mult).then_inc(out_ready, 1)

        @block.tensor
        def _(pe):
            def mm(out, lhsT, rhs, start=True, stop=True):
                return nc.tensor.matmul(out, lhsT, rhs, start=start, stop=stop, skip_group_check=True)

            def at(c, i, step):
                return c if i is None else i * step + c

            def panel(p, g, x_hi, x_lo, i=None, pstep=2, gstep=2, ks=tuple(range(KC)), first=True, last=True,
                      inputs=None, m=None):
                s, nk = p % 2, len(ks)
                w = [t[:, s, :].rearrange("p (k c) -> p k c", c=HALF) for t in (w_hi, w_lo)]
                pe.wait_ge(hi_ready, at(p + 1, i, pstep))
                if first:
                    pe.wait_ge(group_free, at(g + 1, i, gstep))
                for n, k in enumerate(ks):
                    if inputs is not None:
                        pe.wait_ge(inputs[0], inputs[1] + k + 1)
                    for c in range(2):
                        mm(pair(g)[c][:], w[0][:, n, c * P:(c + 1) * P], x_hi[:, k, :], first and n == 0, False)
                        mm(pair(g)[c][:], w[0][:, n, c * P:(c + 1) * P], x_lo[:, k, :], False, False)
                if m is not None:
                    norm(m)
                pe.wait_ge(lo_ready, at(p + 1, i, pstep))
                for c in range(2):
                    for n, k in enumerate(ks):
                        ins = mm(pair(g)[c][:], w[1][:, n, c * P:(c + 1) * P], x_hi[:, k, :], False,
                                 last and n == nk - 1)
                ins.then_inc(panel_done, 1)

            def project(name, n, x_hi, x_lo, m=None):
                first = 0
                if m is not None:
                    first = 2
                    panel(PAN[name], GRP[name], x_hi, x_lo, inputs=(u_ready, KC * m), m=m)
                    panel(PAN[name] + 1, GRP[name] + 1, x_hi, x_lo)
                if n - first <= 2:
                    for t in range(first, n):
                        panel(PAN[name] + t, GRP[name] + t, x_hi, x_lo)
                else:
                    with pe.Fori(0, (n - first) // 2) as i:
                        for s in range(2):
                            panel(PAN[name] + first + s, GRP[name] + first + s, x_hi, x_lo, i)

            def residual(name, x_hi, x_lo, cuts, inputs):
                per = len(cuts) - 1
                with pe.Fori(0, 2) as i:
                    for s in range(2):
                        for t in range(per):
                            panel(PAN[name] + per * s + t, GRP[name] + s, x_hi, x_lo, i, 2 * per, 2,
                                  tuple(range(cuts[t], cuts[t + 1])), t == 0, t == per - 1,
                                  inputs if s == 0 else None)

            def by_tokens(p0, g, n_th, tile_of, beside=None):
                for s in range(2):
                    p = p0 + s
                    w = [t[:, p % 2, :].rearrange("p (k c) -> p k c", c=S) for t in (w_hi, w_lo)]
                    pe.wait_ge(hi_ready, p + 1)
                    pe.wait_ge(lo_ready, p + 1)
                    for t in range(TT):
                        if s == 0 and t % 2 == 0:
                            pe.wait_ge(group_free, g + t // 2 + 1)
                        for n in range(4):
                            k = 4 * s + n
                            for a, (x, v) in enumerate(((u_hi, w[0]), (u_lo, w[0]), (u_hi, w[1]))):
                                ins = mm(PB[t][:], tile_of(x[:, k, :], t), v[:, n, :], k == 0 and a == 0,
                                         k == KC - 1 and a == 2)
                        if s:
                            ins.then_inc(tok_done, 1)
                        if (s, t) == (0, TT - 1):
                            ins.then_inc(panel_done, 1)
                        elif t == TT - 1:
                            pe.wait_ge(tok_done, TT * (n_th + 1))
                            pe.sem_inc(panel_done, 1)
                        if beside:
                            beside(s, t)

            def norm(m):
                if m == 7:
                    pe.wait_ge(sum_added, SQ0[m] + KC - 3)
                    mm(MS[:], ones[:], ssq[:], True, False)
                    for j in (KC - 2, KC - 1):
                        pe.wait_ge(sq_ready, SQ0[m] + j + 1)
                        ins = mm(MS[:], ones[:], sq8[:, j, :], False, j == KC - 1)
                    ins.then_inc(ms_ready, 1)
                    return
                pe.wait_ge(sum_added, SQ0[m] + (2 * KC if m == TWIN else KC))
                ins = mm(MS[:], ones[:], ssq[:])
                if m == TWIN:
                    ins = mm(PB[5][:], ones[:], ssq2[:])
                if m in (0, 2):
                    for t in range(TT):
                        mm(PB[5][:, t:t + 1], near(ssq, t), ones[:, 0:1])
                        ins = mm(PB[5][:, TT + t:TT + t + 1], far(ssq, t), ones[:, 0:1])
                ins.then_inc(ms_ready, 1)

            def near(t, n):
                return t[:, n * P:(n + 1) * P]

            def far(t, n):
                return t[:, n::TT]

            def ffn(f, m):
                project(f"up{f}", FT, u_hi, u_lo, m)
                residual(f"down{f}", act_hi, act_lo, (0, 8, 16, FT), (act_ready, FT * f))

            pe.sem_inc(group_free, 2)
            pe.wait_ge(consts_ready, 2)
            project("f", 4, u_hi, u_lo, 0)
            project("q", 4, u_hi, u_lo)
            for t in range(0, 4, 2):
                by_tokens(PAN["i"] + t, GRP["i"] + t, t // 2, near)

            def level(hd, l):
                n = 8 * hd + l
                if l < len(LEVELS):
                    pe.wait_ge(z_ready, len(LEVELS) * hd + l + 1)
                if n >= 2:
                    pe.wait_ge(lev_free, n - 1)
                a, b = (level_tile(hd, l),) * 2 if l < len(LEVELS) else (key[:, hd, :], query[:, hd, :])
                for c in range(TT):
                    ins = mm(near(PB[5 + l % 2], c), near(a, c), near(b, c))
                ins.then_inc(lev_done, 1)

            def keys_by_token(hd):
                pe.wait_ge(dec_ready, hd + 1)
                if hd:
                    pe.wait_ge(on_ready, hd)
                for c in range(TT - 1):
                    ins = nc.tensor.transpose(near(HB, c), near(k_end, c), ident[:])
                ins.then_inc(ket_done, 1)

            def chunk_states(hd):
                pe.wait_ge(ket_ready, hd + 1)
                for c in range(TT - 1):
                    ins = mm(near(HB, c), k_endt[:, c, :], near(val[:, c, :], hd))
                ins.then_inc(kv_done, 1)

            def outputs(hd):
                pe.wait_ge(states_ready, hd + 1)
                pe.wait_ge(lev_free, 8 * hd + 8)
                for c in range(TT):
                    ins = mm(near(HB, c), near(val[:, c, :], hd), near(scores[hd % 2], c), True, c == 0)
                    if c:
                        ins = mm(near(HB, c), state[:, c - 1, :], near(q_dec, c), False, True)
                ins.then_inc(o_done, 1)

            def mean_squares(hd):
                pe.wait_ge(osq_ready, hd + 1)
                mm(MS[:], ones[:], sq[:, 0, :]).then_inc(oms_done, 1)

            AFTER_LEVEL = (1, 3, 4)

            def gate_part(q, half):
                p, g = PAN["g"] + q, GRP["g"] + q
                w = [t[:, p % 2, :].rearrange("p (k c) -> p k c", c=HALF) for t in (w_hi, w_lo)]
                pe.wait_ge(lo_ready, p + 1)
                if half == 0:
                    pe.wait_ge(group_free, g + 1)
                for k in range(4 * half, 4 * half + 4):
                    for c in range(2):
                        for a, (v, x) in enumerate(((w[0], u_hi), (w[0], u_lo), (w[1], u_hi))):
                            ins = mm(pair(g)[c][:], v[:, k, c * P:(c + 1) * P], x[:, k, :], k == 0 and a == 0,
                                     k == KC - 1 and a == 2)
                if half:
                    ins.then_inc(panel_done, 1)

            panel(PAN["g"], GRP["g"], u_hi, u_lo)
            pe.wait_ge(const_loaded, 64)
            for hd in range(HG):
                for l in range(len(LEVELS) + 1):
                    level(hd, l)
                    if hd and l in AFTER_LEVEL:
                        (chunk_states, outputs, mean_squares)[AFTER_LEVEL.index(l)](hd - 1)
                if 0 < hd < HG - 1:
                    gate_part((hd + 1) // 2, (hd - 1) % 2)
                keys_by_token(hd)
            chunk_states(HG - 1)
            outputs(HG - 1)
            mean_squares(HG - 1)

            residual("hgrn_out", o_hi, o_lo, (0, KC), (oh_ready, 0))
            ffn(0, 1)
            def score(hd):
                tile_of = far if hd >= GH else near
                pe.wait_ge(qk_ready, 4 * (hd // GH + 1))
                if hd:
                    pe.wait_ge(max_ready, hd if hd <= GH else hd - 1)
                q, k = aqk[:, hd, :], aqk[:, AH + hd, :]
                for n in range(TT):
                    ins = mm(near(score_bank(hd), n), tile_of(q, n), tile_of(k, n))
                    if hd < GH and n:
                        ins = mm(near(PB[6], n), near(q, n), near(k, n - 1))
                ins.then_inc(s_done, 1)

            def turn(hd):
                pe.wait_ge(p_ready, hd + 1)
                if 0 < hd <= GH:
                    pe.wait_ge(oraw_ready, hd)
                elif hd:
                    pe.wait_ge(pt_ready, hd - 1)
                for n in range(TT):
                    ins = nc.tensor.transpose(near(turn_bank(hd), n), scores_of(hd)[:, n, :], ident[:])
                    if hd < GH and n:
                        ins = nc.tensor.transpose(near(MS, n), s_ab[1][:, n, :], ident[:])
                ins.then_inc(pt_done, 1)

            def weigh(hd):
                g, c = hd // GH, (hd % GH) * P
                bank = weigh_bank(hd)
                pe.wait_ge(v_ready, g + 1)
                pe.wait_ge(pt_ready, hd + 1)
                for n in range(TT):
                    ins = mm(near(bank, n), av[:, g, n, c:c + P], turned_scores(hd)[:, n, :], True, g > 0 or n == 0)
                    if g == 0 and n:
                        ins = mm(near(bank, n), av[:, g, n - 1, c:c + P], pt_b[:, n, :], False, True)
                ins.then_inc(pv_done, 1)

            def rows(src, done):
                for g in range(3):
                    for n in range(TT):
                        ins = nc.tensor.transpose(PB[5 + g][0:GH, n * P:(n + 1) * P],
                                                  src[:, GH * g:GH * (g + 1), n], ident[:])
                ins.then_inc(done, 1)

            def factor(hd):
                pe.wait_ge(fac_ready, hd // GH + 1)
                if hd < 4:
                    pe.wait_ge(oraw_ready, 2 * GH)
                else:
                    pe.wait_ge(prod_ready, hd - 3)
                mm(factor_bank(hd)[:], sel[:, hd % GH, :], erow[:, hd // GH, :]).then_inc(fac_done, 1)

            project("a0", 4, u_hi, u_lo, 2)
            by_tokens(PAN["a0"] + 4, GRP["a0"] + 4, 2, near)
            for t in range(4):
                panel(PAN["a1"] + t, GRP["a1"] + t, u_hi, u_lo)
                if t:
                    turn(t - 1)
                score(t)
                if t:
                    weigh(t - 1)
            for t in range(4):
                panel(PAN["a2"] + t, GRP["a2"] + t, u_hi, u_lo)
                turn(t + 3)
                score(t + 4)
                if t == 0:
                    weigh(3)

            def beside_v1(s, t):
                if (s, t) == (0, 3):
                    turn(7)
                    score(8)
                    score(9)
                elif (s, t) == (1, 1):
                    turn(8)
                elif (s, t) == (1, 2):
                    turn(9)
                    score(10)
                    score(11)

            def beside_v2(s, t):
                if (s, t) == (0, 0):
                    pe.wait_ge(max_ready, AH)
                    pe.wait_ge(pt_ready, 9)
                    rows(mst, mrows_done)
                elif (s, t) == (0, 2):
                    pe.wait_ge(mrow_ready, 1)
                    turn(10)
                    turn(11)
                elif (s, t) == (0, 3):
                    pe.wait_ge(sums_ready, 1)
                    pe.wait_ge(pt_ready, 11)
                    rows(lst, lrows_done)
                elif (s, t) == (1, 0):
                    pe.wait_ge(pt_ready, AH)
                    weigh(4)
                    pe.wait_ge(lrow_ready, 3)
                    for hd in (5, 6, 7):
                        weigh(hd)

            by_tokens(PAN["v1"], GRP["v1"], 3, far, beside_v1)
            by_tokens(PAN["v2"], GRP["v2"], 4, far, beside_v2)
            for hd in range(4):
                factor(hd)
            pe.wait_ge(group_free, GRP["attn_out"] + 2)
            weigh(8)
            weigh(9)
            factor(4)
            factor(5)
            p, g, cuts = PAN["attn_out"], GRP["attn_out"], (range(0, 6), range(6, AH))
            panel(p, g, ao_hi, ao_lo, ks=cuts[0], last=False, inputs=(ao_ready, 0))
            for hd in (10, 11):
                pe.wait_ge(oraw_ready, hd - 1)
                weigh(hd)
            for hd in range(6, AH):
                factor(hd)
            panel(p + 1, g, ao_hi, ao_lo, ks=cuts[1], first=False, inputs=(ao_ready, 0))
            for q in range(1, 4):
                for t in range(2):
                    panel(p + 2 * q + t, g + q, ao_hi, ao_lo, ks=cuts[t], first=t == 0, last=t == 1)
            ffn(1, 3)
            project("rx", 4, u_hi, u_lo, TWIN)
            project("cx", KC, u_hi, u_lo)
            for s in range(2):
                p = PAN["rg"] + s
                w = [t[:, p % 2, :].rearrange("p (k c) -> p k c", c=HALF) for t in (w_hi, w_lo)]
                pe.wait_ge(lo_ready, p + 1)
                for q in range(4):
                    g = GRP["rg"] + 4 * s + q
                    pe.wait_ge(group_free, g + 1)
                    pe.wait_ge(x4_ready, 2 * q + 2)
                    for c in range(2):
                        for n in range(2):
                            k = 2 * q + n
                            for a, (v, x) in enumerate(((w[0], x4_hi), (w[0], x4_lo), (w[1], x4_hi))):
                                ins = mm(pair(g)[c][:], v[:, k, c * P:(c + 1) * P], x[:, k, :],
                                         n == 0 and a == 0, n == 1 and a == 2)
                    ins.then_inc(gate_done, 1)
                pe.wait_ge(gate_done, 4 * s + 4)
                pe.sem_inc(panel_done, 1)
            project("bg", KC, u_hi, u_lo)
            project("yg", KC, u_hi, u_lo)
            residual("rg_out", m_hi, m_lo, (0, KC), (mg_ready, 0))
            ffn(2, 5)
            project("gate", 4, u_hi, u_lo, 6)
            p = PAN["ple"]
            w = [t[:, p % 2, :].rearrange("p (k c) -> p k c", c=DM) for t in (w_hi, w_lo)]
            pe.wait_ge(lo_ready, p + 1)
            pe.wait_ge(pf_ready, 1)
            for q in range(4):
                g = GRP["ple"] + q
                pe.wait_ge(group_free, g + 1)
                for c in range(2):
                    j = 2 * q + c
                    for k in range(2):
                        for a, (v, x) in enumerate(((w[0], p_hi), (w[0], p_lo), (w[1], p_hi))):
                            ins = mm(pair(g)[c][:], v[:, k, j * P:(j + 1) * P], x[:, k, :],
                                     k == 0 and a == 0, k == 1 and a == 2)
                ins.then_inc(side_done, 1)
            norm(7)


def _tiles(v):
    return np.asarray(v).reshape(-1, P).T


def _panel(w, ks, cols):
    t = np.asarray(w).reshape(-1, P, w.shape[-1])[list(ks)][:, :, cols]
    t = t.transpose(1, 0, 2).reshape(P, -1)
    return np.pad(t, ((0, 0), (0, PANEL - t.shape[1])))


def _panels(i):
    def cols(*starts):
        return np.concatenate([np.arange(c, c + P) for c in starts])

    def whole(w, first, n):
        return [_panel(w, range(KC), cols(first + 256 * k, first + 256 * k + P)) for k in range(n)]

    def paired(w, a, b, n):
        return [_panel(w, range(KC), cols(a + P * k, b + P * k)) for k in range(n)]

    def by_tokens(w, first, n):
        return [_panel(w, range(4 * s, 4 * s + 4), np.arange(first + S * k, first + S * (k + 1)))
                for k in range(n) for s in range(2)]

    def cut(w, cuts):
        return [_panel(w, range(a, b), cols(256 * k, 256 * k + P))
                for k in range(4) for a, b in zip(cuts, cuts[1:])]

    def ffn(w_in, w_down):
        return paired(w_in, 0, DFF, FT), cut(w_down, (0, 8, 16, FT))

    hin, qkv, w2 = i["hgrn_w_in"][0], i["attn_w_qkv"][0], i["w_in_2"][0]
    aw, gw = AH * P, GH * P
    qk = [whole(qkv, g * gw, 2) + whole(qkv, aw + g * gw, 2) for g in range(3)]
    attn_in = qk[0] + by_tokens(qkv, 2 * aw, 1) + qk[1] + qk[2] + by_tokens(qkv, 2 * aw + gw, 2)
    up0, down0 = ffn(i["ffn_w_in"][0], i["ffn_w_down"][0])
    up1, down1 = ffn(i["ffn_w_in"][1], i["ffn_w_down"][1])
    up2, down2 = ffn(i["w_gate_up_2"][0], i["w_down_2"][0])
    out = whole(hin, DM, 4) + whole(hin, 0, 4) + by_tokens(hin, 2 * DM, 2) + whole(hin, 3 * DM, 4)
    out += whole(i["hgrn_w_out"][0], 0, 4) + up0 + down0
    out += attn_in + cut(i["attn_w_out"][0], (0, 6, 12)) + up1 + down1
    out += whole(w2, 0, 4)
    out += paired(w2, 3 * DM, 4 * DM, KC)
    out += [_panel(i[k][0].reshape(DM, 256), range(KC), np.arange(256)) for k in ("w_rg_r_2", "w_rg_i_2")]
    out += paired(w2, 2 * DM, 6 * DM, KC) + paired(w2, DM, 5 * DM, KC)
    out += whole(i["w_out_2"][0], 0, 4) + up2 + down2
    out += whole(i["w_ple_gate_2"][0], 0, 4) + [_panel(i["w_ple_2"][0], range(2), np.arange(DM))]
    assert len(out) == PAN["end"]
    return np.stack(out)


def _vecs(i):
    v = [i["norm_mix"][0], i["norm_ffn"][0], i["norm_mix"][1], i["norm_ffn"][1], i["final_norm"],
         i["g_mix_2"][0], i["g_ffn_2"][0], i["g_ple_2"][0], i["g_final_2"],
         *i["hgrn_lb_logits"], i["hgrn_out_norm"][0], *i["conv4_w_2"][0], i["conv4_b_2"][0],
         i["b_rg_r_2"][0].reshape(-1), i["b_rg_i_2"][0].reshape(-1), i["lru_lambda_2"][0], *i["conv3_w_2"][0]]
    return np.concatenate([_tiles(a) for a in v], axis=1)


def _constants():
    inv = 1.0 / (np.float32(10000.0) ** (np.arange(0, P, 2, dtype=np.float32) / np.float32(P)))
    ang = inv.astype(np.float32)[:, None] * np.arange(S, dtype=np.float32)[None, :]
    cos, sin = np.cos(ang), np.sin(ang)
    cs = np.stack([np.concatenate([cos, cos]), np.concatenate([-sin, sin])], axis=1)
    a, b = np.meshgrid(np.arange(P), np.arange(P), indexing="ij")
    lm = [(a // (2 * m) == b // (2 * m)) & (a % (2 * m) < m) & (b % (2 * m) >= m) for m in LEVELS]
    lmask = np.stack([*lm, a == b], axis=1).astype(np.float32)
    am = [b <= a, b >= a, (b <= a) & (b % 4 == a % 4)]
    amask = np.stack([np.where(m, 0.0, MASKED) for m in am] + [lm[0].astype(np.float64)], axis=1)
    sel = np.zeros((GH, GH, P), np.float32)
    for k in range(GH):
        sel[k, k] = 1.0
    return np.eye(P, dtype=np.float32), cs.astype(np.float32), lmask, amask.astype(np.float32), sel


def kernel(**inputs):
    import concourse.bacc as _bacc
    from concourse.bass_utils import run_bass_kernel_spmd as _run

    i = {k: np.asarray(v) for k, v in inputs.items()}
    ident, cs, lmask, amask, sel = _constants()
    arrays = {
        "wall": _panels(i), "x_t": np.ascontiguousarray(i["x"][0].T), "p_t": np.ascontiguousarray(i["p_2"][0, 0].T),
        "vecs_in": np.ascontiguousarray(_vecs(i)), "ident_in": ident, "cs_in": cs, "lmask_in": lmask,
        "amask_in": amask, "sel_in": sel,
    }
    nc = _bacc.Bacc("TRN2", target_bir_lowering=False, num_devices=1)
    args = [nc.dram_tensor(k, a.shape, mybir.dt.from_np(a.dtype), kind="ExternalInput").ap()
            for k, a in arrays.items()]
    out = nc.dram_tensor("out_t", (DM, S), F32, kind="ExternalOutput").ap()
    build(nc, *args, out)
    r = _run(nc, [arrays], core_ids=[0])
    return np.ascontiguousarray(r.results[0]["out_t"].T)[None]
```
